# Optimizing a Trainium2 kernel written in Bass

```python
import math
import jax, jax.numpy as jnp
from jax import lax
import numpy as np

D_MODEL = 1024
BATCH = 1
SEQ = 256
DEPTH = 1
DEC_BATCH = 1
DEC_SEQ = 512
PAST_LEN = 128

GRID_W = 64
MIX_WIDTH = D_MODEL
NA_HEADS = 8
NA_HEAD_DIM = 64
NA_WIDTH = NA_HEADS * NA_HEAD_DIM
NA_ROWS = 8
NA_COLS = 16
RET_HEADS = 4
RET_HEAD_DIM = 128
RET_WIDTH = RET_HEADS * RET_HEAD_DIM
RET_CHUNK = 128
ROPE_BASE = 10000.0
IN_COLS = 3 * NA_WIDTH + 4 * RET_WIDTH
PEER_HEADS = 8
PEER_QDIM = 256
PEER_HALF = PEER_QDIM // 2
N_KEYS = 128
N_EXPERTS = N_KEYS * N_KEYS
PEER_TOPK = 16
PEER_BLOCK = 128
EPS = 1e-6

kernel_name = 'hymba_na_retnet_peer_encoder'

def rmsnorm(x, g):
    xf = x.astype(jnp.float32)
    y = xf * lax.rsqrt(jnp.mean(xf * xf, axis=-1, keepdims=True) + EPS)
    return (y * g.astype(jnp.float32)).astype(x.dtype)

def rotary(x):
    L, d = x.shape[1], x.shape[-1]
    inv = 1.0 / (ROPE_BASE ** (jnp.arange(0, d, 2, dtype=jnp.float32) / d))
    ang = jnp.arange(L, dtype=jnp.float32)[:, None] * inv[None, :]
    cos = jnp.cos(ang)[None, :, None, :]
    sin = jnp.sin(ang)[None, :, None, :]
    x1 = x[..., : d // 2].astype(jnp.float32)
    x2 = x[..., d // 2:].astype(jnp.float32)
    return jnp.concatenate([x1 * cos - x2 * sin, x1 * sin + x2 * cos], axis=-1).astype(x.dtype)

def neighbourhood_attention(q, k, v, rpb):
    B, L, H, dh = q.shape
    rows = L // GRID_W
    kr = min(NA_ROWS, rows)
    qg = q.reshape(B, rows, GRID_W, H, dh)
    kg = k.reshape(B, rows, GRID_W, H, dh)
    vg = v.reshape(B, rows, GRID_W, H, dh)
    r_idx = jnp.arange(rows)
    row_start = jnp.clip(r_idx - kr // 2, 0, rows - kr)
    c_idx = jnp.arange(GRID_W)
    col_start = jnp.clip(c_idx - NA_COLS // 2, 0, GRID_W - NA_COLS)
    col_idx = col_start[:, None] + jnp.arange(NA_COLS)[None, :]
    col_bias_idx = col_idx - c_idx[:, None] + (NA_COLS - 1)
    scale = dh ** -0.5

    def one_row(args):
        qr, rs, ri = args
        k_band = lax.dynamic_slice_in_dim(kg, rs, kr, axis=1)
        v_band = lax.dynamic_slice_in_dim(vg, rs, kr, axis=1)
        k_nb = k_band[:, :, col_idx]
        v_nb = v_band[:, :, col_idx]
        s = jnp.einsum('bqhd,brqjhd->bhqrj', qr, k_nb).astype(jnp.float32) * scale
        row_bias_idx = rs + jnp.arange(kr) - ri + (NA_ROWS - 1)
        bias = rpb[:, row_bias_idx][:, :, col_bias_idx]
        s = s + jnp.transpose(bias, (0, 2, 1, 3)).astype(jnp.float32)[None]
        p = jax.nn.softmax(s.reshape(B, H, GRID_W, kr * NA_COLS), axis=-1)
        p = p.reshape(B, H, GRID_W, kr, NA_COLS).astype(v.dtype)
        return jnp.einsum('bhqrj,brqjhd->bqhd', p, v_nb)

    out = lax.map(one_row, (jnp.transpose(qg, (1, 0, 2, 3, 4)), row_start, r_idx))
    return jnp.transpose(out, (1, 0, 2, 3, 4)).reshape(B, L, H * dh)

def chunk_retention(q, k, v, log_gamma, strict):
    B, L, H, dk = q.shape
    dv = v.shape[-1]
    C = RET_CHUNK
    nc = L // C
    dt = q.dtype
    qc = q.reshape(B, nc, C, H, dk)
    kc = k.reshape(B, nc, C, H, dk)
    vc = v.reshape(B, nc, C, H, dv)
    pos = jnp.arange(C, dtype=jnp.float32)
    diff = pos[:, None] - pos[None, :]
    mask = (diff > 0) if strict else (diff >= 0)
    decay = jnp.where(mask[None], jnp.exp(log_gamma[:, None, None] * jnp.maximum(diff, 0.0)[None]), 0.0).astype(dt)
    k_decay = jnp.exp(log_gamma[None, :] * (C - 1 - pos)[:, None]).astype(dt)
    q_decay = jnp.exp(log_gamma[None, :] * (pos + 1)[:, None]).astype(dt)
    chunk_decay = jnp.exp(log_gamma * C).astype(dt)
    att = jnp.einsum('bnqhd,bnkhd->bnhqk', qc, kc) * decay[None, None]
    o_intra = jnp.einsum('bnhqk,bnkhe->bnqhe', att, vc)
    S = jnp.einsum('bnkhd,kh,bnkhe->nbhde', kc, k_decay, vc)

    def step(R, S_i):
        return chunk_decay[None, :, None, None] * R + S_i, R

    _, R_prev = lax.scan(step, jnp.zeros(S.shape[1:], S.dtype), S)
    o_inter = jnp.einsum('bnqhd,qh,nbhde->bnqhe', qc, q_decay, R_prev)
    return (o_intra + o_inter).reshape(B, L, H, dv)

def bidirectional_retention(q, k, v, gate, decay_fwd, decay_bwd, norm_g):
    B, L, H, dk = q.shape
    q = rotary(q)
    k = rotary(k) * (dk ** -0.5)
    lg_f = jax.nn.log_sigmoid(decay_fwd.astype(jnp.float32))
    lg_b = jax.nn.log_sigmoid(decay_bwd.astype(jnp.float32))
    o_f = chunk_retention(q, k, v, lg_f, False)
    o_b = jnp.flip(chunk_retention(jnp.flip(q, 1), jnp.flip(k, 1), jnp.flip(v, 1), lg_b, True), 1)
    o = (o_f + o_b).astype(jnp.float32)
    mu = jnp.mean(o, axis=-1, keepdims=True)
    var = jnp.mean(jnp.square(o - mu), axis=-1, keepdims=True)
    o = (o - mu) * lax.rsqrt(var + EPS)
    o = o.reshape(B, L, H * v.shape[-1]) * norm_g.astype(jnp.float32)
    return (jax.nn.silu(gate.astype(jnp.float32)) * o).astype(v.dtype)

def peer(h, w_q, sub_keys, u, v):
    B, L, D = h.shape
    T = B * L
    ht = h.reshape(T, D)
    q = (ht @ w_q).reshape(T, PEER_HEADS, 2, PEER_HALF)
    s = jnp.einsum('thpd,hpnd->thpn', q, sub_keys)
    s_top, i_top = lax.top_k(s, PEER_TOPK)
    cand = s_top[:, :, 0, :, None] + s_top[:, :, 1, None, :]
    cand_idx = i_top[:, :, 0, :, None] * N_KEYS + i_top[:, :, 1, None, :]
    best_s, best_pos = lax.top_k(cand.reshape(T, PEER_HEADS, PEER_TOPK * PEER_TOPK), PEER_TOPK)
    experts = jnp.take_along_axis(cand_idx.reshape(T, PEER_HEADS, PEER_TOPK * PEER_TOPK), best_pos, axis=-1)
    gates = jax.nn.softmax(best_s.astype(jnp.float32), axis=-1).astype(h.dtype)
    nb = T // PEER_BLOCK
    xb = ht.reshape(nb, PEER_BLOCK, D)
    eb = experts.reshape(nb, PEER_BLOCK, PEER_HEADS * PEER_TOPK)
    gb = gates.reshape(nb, PEER_BLOCK, PEER_HEADS * PEER_TOPK)

    def block(args):
        xt, e, g = args
        ue = u[e]
        a = jax.nn.gelu(jnp.einsum('td,tkd->tk', xt, ue))
        ve = v[e]
        return jnp.einsum('tk,tkd->td', g * a, ve)

    return lax.map(block, (xb, eb, gb)).reshape(B, L, D)

def encoder_layer(x, norm1_g, w_in, na_rpb, ret_decay_fwd, ret_decay_bwd, ret_norm_g,
                  w_out, norm2_g, peer_w_q, peer_sub_keys, peer_u, peer_v):
    B, L, D = x.shape
    h = rmsnorm(x, norm1_g)
    proj = h @ w_in
    cuts = [NA_WIDTH, 2 * NA_WIDTH, 3 * NA_WIDTH,
            3 * NA_WIDTH + RET_WIDTH, 3 * NA_WIDTH + 2 * RET_WIDTH, 3 * NA_WIDTH + 3 * RET_WIDTH]
    na_q, na_k, na_v, r_q, r_k, r_v, r_g = jnp.split(proj, cuts, axis=-1)
    na_shape = (B, L, NA_HEADS, NA_HEAD_DIM)
    na_o = neighbourhood_attention(na_q.reshape(na_shape), na_k.reshape(na_shape),
                                   na_v.reshape(na_shape), na_rpb)
    r_shape = (B, L, RET_HEADS, RET_HEAD_DIM)
    ret_o = bidirectional_retention(r_q.reshape(r_shape), r_k.reshape(r_shape), r_v.reshape(r_shape),
                                    r_g, ret_decay_fwd, ret_decay_bwd, ret_norm_g)
    x = x + jnp.concatenate([na_o, ret_o], axis=-1) @ w_out
    x = x + peer(rmsnorm(x, norm2_g), peer_w_q, peer_sub_keys, peer_u, peer_v)
    return x

def setup_inputs(seed: int = 0) -> dict:
    key = jax.random.key(seed)
    ks = jax.random.split(key, 16)
    f32 = jnp.float32
    base = 1.0 - 2.0 ** (-5.0 - jnp.arange(RET_HEADS, dtype=f32))
    logit = jnp.log(base) - jnp.log1p(-base)
    return {
        'x_prompt': jax.random.normal(ks[0], (BATCH, SEQ, D_MODEL), f32),
        'x_sample': jax.random.normal(ks[1], (DEC_BATCH, DEC_SEQ, D_MODEL), f32),
        'norm1_g': 1.0 + 0.02 * jax.random.normal(ks[2], (DEPTH, D_MODEL), f32),
        'w_in': jax.random.normal(ks[3], (DEPTH, D_MODEL, IN_COLS), f32) * D_MODEL ** -0.5,
        'na_rpb': 0.1 * jax.random.normal(ks[4], (DEPTH, NA_HEADS, 2 * NA_ROWS - 1, 2 * NA_COLS - 1), f32),
        'ret_decay_fwd': logit[None, :] + 0.1 * jax.random.normal(ks[5], (DEPTH, RET_HEADS), f32),
        'ret_decay_bwd': logit[None, :] + 0.1 * jax.random.normal(ks[6], (DEPTH, RET_HEADS), f32),
        'ret_norm_g': 1.0 + 0.02 * jax.random.normal(ks[7], (DEPTH, RET_WIDTH), f32),
        'w_out': jax.random.normal(ks[8], (DEPTH, MIX_WIDTH, D_MODEL), f32) * MIX_WIDTH ** -0.5,
        'norm2_g': 1.0 + 0.02 * jax.random.normal(ks[9], (DEPTH, D_MODEL), f32),
        'peer_w_q': jax.random.normal(ks[10], (DEPTH, D_MODEL, PEER_HEADS * PEER_QDIM), f32) * D_MODEL ** -0.5,
        'peer_sub_keys': jax.random.normal(ks[11], (DEPTH, PEER_HEADS, 2, N_KEYS, PEER_HALF), f32) * PEER_HALF ** -0.5,
        'peer_u': jax.random.normal(ks[12], (DEPTH, N_EXPERTS, D_MODEL), f32) * D_MODEL ** -0.5,
        'peer_v': 0.5 * jax.random.normal(ks[13], (DEPTH, N_EXPERTS, D_MODEL), f32),
        'final_g': 1.0 + 0.02 * jax.random.normal(ks[14], (D_MODEL,), f32),
    }

def reference(x_prompt, x_sample, norm1_g, w_in, na_rpb, ret_decay_fwd, ret_decay_bwd, ret_norm_g,
              w_out, norm2_g, peer_w_q, peer_sub_keys, peer_u, peer_v, final_g):
    def trunk(x):
        for l in range(DEPTH):
            x = encoder_layer(x, norm1_g[l], w_in[l], na_rpb[l], ret_decay_fwd[l], ret_decay_bwd[l],
                              ret_norm_g[l], w_out[l], norm2_g[l], peer_w_q[l], peer_sub_keys[l],
                              peer_u[l], peer_v[l])
        return rmsnorm(x, final_g)

    y_prompt = trunk(x_prompt)
    y_sample = trunk(x_sample)
    return (y_prompt, y_sample)


_drawn_inputs = setup_inputs


def setup_inputs(seed=0):
    import zlib

    import numpy as np

    out = dict(_drawn_inputs(seed))
    spreads = {}
    factors = {}
    for name, (base, spread) in spreads.items():
        noise = np.random.default_rng([zlib.crc32(name.encode()), seed]).standard_normal(out[name].shape)
        drawn = base * np.exp(spread * noise) if base else spread * noise
        out[name] = __import__('jax').numpy.asarray(drawn.astype(out[name].dtype))
    for name, factor in factors.items():
        out[name] = (out[name] * factor).astype(out[name].dtype)
    return out
```

```python
import math
from contextlib import ExitStack

import concourse.bass as bass
import numpy as np
from concourse import mybir

F32 = mybir.dt.float32
F32R = mybir.dt.float32r
U32 = mybir.dt.uint32
ALU = mybir.AluOpType
ACT = mybir.ActivationFunctionType
AX = mybir.AxisListType

P = 128
D_MODEL = 1024
SEQ, DEC_SEQ = 256, 512
NT = (SEQ + DEC_SEQ) // P
TOK = NT * P
HALF = TOK // 2
TPH = NT // 2
KD = D_MODEL // P
GRID_W = 64
NA_HEADS, NA_DIM, NA_COLS, NA_ROWS = 8, 64, 16, 8
RET_HEADS, RET_DIM = 4, 128
WIDTH = 512
PEER_HEADS, TOPK, N_KEYS = 8, 16, 128
EPS = 1e-6
SEQS = [(0, SEQ // P), (SEQ // P, DEC_SEQ // P)]

C_NA_QK, C_NA_V, C_RET_QK, C_RET_V, C_RET_G, C_OUT, C_WQ, C_END = 0, 8, 12, 20, 24, 28, 36, 52
RING = 4
AHEAD = 3
BAND_ROWS = 14
DIFF = 896
HOT = 4
UNITS = NA_HEADS * NT
NEG = -1e30


def seq_of(tile):
    return 0 if tile < SEQS[1][0] else 1


class Steps:

    def __init__(self, eng, sem):
        self.eng, self.sem, self.n = eng, sem, 0

    def add(self, ins):
        ins.then_inc(self.sem, 1)
        self.n += 1

    def settle(self):
        self.eng.wait_ge(self.sem, self.n)


def encoder_program(nc, a):
    KB = 1024
    base0 = -(-nc.sbuf_base // 32) * 32
    ctx = ExitStack()
    with ctx:
        def sb(name, at, shape, dt=F32):
            n = int(np.prod(shape[1:])) * 4
            assert base0 + at + n <= nc.sbuf_usable_end, (name, at, n)
            return nc.alloc_sbuf_tensor_at(name, shape, dt, offset=base0 + at)

        def sem(name):
            return ctx.enter_context(nc.semaphore(name))

        ht_hi = sb("ht_hi", 0, [P, KD, TOK], F32R)
        ht_lo = sb("ht_lo", 24 * KB, [P, KD, TOK], F32R)
        at = 48 * KB
        small = {}
        for name, cols in (("ident", 128), ("iota", 128), ("g1", KD), ("g2", KD), ("dec_f", 4), ("dec_b", 4),
                           ("lg", 8), ("lgt", 40), ("ssq", 3 * NT), ("ms", 3 * NT), ("rms", 3 * NT),
                           ("rstd", 3 * NT), ("mx", UNITS), ("nmx", UNITS), ("psum_", UNITS), ("prec", UNITS),
                           ("winmask", GRID_W)):
            small[name] = sb(name, at, [P, cols])
            at += -(-cols * 4 // 32) * 32
        s = small
        A0 = -(-at // 256) * 256
        assert A0 <= 52 * KB

        mix = sb("mix", A0, [P, NT, D_MODEL])
        x2 = sb("x2", A0, [P, NT, D_MODEL])
        raw = sb("raw", A0 + 24 * KB, [P, RING, 1024])
        sp_hi = sb("sp_hi", A0 + 40 * KB, [P, RING, 1024], F32R)
        sp_lo = sb("sp_lo", A0 + 56 * KB, [P, RING, 1024], F32R)
        R0 = A0 + 72 * KB
        na_qk = sb("na_qk", R0, [P, 8, TOK])
        ret_v = sb("ret_v", R0, [P, NT, WIDTH])
        ret_gate = sb("ret_gate", R0 + 12 * KB, [P, NT, WIDTH])
        ret_qk = sb("ret_qk", R0 + 24 * KB, [P, 8, TOK])
        x_again = sb("x_again", R0 + 24 * KB, [P, NT, D_MODEL])
        W0 = R0 + 48 * KB
        h_tile = sb("h_tile", W0, [P, 2, D_MODEL])
        junk = sb("junk", W0 + 8 * KB, [P, D_MODEL])
        band = sb("band", W0 + 12 * KB, [P, 2, BAND_ROWS, GRID_W])
        na_sc = sb("na_sc", W0 + 19 * KB, [P, 2, 512])
        na_p = sb("na_p", W0 + 23 * KB, [P, 2, 512])
        na_pt = sb("na_pt", W0 + 27 * KB, [P, 2, 512])
        att = sb("att", W0, [P, 2, 4, 512])
        rot_sin = sb("rot_sin", W0, [P, 2, HALF])
        rot_cos = sb("rot_cos", W0 + 4 * KB, [P, 2, HALF])
        dmat = sb("dmat", W0 + 16 * KB, [P, 2, DIFF])
        diff = sb("diff", W0 + 23 * KB, [P, DIFF])
        cos = sb("cos", W0 + 26 * KB + 512, [P, TOK])
        sin = sb("sin", W0 + 29 * KB + 512, [P, TOK])
        back = sb("back", W0 + 26 * KB + 512, [P, DIFF])
        ngain = sb("ngain", W0 + 32 * KB + 512, [P, WIDTH])
        perm = sb("perm", W0 + 34 * KB + 512, [P, P])
        stats = sb("stats", W0 + 35 * KB, [P, NT * RET_HEADS, 6])
        mv = sb("mv", W0 + 35 * KB + 576, [P, NT * RET_HEADS, 2])
        ret_std = sb("ret_std", W0 + 35 * KB + 768, [P, NT * RET_HEADS])
        ret_rs = sb("ret_rs", W0 + 35 * KB + 864, [P, NT * RET_HEADS])

        q_t = sb("q_t", R0, [P, 16, TOK])
        keys_t = sb("keys_t", W0 + 12 * KB, [P, 16, N_KEYS])
        cand = sb("cand", A0 + 24 * KB, [P, PEER_HEADS, 256])
        one1 = sb("one1", A0 + 40 * KB, [P, P, TOPK])
        one2 = sb("one2", A0 + 48 * KB, [P, P, TOPK])
        rep = sb("rep", A0 + 32 * KB, [P, 4, N_KEYS])
        tv = sb("tv", A0 + 34 * KB, [P, 2, 16, TOPK])
        ti = sb("ti", A0 + 36 * KB, [P, 2, 16, TOPK], U32)
        tif = sb("tif", A0 + 38 * KB, [P, 2, 16, TOPK])
        T0 = A0 + 56 * KB
        bv = sb("bv", T0, [P, PEER_HEADS, TOPK])
        bp = sb("bp", T0 + 512, [P, PEER_HEADS, TOPK], U32)
        pa = sb("pa", T0 + 1024, [P, 2, P], U32)
        paf = sb("paf", T0 + 2048, [P, 2, P])
        pbf = sb("pbf", T0 + 3072, [P, 2, P])
        gexp = sb("gexp", T0 + 4096, [P, 2, PEER_HEADS, TOPK])
        gsum = sb("gsum", T0 + 5120, [P, PEER_HEADS])
        grec = sb("grec", T0 + 5152, [P, PEER_HEADS])
        chosen = sb("chosen", T0 + 5632, [P, 3, P])
        idx_t = sb("idx_t", W0 + 24 * KB, [P, 3, TOK])
        TB = P
        stage = sb("stage", A0, [P, 2, N_KEYS, TB])
        hot_a = sb("hot_a", W0 + 8 * KB, [P, HOT, 4, P])
        hot_b = sb("hot_b", W0 + 16 * KB, [P, HOT, 4, P])
        assert A0 + 128 * KB <= W0 + 8 * KB
        M0 = R0
        g_in = sb("g_in", M0, [P, 2, HALF])
        act_g = sb("act_g", M0 + 3 * KB, [P, 2, HALF])
        w_f = sb("w_f", M0 + 6 * KB, [P, 2, HALF])
        w_hi = sb("w_hi", M0 + 9 * KB, [P, 2, HALF], F32R)
        w_lo = sb("w_lo", M0 + 12 * KB, [P, 2, HALF], F32R)
        fgain = sb("fgain", M0 + 16 * KB, [P, D_MODEL])
        junk2 = sb("junk2", M0 + 20 * KB, [P, D_MODEL])

        ps = ctx.enter_context(nc.psum_tensor("ps", [P, 8, 512], F32))

        S = {n: sem(n) for n in (
            "pool_const", "const_in", "x_in", "mid_in", "late_in", "raw_in0", "raw_in1", "raw_in2", "raw_in3",
            "hi_ready", "lo_ready", "v_used", "ss_done", "ms_ready", "rms_ready", "src_ready", "tr_done",
            "hi_evac", "lo_evac", "t_done", "t_evac", "v_done", "v_evac", "band_in0", "band_in1", "band_ready",
            "na_scored", "na_max", "na_exp", "na_turned", "na_copied", "na_summed", "na_out",
            "rot_mm", "rot_c", "rot_s", "rot_done", "decay_arg", "decay_ready", "ret_qk_done", "ret_att",
            "ret_o", "ret_stat", "ret_copied", "ret_var", "ret_sd", "gate_silu", "gate_ready", "xa_in",
            "dve_step", "pool_step", "sc_done", "tk_first", "cand_ready", "tk_second", "tk_diff", "tk_exp", "tk_pos",
            "one_ready", "tk_chosen", "idx_turned", "idx_ready", "x2_out", "hot_ready", "hot_gated",
            "gate_mm", "gate_evac", "g_out0", "g_out1", "x2_in", "keys_in", "fg_in", "lg_arg", "pool_pass", "lg_exp",
            "u_in0", "u_in1", "v_in0", "v_in1", "g_in0", "g_in1", "u_hi", "u_lo", "v_hi", "v_lo",
            "a_done", "gelu_done", "w_ready", "w_hi_ready", "w_lo_ready", "y_done", "y_added", "y_out")}
        raw_in = [S[f"raw_in{i}"] for i in range(RING)]
        band_in = [S["band_in0"], S["band_in1"]]
        g_out = [S["g_out0"], S["g_out1"]]
        u_in, v_in = [S["u_in0"], S["u_in1"]], [S["v_in0"], S["v_in1"]]
        gate_in = [S["g_in0"], S["g_in1"]]

        def tile_cols(t):
            return slice(t * P, (t + 1) * P)

        def half_cols(m):
            return slice(m * HALF, (m + 1) * HALF)

        def is_token_major(c):
            return C_NA_V <= c < C_RET_QK or C_RET_V <= c < C_WQ

        def t_index(c):
            return c if c < C_NA_V else c - 4 if c < C_RET_V else c - 20

        def v_group(c):
            return {C_NA_V: 0, C_RET_V: 1, C_RET_G: 2, C_OUT: 3, C_OUT + 4: 4}[c - c % 4]

        def used(c):
            if not is_token_major(c):
                return S["t_done"], 2 * t_index(c) + 2
            return (S["v_done"], NT * v_group(c) + NT) if c % 4 == 3 else (S["v_used"], 3 * v_group(c) + c % 4 + 1)

        ret_units = [(h, q) for h in range(RET_HEADS) for q in range(2)]
        att_first = [0]
        for h, q in ret_units:
            att_first.append(att_first[-1] + SEQS[q][1])

        block = ctx.enter_context(nc.Block())

        @block.sync
        def _(sp):
            for t in range(NT):
                sp.dma_start(mix[:, t, :], a["x"][t]).then_inc(S["x_in"], 16)

            def load_chunk(c):
                if c >= RING:
                    sp.wait_ge(S["lo_ready"], c - RING + 1)
                sp.dma_start(raw[:, c % RING, :], a["front"][c]).then_inc(raw_in[c % RING], 16)

            for c in range(C_OUT):
                load_chunk(c)
            sp.wait_ge(S["ret_o"], len(ret_units))
            for t in range(NT):
                sp.dma_start(x_again[:, t, :], a["x"][t]).then_inc(S["xa_in"], 16)
            for c in range(C_OUT, C_END):
                load_chunk(c)
            sp.wait_ge(S["src_ready"], 3 * NT)
            sp.dma_start(a["x2_park"], x2[:, :, :]).then_inc(S["x2_out"], 16)
            for t in range(NT):
                sp.wait_ge(S["gate_evac"], 32 * (t + 1))
                sp.dma_start(a["gates"][:, :, tile_cols(t)].rearrange("i j t -> j i t"),
                             stage[:, t % 2]).then_inc(g_out[t % 2], 16)
            for k in range(2):
                sp.wait_ge(g_out[k], 16 * (NT // 2))
            sp.dma_start(x2[:, :, :], a["x2_park"]).then_inc(S["x2_in"], 16)

            def load_u(jj, row, par):
                sp.dma_start(raw[:, par, :], a["experts"][row, 0]).then_inc(u_in[par], 16)

            def load_v(jj, row, par):
                sp.dma_start(raw[:, 2 + par, :], a["experts"][row, 1]).then_inc(v_in[par], 16)

            def load_g(row, half, par):
                sp.dma_start(g_in[:, par, :], a["gates"][row, :, half_cols(half)]).then_inc(gate_in[par], 16)

            for par in range(2):
                load_u(par, par, par)
                load_v(par, par, par)
                load_g(par, 0, par)
            sp.wait_ge(S["u_lo"], 1)
            load_u(2, 2, 0)
            sp.wait_ge(S["u_lo"], 2)
            load_u(3, 3, 1)
            sp.wait_ge(S["v_lo"], 1)
            load_v(2, 2, 0)

            def step(jj, row, half, par, u_row, v_row, g_row, g_half):
                if g_row is not None:
                    sp.wait_ge(S["w_ready"], jj + 1)
                    load_g(g_row, g_half, par)
                if u_row is not None:
                    sp.wait_ge(S["u_lo"], jj + 3)
                    load_u(jj + 4, u_row, par)
                if v_row is not None:
                    sp.wait_ge(S["v_lo"], jj + 2)
                    load_v(jj + 3, v_row, 1 - par)

            def plain(jj):
                half = jj // N_KEYS
                last = 2 * N_KEYS
                step(jj, jj % N_KEYS, half, jj % 2,
                     (jj + 4) % N_KEYS if jj + 4 < last else None,
                     (jj + 3) % N_KEYS if jj + 3 < last else None,
                     (jj + 2) % N_KEYS if jj + 2 < last else None, (jj + 2) // N_KEYS)

            for half in range(2):
                with sp.Fori(0, N_KEYS // 2 - 2) as i:
                    for par in range(2):
                        row = i * 2 + par
                        step(row + half * N_KEYS, row, half, par, row + 4, row + 3, row + 2, half)
                for jj in range((half + 1) * N_KEYS - 4, (half + 1) * N_KEYS):
                    plain(jj)
            for t in range(NT):
                sp.wait_ge(S["y_out"], t + 1)
                sp.dma_start(a["y"][t], x2[:, t, :]).then_inc(S["late_in"], 16)
            sp.wait_ge(S["late_in"], 16 * NT)

        @block.gpsimd
        def _(pool):
            steps = Steps(pool, S["pool_step"])
            steps.add(pool.memset(s["ident"][:, :], 0.0))
            pool.iota(s["iota"][:, :], [[1, P]], base=0, channel_multiplier=0,
                      allow_small_or_imprecise_dtypes=True).then_inc(S["pool_const"], 1)
            steps.settle()
            pool.affine_select(out=s["ident"][:, :], in_=s["ident"][:, :], compare_op=ALU.not_equal, fill=1.0,
                               base=0, pattern=[[-1, P]], channel_multiplier=1).then_inc(S["pool_const"], 1)
            for dst, src in ((s["g1"], a["g1"]), (s["g2"], a["g2"]), (s["winmask"], a["winmask"])):
                pool.dma_start(dst[:, :], src).then_inc(S["const_in"], 16)
            pool.dma_start(s["dec_f"][:, :], a["dec_f"].partition_broadcast(P)).then_inc(S["const_in"], 16)
            pool.dma_start(s["dec_b"][:, :], a["dec_b"].partition_broadcast(P)).then_inc(S["const_in"], 16)
            pool.wait_ge(S["const_in"], 80)
            for h in range(NA_HEADS):
                if h >= 2:
                    pool.wait_ge(S["na_max"], NT * (h - 1))
                pool.dma_start(band[:, h % 2], a["band"][h].rearrange("p (r c) -> p r c", c=GRID_W)
                               ).then_inc(band_in[h % 2], 16)
                pool.wait_ge(band_in[h % 2], 16 * (h // 2 + 1))
                pool.tensor_tensor(band[:, h % 2], band[:, h % 2],
                                   s["winmask"][:, None, :].broadcast_to([P, BAND_ROWS, GRID_W]),
                                   ALU.add).then_inc(S["band_ready"], 1)
            pool.wait_ge(S["na_out"], UNITS)
            for dst, src in ((cos, a["cos"]), (sin, a["sin"]), (diff, a["diff"]), (perm, a["perm"])):
                pool.dma_start(dst[:, :], src).then_inc(S["mid_in"], 16)
            pool.dma_start(ngain[:, :], a["ret_norm"].partition_broadcast(P)).then_inc(S["mid_in"], 16)
            pool.wait_ge(S["mid_in"], 80)
            pool.wait_ge(S["t_evac"], 32)
            for r in range(16):
                if r >= 2:
                    pool.wait_ge(S["rot_done"], r - 1)
                pool.tensor_tensor(rot_cos[:, r % 2], ret_qk[:, r // 2, half_cols(r % 2)],
                                   cos[:, half_cols(r % 2)], ALU.mult).then_inc(S["rot_c"], 1)
            for t in range(NT):
                pool.wait_ge(S["gate_silu"], t + 1)
                pool.tensor_tensor(ret_gate[:, t], ret_gate[:, t], ngain[:, :], ALU.mult
                                   ).then_inc(S["gate_ready"], 1)
            pool.wait_ge(S["src_ready"], 3 * NT)
            pool.wait_ge(S["tr_done"], 3 * NT)
            pool.dma_start(keys_t[:, :, :], a["keys"]).then_inc(S["keys_in"], 16)

            def sums(t):
                pool.wait_ge(S["tk_first"], 4 * (t + 1))
                if t:
                    pool.wait_ge(S["tk_second"], t)
                v = tv[:, t % 2].rearrange("p (h two) k -> p h two k", two=2)
                pool.tensor_tensor(cand[:, :, :].rearrange("p h (x y) -> p h x y", x=TOPK),
                                   v[:, :, 0, :, None].broadcast_to([P, PEER_HEADS, TOPK, TOPK]),
                                   v[:, :, 1, None, :].broadcast_to([P, PEER_HEADS, TOPK, TOPK]),
                                   ALU.add).then_inc(S["cand_ready"], 1)

            def decode(t):
                pool.wait_ge(S["tk_pos"], t + 1)
                keys = tif[:, t % 2].rearrange("p (h two) k -> p h two k", two=2)
                for k, one in enumerate((one1, one2)):
                    o4 = one[:, :, :].rearrange("p (h k) j -> p h k j", h=PEER_HEADS)
                    pool.tensor_tensor(o4, o4, keys[:, :, k, None, :].broadcast_to([P, PEER_HEADS, TOPK, TOPK]),
                                       ALU.mult).then_inc(S["one_ready"], 1)

            sums(0)
            for t in range(NT):
                if t + 1 < NT:
                    sums(t + 1)
                decode(t)
            pool.wait_ge(S["idx_ready"], NT)
            def hold(ready, n):
                pool.wait_ge(ready, n)
                pool.sem_inc(S["pool_pass"], 1)

            with pool.Fori(0, TOK // (4 * HOT)) as i:
                for k in range(HOT):
                    hold(S["hot_ready"], i * HOT + (k + 1))
                    pool.tensor_tensor(hot_a[:, k], hot_a[:, k],
                                       idx_t[:, 2, bass.ds(i * (4 * HOT) + 4 * k, 4), None].broadcast_to([P, 4, P]),
                                       ALU.mult).then_inc(S["hot_gated"], 1)
            for k in range(2):
                pool.wait_ge(g_out[k], 16 * (NT // 2))
            pool.dma_start(fgain[:, :], a["fgain"].partition_broadcast(P)).then_inc(S["fg_in"], 16)

        @block.scalar
        def _(act):
            def hi(c):
                act.wait_ge(raw_in[c % RING], 16 * (c // RING + 1))
                if c >= RING:
                    act.wait_ge(*used(c - RING))
                act.activation(sp_hi[:, c % RING], raw[:, c % RING], ACT.Copy).then_inc(S["hi_ready"], 1)

            def squares(n, ready):
                src, scratch = (mix, junk) if n == 0 else (x2, junk) if n == 1 else (x2, junk2)
                for t in range(NT):
                    act.wait_ge(*ready(t))
                    if n + t:
                        act.wait_ge(S["ss_done"], NT * n + t)
                    act.activation(scratch[:, :], src[:, t, :], ACT.Square,
                                   accum_out=s["ssq"][:, NT * n + t:NT * n + t + 1]).then_inc(S["ss_done"], 1)
                act.wait_ge(S["ms_ready"], n + 1)
                act.activation(s["rms"][:, NT * n:NT * n + NT], s["ms"][:, NT * n:NT * n + NT],
                               ACT.Sqrt).then_inc(S["rms_ready"], 1)

            def turned_hi(n, gain):
                for t in range(NT):
                    tt = n * NT + t
                    act.wait_ge(S["tr_done"], tt + 1)
                    if n == 1:
                        act.wait_ge(*used(C_OUT - 1))
                    if n == 2:
                        act.wait_ge(*used(C_WQ - 1))
                    bank = 2 + 2 * (tt % 2)
                    for k in range(KD):
                        src = ps[:, bank + k // 4, (k % 4) * P:(k % 4 + 1) * P]
                        dst = ht_hi[:, k, tile_cols(t)]
                        if gain is None:
                            last = act.activation(dst, src, ACT.Copy)
                        else:
                            last = act.activation(dst, src, ACT.Copy, scale=gain[:, k:k + 1])
                    last.then_inc(S["hi_evac"], 1)

            def t_out(c, m, dst):
                n = 2 * t_index(c) + m
                act.wait_ge(S["t_done"], n + 1)
                act.activation(dst[:, half_cols(m)], ps[:, m, 0:HALF], ACT.Copy).then_inc(S["t_evac"], 1)

            for c in range(AHEAD):
                hi(c)
            squares(0, lambda t: (S["x_in"], 16 * NT))
            act.wait_ge(S["const_in"], 80)
            turned_hi(0, s["g1"])
            act.wait_ge(S["lg_arg"], 1)
            act.activation(s["lgt"][:, 8:16], s["lgt"][:, 16:24], ACT.Exp).then_inc(S["lg_exp"], 1)
            for c in range(C_NA_V):
                hi(c + AHEAD)
                for m in range(2):
                    t_out(c, m, na_qk[:, c, :])
            for c in range(C_NA_V, C_RET_QK):
                hi(c + AHEAD)
            for t in range(NT):
                act.wait_ge(S["v_done"], t + 1)
                act.activation(mix[:, t, WIDTH:], ps[:, 2 + t, :], ACT.Copy).then_inc(S["v_evac"], 1)
            for n in range(UNITS + 2):
                if n < UNITS:
                    L = SEQS[seq_of(n % NT)][1] * P
                    act.wait_ge(S["na_max"], n + 1)
                    if n >= 2:
                        act.wait_ge(S["na_turned"], n - 1)
                    act.activation(na_p[:, n % 2, 0:L], na_sc[:, n % 2, 0:L], ACT.Exp, bias=s["nmx"][:, n:n + 1],
                                   accum_out=s["psum_"][:, n:n + 1]).then_inc(S["na_exp"], 1)
                if 1 <= n <= UNITS:
                    u = n - 1
                    L = SEQS[seq_of(u % NT)][1] * P
                    act.wait_ge(S["na_turned"], u + 1)
                    if u >= 2:
                        act.wait_ge(S["na_summed"], u - 1)
                    act.activation(na_pt[:, u % 2, 0:L], ps[:, 4 + u % 2, 0:L], ACT.Copy
                                   ).then_inc(S["na_copied"], 1)
                c = C_RET_QK + n // 6
                if n < UNITS and n % 6 == 1:
                    hi(c + AHEAD)
                if n < UNITS and n % 6 == 3:
                    t_out(c, 0, ret_qk[:, c - C_RET_QK, :])
                if n and n <= UNITS and n % 6 == 0:
                    t_out(c - 1, 1, ret_qk[:, c - 1 - C_RET_QK, :])
            for g in range(2):
                for c in range(C_RET_V + 4 * g, C_RET_G + 4 * g):
                    if c + AHEAD < C_OUT:
                        hi(c + AHEAD)
                for t in range(NT):
                    act.wait_ge(S["v_done"], NT * (g + 1) + t + 1)
                    if g == 0:
                        act.activation(ret_v[:, t], ps[:, 2 + t, :], ACT.Copy).then_inc(S["v_evac"], 1)
                    else:
                        act.activation(ret_gate[:, t], ps[:, 2 + t, :], ACT.Silu).then_inc(S["gate_silu"], 1)
            for r, (h, q) in enumerate(ret_units):
                if q == 0:
                    act.wait_ge(S["decay_arg"], h + 1)
                    act.activation(dmat[:, h % 2], dmat[:, h % 2], ACT.Exp).then_inc(S["decay_ready"], 1)
                t0, n = SEQS[q]
                act.wait_ge(S["ret_stat"], r + 1)
                act.activation(mix[:, t0:t0 + n, WIDTH + h * P:WIDTH + (h + 1) * P],
                               ps[:, 6 + r % 2, 0:n * P].rearrange("p (t e) -> p t e", t=n),
                               ACT.Copy).then_inc(S["ret_copied"], 1)
            act.wait_ge(S["ret_var"], 1)
            act.activation(ret_std[:, :], ret_rs[:, :], ACT.Sqrt).then_inc(S["ret_sd"], 1)
            for c in range(C_OUT, C_OUT + AHEAD):
                hi(c)
            turned_hi(1, None)
            for c in range(C_OUT, C_WQ):
                hi(c + AHEAD)
            squares(1, lambda t: (S["v_evac"], 2 * NT + NT + t + 1))
            turned_hi(2, s["g2"])
            for c in range(C_WQ, C_END):
                if c + AHEAD < C_END:
                    hi(c + AHEAD)
                for m in range(2):
                    t_out(c, m, q_t[:, c - C_WQ, :])
            def turned_choice(t):
                act.wait_ge(S["idx_turned"], t + 1)
                act.activation(idx_t[:, :, tile_cols(t)], ps[:, 6, 0:3 * P].rearrange("p (c n) -> p c n", c=3),
                               ACT.Copy).then_inc(S["idx_ready"], 1)

            for t in range(NT):
                act.wait_ge(S["tk_diff"], t + 1)
                act.activation(gexp[:, t % 2], gexp[:, t % 2], ACT.Exp).then_inc(S["tk_exp"], 1)
                if t >= 2:
                    turned_choice(t - 2)
            for t in (NT - 2, NT - 1):
                turned_choice(t)
            act.wait_ge(S["x2_out"], 16)

            def gates_out(g, col, slot, k):
                act.wait_ge(S["gate_mm"], g + 1)
                act.activation(stage[:, slot, :, bass.ds(col, 4)],
                               ps[:, k, :].rearrange("p (t i) -> p i t", t=4), ACT.Copy
                               ).then_inc(S["gate_evac"], 1)

            for t in range(NT):
                if t >= 2:
                    act.wait_ge(g_out[t % 2], 16 * (t // 2))
                with act.Fori(0, P // (4 * HOT)) as i:
                    for k in range(HOT):
                        gates_out(i * HOT + (32 * t + k), i * (4 * HOT) + 4 * k, t % 2, k)

            def u_hi(jj, n_in, par):
                act.wait_ge(u_in[par], n_in)
                if not isinstance(jj, int) or jj >= 2:
                    act.wait_ge(S["a_done"], jj - 1)
                act.activation(sp_hi[:, par], raw[:, par], ACT.Copy).then_inc(S["u_hi"], 1)

            def v_hi(jj, n_in, par):
                act.wait_ge(v_in[par], n_in)
                if not isinstance(jj, int) or jj >= 2:
                    act.wait_ge(S["y_done"], jj - 1)
                act.activation(sp_hi[:, 2 + par], raw[:, 2 + par], ACT.Copy).then_inc(S["v_hi"], 1)

            def step(jj, i, par, first=False, last=False):
                act.wait_ge(S["a_done"], jj + 1)
                if not first:
                    act.wait_ge(S["w_ready"], jj - 1)
                act.activation(act_g[:, par], ps[:, 6 + par, 0:HALF], ACT.Gelu_apprx_tanh
                               ).then_inc(S["gelu_done"], 1)
                act.wait_ge(S["w_ready"], jj + 1)
                if not first:
                    act.wait_ge(S["y_done"], jj - 1)
                act.activation(w_hi[:, par], w_f[:, par], ACT.Copy).then_inc(S["w_hi_ready"], 1)
                if not last:
                    u_hi(jj + 2, i * 16 + 32, par)
                if not last or par == 0:
                    v_hi(jj + 1, i * 16 + (16 if par == 0 else 32), 1 - par)

            u_hi(0, 16, 0)
            u_hi(1, 16, 1)
            v_hi(0, 16, 0)
            for par in range(2):
                step(par, 0, par, first=True)
            with act.Fori(1, N_KEYS - 1) as i:
                for par in range(2):
                    step(i * 2 + par, i, par)
            for par in range(2):
                step(2 * N_KEYS - 2 + par, N_KEYS - 1, par, last=True)
            squares(2, lambda t: (S["y_added"], 2))

        @block.tensor
        def _(pe):
            def exact(out, lhs, rhs, start, stop):
                for k, (l, r) in enumerate(((lhs[0], rhs[0]), (lhs[0], rhs[1]), (lhs[1], rhs[0]))):
                    last = pe.matmul(out, l, r, start=start and k == 0, stop=stop and k == 2,
                                     skip_group_check=True)
                return last

            def turn(n, src):
                for t in range(NT):
                    tt = n * NT + t
                    pe.wait_ge(S["src_ready"], tt + 1)
                    if tt >= 2:
                        pe.wait_ge(S["lo_evac"], tt - 1)
                    bank = 2 + 2 * (tt % 2)
                    for k in range(KD):
                        last = pe.transpose(ps[:, bank + k // 4, (k % 4) * P:(k % 4 + 1) * P],
                                            src(t)[:, k * P:(k + 1) * P], s["ident"][:, :])
                    last.then_inc(S["tr_done"], 1)

            def t_part(c, m, part):
                n = 2 * t_index(c) + m
                sl = c % RING
                if part == 0:
                    pe.wait_ge(S["lo_ready"], c + 1)
                    if n >= 2:
                        pe.wait_ge(S["t_evac"], n - 1)
                for e in range(8 * part, 8 * part + 8):
                    k, which = e // 3, e % 3
                    w = (sp_hi, sp_hi, sp_lo)[which][:, sl, k * P:(k + 1) * P]
                    x = (ht_hi, ht_lo, ht_hi)[which][:, k, half_cols(m)]
                    last = pe.matmul(ps[:, m, 0:HALF], w, x, start=e == 0, stop=e == 23, skip_group_check=True)
                if part == 2:
                    last.then_inc(S["t_done"], 1)

            def v_chunk(c):
                g, cc, sl = v_group(c), c % 4, c % RING
                pe.wait_ge(S["lo_ready"], c + 1)
                for t in range(NT):
                    for kk in range(2):
                        k, cols = 2 * cc + kk, slice(kk * 512, kk * 512 + 512)
                        last = exact(ps[:, 2 + t, :], (ht_hi[:, k, tile_cols(t)], ht_lo[:, k, tile_cols(t)]),
                                     (sp_hi[:, sl, cols], sp_lo[:, sl, cols]), k == 0, k == KD - 1)
                    if cc == 3:
                        last.then_inc(S["v_done"], 1)
                if cc < 3:
                    last.then_inc(S["v_used"], 1)

            pe.wait_ge(S["pool_const"], 2)
            turn(0, lambda t: h_tile[:, t % 2])
            pe.wait_ge(S["lo_evac"], NT)
            for c in range(C_NA_V):
                for m in range(2):
                    for part in range(3):
                        t_part(c, m, part)
            for c in range(C_NA_V, C_RET_QK):
                v_chunk(c)
            pe.wait_ge(S["t_evac"], 2 * C_NA_V)
            pe.wait_ge(S["v_evac"], NT)
            for n in range(UNITS + 2):
                if n < UNITS:
                    h, t = n // NT, n % NT
                    t0, nt = SEQS[seq_of(t)]
                    part = slice(64 * (h % 2), 64 * (h % 2) + 64)
                    if n >= 2:
                        pe.wait_ge(S["na_max"], n - 1)
                    pe.matmul(ps[:, 2 + n % 2, 0:nt * P], na_qk[part, h // 2, tile_cols(t)],
                              na_qk[part, 4 + h // 2, t0 * P:(t0 + nt) * P], start=True, stop=True
                              ).then_inc(S["na_scored"], 1)
                if 1 <= n <= UNITS:
                    u = n - 1
                    nt = SEQS[seq_of(u % NT)][1]
                    pe.wait_ge(S["na_exp"], u + 1)
                    if u >= 2:
                        pe.wait_ge(S["na_copied"], u - 1)
                    for k in range(nt):
                        last = pe.transpose(ps[:, 4 + u % 2, tile_cols(k)], na_p[:, u % 2, tile_cols(k)],
                                            s["ident"][:, :])
                    last.then_inc(S["na_turned"], 1)
                if n >= 2:
                    u = n - 2
                    h, t = u // NT, u % NT
                    t0, nt = SEQS[seq_of(t)]
                    pe.wait_ge(S["na_copied"], u + 1)
                    if u >= 2:
                        pe.wait_ge(S["na_out"], u - 1)
                    for k in range(nt):
                        last = pe.matmul(ps[:, 6 + u % 2, 0:NA_DIM], na_pt[:, u % 2, tile_cols(k)],
                                         mix[:, t0 + k, WIDTH + h * NA_DIM:WIDTH + (h + 1) * NA_DIM],
                                         start=k == 0, stop=k == nt - 1)
                    last.then_inc(S["na_summed"], 1)
                if n < UNITS:
                    t_part(C_RET_QK + n // 6, n % 6 // 3, n % 3)
            pe.wait_ge(S["na_out"], UNITS)
            pe.wait_ge(S["mid_in"], 80)
            for c in range(C_RET_V, C_OUT):
                if c == C_RET_G:
                    pe.wait_ge(S["v_evac"], 2 * NT)
                v_chunk(c)
                for r in (2 * (c - C_RET_V), 2 * (c - C_RET_V) + 1):
                    if r == 0:
                        pe.wait_ge(S["t_evac"], 32)
                    if r >= 2:
                        pe.wait_ge(S["rot_s"], r - 1)
                    pe.matmul(ps[:, r % 2, 0:HALF], perm[:, :], ret_qk[:, r // 2, half_cols(r % 2)],
                              start=True, stop=True).then_inc(S["rot_mm"], 1)
            pe.wait_ge(S["rot_done"], 16)
            pe.wait_ge(S["gate_silu"], NT)
            for r, (h, q) in enumerate(ret_units):
                t0, nt = SEQS[q]
                cols = slice(t0 * P, (t0 + nt) * P)
                for k in range(nt):
                    n = att_first[r] + k
                    if n >= 4:
                        pe.wait_ge(S["ret_att"], n - 3)
                    pe.matmul(ps[:, 2 + n % 4, 0:nt * P], ret_qk[:, 4 + h, tile_cols(t0 + k)],
                              ret_qk[:, h, cols], start=True, stop=True).then_inc(S["ret_qk_done"], 1)
                pe.wait_ge(S["ret_att"], att_first[r + 1])
                if r >= 2:
                    pe.wait_ge(S["ret_stat"], r - 1)
                    pe.wait_ge(S["ret_copied"], r - 1)
                for t in range(nt):
                    for k in range(nt):
                        last = pe.matmul(ps[:, 6 + r % 2, tile_cols(t)], att[:, r % 2, k, tile_cols(t)],
                                         ret_v[:, t0 + k, h * P:(h + 1) * P], start=k == 0, stop=k == nt - 1,
                                         skip_group_check=True)
                last.then_inc(S["ret_o"], 1)
            turn(1, lambda t: mix[:, t, :])
            pe.wait_ge(S["lo_evac"], 2 * NT)
            for c in range(C_OUT, C_WQ):
                if c == C_OUT + 4:
                    pe.wait_ge(S["v_evac"], 3 * NT)
                v_chunk(c)
            turn(2, lambda t: h_tile[:, t % 2])
            pe.wait_ge(S["lo_evac"], 3 * NT)
            for c in range(C_WQ, C_END):
                for m in range(2):
                    for part in range(3):
                        t_part(c, m, part)
            def turn_choice(t):
                pe.wait_ge(S["tk_chosen"], t + 1)
                if t:
                    pe.wait_ge(S["idx_ready"], t)
                for k in range(3):
                    last = pe.transpose(ps[:, 6, tile_cols(k)], chosen[:, k, :], s["ident"][:, :])
                last.then_inc(S["idx_turned"], 1)

            pe.wait_ge(S["t_evac"], 64)
            pe.wait_ge(S["keys_in"], 16)
            for t in range(NT):
                for g in range(4):
                    if 4 * t + g >= 4:
                        pe.wait_ge(S["tk_first"], 4 * t + g - 3)
                    for k in range(4):
                        last = pe.matmul(ps[:, 2 + g, tile_cols(k)], q_t[:, 4 * g + k, tile_cols(t)],
                                         keys_t[:, 4 * g + k, :], start=True, stop=True, skip_group_check=True)
                    last.then_inc(S["sc_done"], 1)
                if t >= 2:
                    turn_choice(t - 2)
            for t in (NT - 2, NT - 1):
                turn_choice(t)
            pe.wait_ge(S["idx_ready"], NT)

            def gates(g, k, first=False):
                pe.wait_ge(S["hot_gated"], g + 1)
                if not first:
                    pe.wait_ge(S["gate_evac"], g - (HOT - 1))
                for q in range(4):
                    last = pe.matmul(ps[:, k, tile_cols(q)], hot_b[:, k, q, :], hot_a[:, k, q, :],
                                     start=True, stop=True, skip_group_check=True)
                last.then_inc(S["gate_mm"], 1)

            for k in range(HOT):
                gates(k, k, first=True)
            with pe.Fori(1, TOK // (4 * HOT)) as i:
                for k in range(HOT):
                    gates(i * HOT + k, k)

            def scores(jj, par, half, first=False):
                pe.wait_ge(S["u_lo"], jj + 1)
                if not first:
                    pe.wait_ge(S["gelu_done"], jj - 1)
                for k in range(KD):
                    w = slice(k * P, (k + 1) * P)
                    last = exact(ps[:, 6 + par, 0:HALF], (sp_hi[:, par, w], sp_lo[:, par, w]),
                                 (ht_hi[:, k, half_cols(half)], ht_lo[:, k, half_cols(half)]),
                                 k == 0, k == KD - 1)
                last.then_inc(S["a_done"], 1)

            def add_experts(jj, par, start=False, stop=False):
                pe.wait_ge(S["v_lo"], jj + 1)
                pe.wait_ge(S["w_lo_ready"], jj + 1)
                for t in range(TPH):
                    w = (w_hi[:, par, tile_cols(t)], w_lo[:, par, tile_cols(t)])
                    for c in range(2):
                        cols = slice(c * 512, c * 512 + 512)
                        last = exact(ps[:, 2 * t + c, :], w, (sp_hi[:, 2 + par, cols], sp_lo[:, 2 + par, cols]),
                                     start, stop)
                last.then_inc(S["y_done"], 1)

            scores(0, 0, 0, first=True)
            for half in range(2):
                j0 = half * N_KEYS
                scores(j0 + 1, 1, half, first=half == 0)
                if half:
                    pe.wait_ge(S["y_added"], 1)
                add_experts(j0, 0, start=True)
                scores(j0 + 2, 0, half)
                add_experts(j0 + 1, 1)
                with pe.Fori(1, N_KEYS // 2 - 1) as i:
                    for par in range(2):
                        scores(i * 2 + (j0 + par + 1), 1 - par, half)
                        add_experts(i * 2 + (j0 + par), par)
                scores(j0 + N_KEYS - 1, 1, half)
                add_experts(j0 + N_KEYS - 2, 0)
                if half == 0:
                    scores(N_KEYS, 0, 1)
                add_experts(j0 + N_KEYS - 1, 1, stop=True)

        @block.vector
        def _(dve):
            steps = Steps(dve, S["dve_step"])

            def lo(c):
                dve.wait_ge(S["hi_ready"], c + 1)
                dve.tensor_tensor(sp_lo[:, c % RING], raw[:, c % RING], sp_hi[:, c % RING].bitcast(F32),
                                  ALU.subtract).then_inc(S["lo_ready"], 1)

            def rstd(n):
                cols = slice(NT * n, NT * n + NT)
                dve.wait_ge(S["ss_done"], NT * (n + 1))
                dve.tensor_scalar(s["ms"][:, cols], s["ssq"][:, cols], 1.0 / D_MODEL, EPS, ALU.mult, ALU.add
                                  ).then_inc(S["ms_ready"], 1)
                dve.wait_ge(S["rms_ready"], n + 1)
                steps.add(dve.reciprocal(s["rstd"][:, cols], s["rms"][:, cols]))
                steps.settle()

            def normed(n, t):
                src, col = (mix, t) if n == 0 else (x2, NT + t)
                tt = n * NT + t
                if t >= 2:
                    dve.wait_ge(S["tr_done"], tt - 1)
                dve.tensor_scalar(h_tile[:, t % 2], src[:, t, :], s["rstd"][:, col:col + 1], None, ALU.mult
                                  ).then_inc(S["src_ready"], 1)

            def turned_lo(n, t, gain):
                tt = n * NT + t
                dve.wait_ge(S["hi_evac"], tt + 1)
                bank = 2 + 2 * (tt % 2)
                for k in range(KD):
                    src = ps[:, bank + k // 4, (k % 4) * P:(k % 4 + 1) * P]
                    hi_part = ht_hi[:, k, tile_cols(t)].bitcast(F32)
                    dst = ht_lo[:, k, tile_cols(t)]
                    if gain is None:
                        last = dve.tensor_tensor(dst, src, hi_part, ALU.subtract)
                    else:
                        last = dve.scalar_tensor_tensor(dst, src, gain[:, k:k + 1], hi_part, ALU.mult, ALU.subtract)
                last.then_inc(S["lo_evac"], 1)

            def log_decays():
                lg, w = s["lg"], s["lgt"]
                d, y, z, z2, acc = (w[:, 8 * k:8 * k + 8] for k in range(5))
                dve.wait_ge(S["const_in"], 80)
                for k, src in enumerate((s["dec_f"], s["dec_b"])):
                    steps.add(dve.tensor_copy(d[:, 4 * k:4 * k + 4], src[:, :]))
                steps.settle()
                dve.tensor_scalar(y, d, -1.0, None, ALU.mult).then_inc(S["dve_step"], 1)
                steps.n += 1
                steps.settle()
                steps.add(dve.tensor_tensor(y, y, d, ALU.min))
                steps.settle()
                dve.tensor_copy(z, y).then_inc(S["lg_arg"], 1)
                dve.wait_ge(S["lg_exp"], 1)
                steps.add(dve.tensor_scalar(z2, y, 2.0, None, ALU.add))
                steps.settle()
                steps.add(dve.reciprocal(z, z2))
                steps.settle()
                steps.add(dve.tensor_tensor(z, z, y, ALU.mult))
                steps.settle()
                steps.add(dve.tensor_tensor(z2, z, z, ALU.mult))
                steps.add(dve.memset(acc, 2.0 / 19))
                steps.settle()
                for odd in range(17, 0, -2):
                    steps.add(dve.tensor_tensor(acc, acc, z2, ALU.mult))
                    steps.settle()
                    steps.add(dve.tensor_scalar(acc, acc, 2.0 / odd, None, ALU.add))
                    steps.settle()
                steps.add(dve.tensor_tensor(acc, acc, z, ALU.mult))
                steps.add(dve.tensor_scalar(y, d, 0.0, None, ALU.min))
                steps.settle()
                steps.add(dve.tensor_tensor(lg[:, :], y, acc, ALU.subtract))
                steps.settle()
                steps.add(dve.tensor_scalar(lg[:, 4:8], lg[:, 4:8], -1.0, None, ALU.mult))

            for c in range(AHEAD):
                lo(c)
            rstd(0)
            dve.wait_ge(S["const_in"], 80)
            for t in range(NT):
                normed(0, t)
                if t:
                    turned_lo(0, t - 1, s["g1"])
            turned_lo(0, NT - 1, s["g1"])
            log_decays()
            for c in range(C_NA_V):
                lo(c + AHEAD)
            for c in range(C_NA_V, C_RET_QK):
                lo(c + AHEAD)
            for n in range(UNITS + 2):
                if n < UNITS:
                    h, t = n // NT, n % NT
                    q = seq_of(t)
                    L = SEQS[q][1] * P
                    row = (6 - 2 * (t - SEQS[q][0]))
                    dve.wait_ge(S["na_scored"], n + 1)
                    dve.wait_ge(S["band_ready"], h + 1)
                    if n >= 2:
                        dve.wait_ge(S["na_exp"], n - 1)
                    sc = na_sc[:, n % 2, 0:L]
                    steps.add(dve.scalar_tensor_tensor(
                        sc, ps[:, 2 + n % 2, 0:L], NA_DIM ** -0.5,
                        band[:, h % 2, row:row + L // GRID_W, :].rearrange("p r c -> p (r c)"),
                        ALU.mult, ALU.add))
                    steps.settle()
                    steps.add(dve.reduce_max(s["mx"][:, n:n + 1], sc, AX.X))
                    steps.settle()
                    dve.tensor_scalar(s["nmx"][:, n:n + 1], s["mx"][:, n:n + 1], -1.0, None, ALU.mult
                                      ).then_inc(S["na_max"], 1)
                if n >= 2:
                    u = n - 2
                    h, t = u // NT, u % NT
                    dve.wait_ge(S["na_exp"], u + 1)
                    steps.add(dve.reciprocal(s["prec"][:, u:u + 1], s["psum_"][:, u:u + 1]))
                    steps.settle()
                    dve.wait_ge(S["na_summed"], u + 1)
                    dve.tensor_scalar(mix[:, t, h * NA_DIM:(h + 1) * NA_DIM], ps[:, 6 + u % 2, 0:NA_DIM],
                                      s["prec"][:, u:u + 1], None, ALU.mult).then_inc(S["na_out"], 1)
                if n < UNITS and n % 6 == 1:
                    lo(C_RET_QK + n // 6 + AHEAD)
            dve.wait_ge(S["mid_in"], 80)
            for c in range(C_RET_V, C_OUT):
                if c + AHEAD < C_OUT:
                    lo(c + AHEAD)
                for r in (2 * (c - C_RET_V), 2 * (c - C_RET_V) + 1):
                    dve.wait_ge(S["rot_mm"], r + 1)
                    dve.tensor_tensor(rot_sin[:, r % 2], ps[:, r % 2, 0:HALF], sin[:, half_cols(r % 2)],
                                      ALU.mult).then_inc(S["rot_s"], 1)
                    dve.wait_ge(S["rot_s"], r + 1)
                    dve.wait_ge(S["rot_c"], r + 1)
                    dve.tensor_tensor(ret_qk[:, r // 2, half_cols(r % 2)], rot_cos[:, r % 2], rot_sin[:, r % 2],
                                      ALU.add).then_inc(S["rot_done"], 1)

            def decay_argument(h):
                steps.add(dve.tensor_scalar(back[:, :], diff[:, :], 0.0, s["lg"][:, 4 + h:5 + h], ALU.min, ALU.mult))
                steps.add(dve.tensor_scalar(dmat[:, h % 2], diff[:, :], 0.0, s["lg"][:, h:h + 1], ALU.max, ALU.mult))
                steps.settle()
                dve.tensor_tensor(dmat[:, h % 2], dmat[:, h % 2], back[:, :], ALU.add
                                  ).then_inc(S["decay_arg"], 1)

            dve.wait_ge(S["rot_done"], 16)
            dve.wait_ge(S["na_exp"], UNITS)
            decay_argument(0)
            for r, (h, q) in enumerate(ret_units):
                t0, nt = SEQS[q]
                L = nt * P
                if q == 0 and h + 1 < RET_HEADS:
                    dve.wait_ge(S["decay_arg"], h + 1)
                    decay_argument(h + 1)
                if r >= 2:
                    dve.wait_ge(S["ret_o"], r - 1)
                dve.wait_ge(S["decay_ready"], h + 1)
                for k in range(nt):
                    dve.wait_ge(S["ret_qk_done"], att_first[r] + k + 1)
                    off = 384 - k * P
                    dve.scalar_tensor_tensor(att[:, r % 2, k, 0:L], ps[:, 2 + (att_first[r] + k) % 4, 0:L],
                                             RET_DIM ** -0.5, dmat[:, h % 2, off:off + L], ALU.mult, ALU.mult
                                             ).then_inc(S["ret_att"], 1)
                dve.wait_ge(S["ret_o"], r + 1)
                for t in range(nt):
                    last = dve.bn_stats(stats[:, (t0 + t) * RET_HEADS + h, :], ps[:, 6 + r % 2, tile_cols(t)])
                last.then_inc(S["ret_stat"], 1)
            dve.wait_ge(S["ret_stat"], len(ret_units))
            for k in range(NT * RET_HEADS):
                last = dve.bn_aggr(mv[:, k, :], stats[:, k, :])
            steps.add(last)
            steps.settle()
            dve.tensor_scalar(ret_rs[:, :], mv[:, :, 1], EPS, None, ALU.add).then_inc(S["ret_var"], 1)
            dve.wait_ge(S["ret_sd"], 1)
            steps.add(dve.reciprocal(ret_rs[:, :], ret_std[:, :]))
            steps.settle()
            dve.wait_ge(S["ret_copied"], len(ret_units))
            dve.wait_ge(S["gate_ready"], NT)
            for t in range(NT):
                for h in range(RET_HEADS):
                    o = mix[:, t, WIDTH + h * P:WIDTH + (h + 1) * P]
                    k = t * RET_HEADS + h
                    last = dve.tensor_scalar(o, o, mv[:, k, 0:1], ret_rs[:, k:k + 1], ALU.subtract, ALU.mult)
                steps.add(last)
                steps.settle()
                dve.tensor_tensor(mix[:, t, WIDTH:], mix[:, t, WIDTH:], ret_gate[:, t], ALU.mult
                                  ).then_inc(S["src_ready"], 1)
            for c in range(C_OUT, C_OUT + AHEAD):
                lo(c)
            for t in range(NT):
                turned_lo(1, t, None)
            dve.wait_ge(S["xa_in"], 16 * NT)
            for half in range(2):
                for c in range(C_OUT + 4 * half, C_OUT + 4 * half + 4):
                    lo(c + AHEAD)
                cols = slice(half * 512, half * 512 + 512)
                for t in range(NT):
                    dve.wait_ge(S["v_done"], NT * (3 + half) + t + 1)
                    dve.tensor_tensor(x2[:, t, cols], ps[:, 2 + t, :], x_again[:, t, cols], ALU.add
                                      ).then_inc(S["v_evac"], 1)
            rstd(1)
            for t in range(NT):
                normed(1, t)
                if t:
                    turned_lo(2, t - 1, s["g2"])
            turned_lo(2, NT - 1, s["g2"])
            for c in range(C_WQ, C_END - AHEAD):
                lo(c + AHEAD)

            def best_keys(t):
                sl = t % 2
                for g in range(4):
                    dve.wait_ge(S["sc_done"], 4 * t + g + 1)
                    sc = [ps[:, 2 + g, tile_cols(k)] for k in range(4)]
                    ks = [4 * g + k for k in range(4)]
                    for k in range(4):
                        last = dve.max(tv[:, sl, ks[k], 0:8], sc[k])
                    steps.add(last)
                    steps.settle()
                    for k in range(4):
                        dve.max_index(ti[:, sl, ks[k], 0:8], tv[:, sl, ks[k], 0:8], sc[k])
                        last = dve.match_replace(rep[:, k, :], tv[:, sl, ks[k], 0:8], sc[k], imm_value=-3e38)
                    steps.add(last)
                    steps.settle()
                    for k in range(4):
                        last = dve.max(tv[:, sl, ks[k], 8:16], rep[:, k, :])
                    steps.add(last)
                    steps.settle()
                    for k in range(4):
                        last = dve.max_index(ti[:, sl, ks[k], 8:16], tv[:, sl, ks[k], 8:16], rep[:, k, :])
                    last.then_inc(S["tk_first"], 1)

            def best_pairs(t):
                sl = t % 2
                dve.wait_ge(S["cand_ready"], t + 1)
                hs = range(PEER_HEADS)
                for h in hs:
                    last = dve.max(bv[:, h, 0:8], cand[:, h, :])
                steps.add(last)
                steps.settle()
                for h in hs:
                    last = dve.max_index(bp[:, h, 0:8], bv[:, h, 0:8], cand[:, h, :])
                for h in hs:
                    last = dve.match_replace(cand[:, h, :], bv[:, h, 0:8], cand[:, h, :], imm_value=-3e38)
                steps.add(last)
                steps.settle()
                for h in hs:
                    last = dve.max(bv[:, h, 8:16], cand[:, h, :])
                steps.add(last)
                steps.settle()
                for h in hs:
                    last = dve.max_index(bp[:, h, 8:16], bv[:, h, 8:16], cand[:, h, :])
                last.then_inc(S["tk_second"], 1)
                dve.wait_ge(S["tk_second"], t + 1)
                dve.tensor_tensor(gexp[:, sl], bv[:, :, :], bv[:, :, 0:1].broadcast_to([P, PEER_HEADS, TOPK]),
                                  ALU.subtract).then_inc(S["tk_diff"], 1)
                flat = bp[:, :, :].rearrange("p h k -> p (h k)")
                steps.add(dve.tensor_scalar(pa[:, 0, :], flat, 4, None, ALU.logical_shift_right))
                steps.add(dve.tensor_scalar(pa[:, 1, :], flat, 15, None, ALU.bitwise_and))
                steps.settle()
                dve.tensor_copy(paf[:, sl], pa[:, 0, :])
                dve.tensor_copy(pbf[:, sl], pa[:, 1, :])
                steps.add(dve.tensor_copy(tif[:, sl], ti[:, sl]))

            def hot_ranks(t):
                steps.settle()
                if t:
                    dve.wait_ge(S["tk_chosen"], t)
                for one, pos in ((one1, paf), (one2, pbf)):
                    last = dve.tensor_tensor(one[:, :, :], pos[:, t % 2, :, None].broadcast_to([P, P, TOPK]),
                                             s["iota"][:, None, 0:TOPK].broadcast_to([P, P, TOPK]), ALU.is_equal)
                last.then_inc(S["tk_pos"], 1)

            def choices(t):
                sl = t % 2
                dve.wait_ge(S["tk_exp"], t + 1)
                if t:
                    dve.wait_ge(S["idx_turned"], t)
                steps.add(dve.reduce_sum(gsum[:, :], gexp[:, sl], AX.X))
                steps.settle()
                steps.add(dve.reciprocal(grec[:, :], gsum[:, :]))
                steps.settle()
                dve.tensor_tensor(chosen[:, 2, :].rearrange("p (h k) -> p h k", h=PEER_HEADS), gexp[:, sl],
                                  grec[:, :, None].broadcast_to([P, PEER_HEADS, TOPK]), ALU.mult)
                for k, one in enumerate((one1, one2)):
                    dve.wait_ge(S["one_ready"], 2 * t + k + 1)
                    last = dve.reduce_sum(chosen[:, k, :], one[:, :, :], AX.X)
                last.then_inc(S["tk_chosen"], 1)

            best_keys(0)
            for t in range(NT):
                if t + 1 < NT:
                    best_keys(t + 1)
                best_pairs(t)
                if t:
                    choices(t - 1)
                hot_ranks(t)
            choices(NT - 1)
            dve.wait_ge(S["idx_ready"], NT)

            def hot(g, token, k, first=False):
                if not first:
                    dve.wait_ge(S["gate_mm"], g - (HOT - 1))
                for c, dst in ((1, hot_b), (0, hot_a)):
                    last = dve.tensor_tensor(dst[:, k], s["iota"][:, None, :].broadcast_to([P, 4, P]),
                                             idx_t[:, c, bass.ds(token, 4), None].broadcast_to([P, 4, P]),
                                             ALU.is_equal)
                last.then_inc(S["hot_ready"], 1)

            for k in range(HOT):
                hot(k, 4 * k, k, first=True)
            with dve.Fori(1, TOK // (4 * HOT)) as i:
                for k in range(HOT):
                    hot(i * HOT + k, i * (4 * HOT) + 4 * k, k)

            def part(jj, which, par, slot):
                dve.wait_ge(S[which + "_hi"], jj + 1)
                dve.tensor_tensor(sp_lo[:, slot], raw[:, slot], sp_hi[:, slot].bitcast(F32), ALU.subtract
                                  ).then_inc(S[which + "_lo"], 1)

            def step(jj, i, par, last=False):
                dve.wait_ge(S["gelu_done"], jj + 1)
                dve.wait_ge(gate_in[par], i * 16 + 16)
                dve.tensor_tensor(w_f[:, par], act_g[:, par], g_in[:, par], ALU.mult).then_inc(S["w_ready"], 1)
                dve.wait_ge(S["w_hi_ready"], jj + 1)
                dve.tensor_tensor(w_lo[:, par], w_f[:, par], w_hi[:, par].bitcast(F32), ALU.subtract
                                  ).then_inc(S["w_lo_ready"], 1)
                if not last:
                    part(jj + 2, "u", par, par)
                if not last or par == 0:
                    part(jj + 1, "v", 1 - par, 2 + 1 - par)

            part(0, "u", 0, 0)
            part(1, "u", 1, 1)
            part(0, "v", 0, 2)
            for half in range(2):
                n = N_KEYS // 2
                with dve.Fori(n * half, n * (half + 1) - half) as i:
                    for par in range(2):
                        step(i * 2 + par, i, par)
                if half:
                    for par in range(2):
                        step(2 * N_KEYS - 2 + par, N_KEYS - 1, par, last=True)
                else:
                    dve.wait_ge(S["x2_in"], 16)
                dve.wait_ge(S["y_done"], N_KEYS * (half + 1))
                for t in range(TPH):
                    for c in range(2):
                        o = x2[:, half * TPH + t, c * 512:c * 512 + 512]
                        last = dve.tensor_tensor(o, ps[:, 2 * t + c, :], o, ALU.add)
                last.then_inc(S["y_added"], 1)
            rstd(2)
            dve.wait_ge(S["fg_in"], 16)
            for t in range(NT):
                col = 2 * NT + t
                dve.scalar_tensor_tensor(x2[:, t, :], x2[:, t, :], s["rstd"][:, col:col + 1], fgain[:, :],
                                         ALU.mult, ALU.mult).then_inc(S["y_out"], 1)


def shape_constants():
    f = np.float32
    d = RET_DIM
    inv = (f(1.0) / (f(10000.0) ** (np.arange(0, d, 2, dtype=f) / f(d)))).astype(f)
    pos = np.concatenate([np.arange(SEQ), np.arange(DEC_SEQ)]).astype(f)
    ang = (inv[:, None] * pos[None, :]).astype(f)
    cos, sin = np.cos(ang), np.sin(ang)
    perm = np.zeros((P, P), f)
    for i in range(P // 2):
        perm[i + P // 2, i] = -1.0
        perm[i, i + P // 2] = 1.0
    diff = (np.arange(DIFF)[None, :] - 384 - np.arange(P)[:, None]).astype(f)
    start = np.clip(np.arange(GRID_W) - NA_COLS // 2, 0, GRID_W - NA_COLS)
    c = np.arange(GRID_W)
    inside = (c[None, :] >= start[:, None]) & (c[None, :] < start[:, None] + NA_COLS)
    mask = np.where(inside, 0.0, NEG).astype(f)
    return {"cos": np.concatenate([cos, cos]).astype(f), "sin": np.concatenate([sin, sin]).astype(f),
            "perm": perm, "diff": diff, "winmask": np.concatenate([mask, mask])}


def laid_out(x_prompt, x_sample, norm1_g, w_in, na_rpb, ret_decay_fwd, ret_decay_bwd, ret_norm_g, w_out,
             norm2_g, peer_w_q, peer_sub_keys, peer_u, peer_v, final_g):
    x = np.concatenate([x_prompt[0], x_sample[0]]).reshape(NT, P, D_MODEL)

    def stationary(w):
        n = w.shape[1] // P
        return w.reshape(KD, P, n, P).transpose(2, 1, 0, 3).reshape(n, P, 1024)

    def moving(w):
        n = w.shape[1] // 512
        return w.reshape(4, 2, P, n, 512).transpose(3, 0, 2, 1, 4).reshape(4 * n, P, 1024)

    w = w_in[0]
    cut = [w[:, 512 * k:512 * k + 512] for k in range(7)]
    front = np.concatenate([stationary(cut[0]), stationary(cut[1]), moving(cut[2]), stationary(cut[3]),
                            stationary(cut[4]), moving(cut[5]), moving(cut[6]), moving(w_out[0]),
                            stationary(peer_w_q[0])])
    u = peer_u[0].reshape(N_KEYS, N_KEYS, KD, P).transpose(0, 3, 2, 1).reshape(N_KEYS, 1, P, 1024)
    v = peer_v[0].reshape(N_KEYS, 1, P, 1024)
    par = np.arange(2)[:, None, None, None]
    qc = np.arange(GRID_W)[None, :, None, None]
    off = np.arange(BAND_ROWS)[None, None, :, None]
    kc = np.arange(GRID_W)[None, None, None, :]
    col = np.clip(kc - qc + NA_COLS - 1, 0, 2 * NA_COLS - 2)
    band = na_rpb[0][:, off + 1 - par, col].reshape(NA_HEADS, P, BAND_ROWS * GRID_W)
    out = {"x": x, "front": front, "experts": np.concatenate([u, v], axis=1), "band": band,
           "g1": norm1_g[0].reshape(KD, P).T, "g2": norm2_g[0].reshape(KD, P).T,
           "dec_f": ret_decay_fwd[0], "dec_b": ret_decay_bwd[0], "ret_norm": ret_norm_g[0], "fgain": final_g,
           "keys": peer_sub_keys[0].reshape(16, N_KEYS, P).transpose(2, 0, 1)}
    out.update(shape_constants())
    return {k: np.ascontiguousarray(v) for k, v in out.items()}


def kernel(**inputs):
    import concourse.bacc as bacc
    from concourse.bass_utils import run_bass_kernel_spmd

    nc = bacc.Bacc("TRN2", target_bir_lowering=False, num_devices=1)
    arrays, aps = {}, {}
    for name, v in laid_out(**{k: np.asarray(x) for k, x in inputs.items()}).items():
        arrays[f"in_{name}"] = v
        aps[name] = nc.dram_tensor(f"in_{name}", v.shape, mybir.dt.from_np(v.dtype), kind="ExternalInput").ap()
    aps["gates"] = nc.dram_tensor("gates", (N_KEYS, N_KEYS, TOK), F32, kind="Internal").ap()
    aps["x2_park"] = nc.dram_tensor("x2_park", (P, NT, D_MODEL), F32, kind="Internal").ap()
    aps["y"] = nc.dram_tensor("out_y", (NT, P, D_MODEL), F32, kind="ExternalOutput").ap()
    encoder_program(nc, aps)
    got = run_bass_kernel_spmd(nc, [arrays], core_ids=[0]).results[0]["out_y"]
    y = got.reshape(TOK, D_MODEL)
    return y[:SEQ].reshape(1, SEQ, D_MODEL), y[SEQ:].reshape(1, DEC_SEQ, D_MODEL)
```

```python
import math
from contextlib import ExitStack

import concourse.bass as bass
import numpy as np
from concourse import mybir

F32 = mybir.dt.float32
F32R = mybir.dt.float32r
U32 = mybir.dt.uint32
ALU = mybir.AluOpType
ACT = mybir.ActivationFunctionType
AX = mybir.AxisListType

P = 128
D_MODEL = 1024
SEQ, DEC_SEQ = 256, 512
NT = (SEQ + DEC_SEQ) // P
TOK = NT * P
HALF = TOK // 2
TPH = NT // 2
KD = D_MODEL // P
GRID_W = 64
NA_HEADS, NA_DIM, NA_COLS, NA_ROWS = 8, 64, 16, 8
RET_HEADS, RET_DIM = 4, 128
WIDTH = 512
PEER_HEADS, TOPK, N_KEYS = 8, 16, 128
EPS = 1e-6
SEQS = [(0, SEQ // P), (SEQ // P, DEC_SEQ // P)]

C_NA_QK, C_NA_V, C_RET_QK, C_RET_V, C_RET_G, C_OUT, C_WQ, C_END = 0, 8, 12, 20, 24, 28, 36, 52
RING = 4
AHEAD = 3
BAND_ROWS = 14
DIFF = 896
EARLY = 32
PERIODS = [6, 4, 6, 4, 6, 4]
HOT = 4
UNITS = NA_HEADS * NT
NEG = -1e30


def seq_of(tile):
    return 0 if tile < SEQS[1][0] else 1


class Steps:

    def __init__(self, eng, sem):
        self.eng, self.sem, self.n = eng, sem, 0

    def add(self, ins):
        ins.then_inc(self.sem, 1)
        self.n += 1

    def settle(self):
        self.eng.wait_ge(self.sem, self.n)


def encoder_program(nc, a):
    KB = 1024
    base0 = -(-nc.sbuf_base // 32) * 32
    ctx = ExitStack()
    with ctx:
        def sb(name, at, shape, dt=F32):
            n = int(np.prod(shape[1:])) * 4
            assert base0 + at + n <= nc.sbuf_usable_end, (name, at, n)
            return nc.alloc_sbuf_tensor_at(name, shape, dt, offset=base0 + at)

        def sem(name):
            return ctx.enter_context(nc.semaphore(name))

        ht_hi = sb("ht_hi", 0, [P, KD, TOK], F32R)
        ht_lo = sb("ht_lo", 24 * KB, [P, KD, TOK], F32R)
        at = 48 * KB
        small = {}
        for name, cols in (("ident", 128), ("iota", 128), ("g1", KD), ("g2", KD), ("dec_f", 4), ("dec_b", 4),
                           ("lg", 8), ("lgt", 40), ("ssq", 3 * NT), ("ms", 3 * NT), ("rms", 3 * NT),
                           ("rstd", 3 * NT), ("mx", UNITS), ("nmx", UNITS), ("psum_", UNITS), ("prec", UNITS),
                           ("winmask", GRID_W)):
            small[name] = sb(name, at, [P, cols])
            at += -(-cols * 4 // 32) * 32
        s = small
        A0 = -(-at // 256) * 256
        assert A0 <= 52 * KB

        mix = sb("mix", A0, [P, NT, D_MODEL])
        x2 = sb("x2", A0, [P, NT, D_MODEL])
        raw = sb("raw", A0 + 24 * KB, [P, RING, 1024])
        sp_hi = sb("sp_hi", A0 + 40 * KB, [P, RING, 1024], F32R)
        sp_lo = sb("sp_lo", A0 + 56 * KB, [P, RING, 1024], F32R)
        R0 = A0 + 72 * KB
        na_qk = sb("na_qk", R0, [P, 8, TOK])
        ret_v = sb("ret_v", R0, [P, NT, WIDTH])
        ret_gate = sb("ret_gate", R0 + 12 * KB, [P, NT, WIDTH])
        ret_qk = sb("ret_qk", R0 + 24 * KB, [P, 8, TOK])
        x_again = sb("x_again", R0 + 24 * KB, [P, NT, D_MODEL])
        W0 = R0 + 48 * KB
        h_tile = sb("h_tile", W0, [P, 2, D_MODEL])
        junk = sb("junk", W0 + 8 * KB, [P, D_MODEL])
        band = sb("band", W0 + 12 * KB, [P, 2, BAND_ROWS, GRID_W])
        na_sc = sb("na_sc", W0 + 19 * KB, [P, 2, 512])
        na_p = sb("na_p", W0 + 23 * KB, [P, 2, 512])
        na_pt = sb("na_pt", W0 + 27 * KB, [P, 2, 512])
        att = sb("att", W0, [P, 2, 4, 512])
        rot_sin = sb("rot_sin", W0, [P, 2, HALF])
        rot_cos = sb("rot_cos", W0 + 4 * KB, [P, 2, HALF])
        dmat = sb("dmat", W0 + 16 * KB, [P, 2, DIFF])
        diff = sb("diff", W0 + 23 * KB, [P, DIFF])
        cos = sb("cos", W0 + 26 * KB + 512, [P, TOK])
        sin = sb("sin", W0 + 29 * KB + 512, [P, TOK])
        back = sb("back", W0 + 26 * KB + 512, [P, DIFF])
        ngain = sb("ngain", W0 + 32 * KB + 512, [P, WIDTH])
        perm = sb("perm", W0 + 34 * KB + 512, [P, P])
        stats = sb("stats", W0 + 35 * KB, [P, NT * RET_HEADS, 6])
        mv = sb("mv", W0 + 35 * KB + 576, [P, NT * RET_HEADS, 2])
        ret_std = sb("ret_std", W0 + 35 * KB + 768, [P, NT * RET_HEADS])
        ret_rs = sb("ret_rs", W0 + 35 * KB + 864, [P, NT * RET_HEADS])

        q_t = sb("q_t", R0, [P, 16, TOK])
        keys_t = sb("keys_t", W0 + 12 * KB, [P, 16, N_KEYS])
        cand = sb("cand", A0 + 32 * KB, [P, PEER_HEADS, 256])
        one1 = sb("one1", A0 + 48 * KB, [P, P, TOPK])
        one2 = sb("one2", A0 + 64 * KB, [P, P, TOPK])
        rep = sb("rep", W0, [P, 4, N_KEYS])
        tv = sb("tv", W0 + 2 * KB, [P, 2, 16, TOPK])
        ti = sb("ti", W0 + 4 * KB, [P, 2, 16, TOPK], U32)
        tif = sb("tif", W0 + 6 * KB, [P, 2, 16, TOPK])
        early_g = sb("early_g", W0 + 8 * KB, [P, 2, HALF])
        T0 = W0 + 20 * KB
        bv = sb("bv", T0, [P, PEER_HEADS, TOPK])
        bp = sb("bp", T0 + 512, [P, PEER_HEADS, TOPK], U32)
        pa = sb("pa", T0 + 1024, [P, 2, P], U32)
        paf = sb("paf", T0 + 2048, [P, 2, P])
        pbf = sb("pbf", T0 + 3072, [P, 2, P])
        gexp = sb("gexp", T0 + 4096, [P, 2, PEER_HEADS, TOPK])
        gsum = sb("gsum", T0 + 5120, [P, PEER_HEADS])
        grec = sb("grec", T0 + 5152, [P, PEER_HEADS])
        chosen = sb("chosen", T0 + 5632, [P, 3, P])
        idx_t = sb("idx_t", W0 + 28 * KB, [P, 3, TOK])
        TB = P
        stage = sb("stage", A0, [P, 2, N_KEYS, TB])
        hot_a = sb("hot_a", W0 + 8 * KB, [P, HOT, 4, P])
        hot_b = sb("hot_b", W0 + 16 * KB, [P, HOT, 4, P])
        assert A0 + 128 * KB <= W0 + 8 * KB
        m_hi = sb("m_hi", A0 + 40 * KB, [P, 8, 1024], F32R)
        m_lo = sb("m_lo", A0 + 72 * KB, [P, 8, 1024], F32R)
        M0 = A0 + 104 * KB
        g_in = sb("g_in", M0, [P, 2, HALF])
        act_g = sb("act_g", M0 + 3 * KB, [P, 2, HALF])
        w_f = sb("w_f", M0 + 6 * KB, [P, 2, HALF])
        w_hi = sb("w_hi", M0 + 9 * KB, [P, 2, HALF], F32R)
        w_lo = sb("w_lo", M0 + 12 * KB, [P, 2, HALF], F32R)
        fgain = sb("fgain", M0 + 16 * KB, [P, D_MODEL])
        junk2 = sb("junk2", M0 + 20 * KB, [P, D_MODEL])

        ps = ctx.enter_context(nc.psum_tensor("ps", [P, 8, 512], F32))

        S = {n: sem(n) for n in (
            "pool_const", "const_in", "x_in", "mid_in", "late_in", "raw_in0", "raw_in1", "raw_in2", "raw_in3",
            "hi_ready", "lo_ready", "v_used", "ss_done", "ms_ready", "rms_ready", "src_ready", "tr_done",
            "hi_evac", "lo_evac", "t_done", "t_evac", "v_done", "v_evac", "band_in0", "band_in1", "band_ready",
            "na_scored", "na_max", "na_exp", "na_turned", "na_copied", "na_summed", "na_out",
            "rot_mm", "rot_c", "rot_s", "rot_done", "decay_arg", "decay_ready", "ret_qk_done", "ret_att",
            "ret_o", "ret_stat", "ret_copied", "ret_var", "ret_sd", "gate_silu", "gate_ready", "xa_in",
            "dve_step", "pool_step", "sc_done", "tk_first", "cand_ready", "tk_second", "tk_diff", "tk_exp", "tk_pos",
            "one_ready", "tk_chosen", "idx_turned", "idx_ready", "x2_out", "hot_ready", "hot_gated",
            "gate_mm", "gate_evac", "g_out0", "g_out1", "x2_in", "keys_in", "fg_in", "lg_arg", "pool_pass", "lg_exp",
            "u_in0", "u_in1", "v_in0", "v_in1", "g_in0", "g_in1", "act_in0", "act_in1", "early_out0", "early_out1", "u_hi", "u_lo", "v_hi", "v_lo",
            "a_done", "gelu_done", "w_ready", "w_hi_ready", "w_lo_ready", "y_done", "y_added", "y_out")}
        raw_in = [S[f"raw_in{i}"] for i in range(RING)]
        band_in = [S["band_in0"], S["band_in1"]]
        g_out = [S["g_out0"], S["g_out1"]]
        u_in, v_in = [S["u_in0"], S["u_in1"]], [S["v_in0"], S["v_in1"]]
        gate_in = [S["g_in0"], S["g_in1"]]
        act_in, early_out = [S["act_in0"], S["act_in1"]], [S["early_out0"], S["early_out1"]]

        ITERS, EARLY_ITERS = N_KEYS // 4, EARLY // 4

        def row_of(i, e):
            return i * 4 + (2 * (e // 4) + e % 2)

        def half_of(e):
            return e // 2 % 2

        def slot_of(e):
            return 2 * (e // 4 % 2) + e % 2

        def positive(n):
            return not isinstance(n, int) or n > 0

        def tile_cols(t):
            return slice(t * P, (t + 1) * P)

        def half_cols(m):
            return slice(m * HALF, (m + 1) * HALF)

        def is_token_major(c):
            return C_NA_V <= c < C_RET_QK or C_RET_V <= c < C_WQ

        def t_index(c):
            return c if c < C_NA_V else c - 4 if c < C_RET_V else c - 20

        def v_group(c):
            return {C_NA_V: 0, C_RET_V: 1, C_RET_G: 2, C_OUT: 3, C_OUT + 4: 4}[c - c % 4]

        def used(c):
            if not is_token_major(c):
                return S["t_done"], 2 * t_index(c) + 2
            return (S["v_done"], NT * v_group(c) + NT) if c % 4 == 3 else (S["v_used"], 3 * v_group(c) + c % 4 + 1)

        ret_units = [(h, q) for h in range(RET_HEADS) for q in range(2)]
        att_first = [0]
        for h, q in ret_units:
            att_first.append(att_first[-1] + SEQS[q][1])

        block = ctx.enter_context(nc.Block())

        @block.sync
        def _(sp):
            for t in range(NT):
                sp.dma_start(mix[:, t, :], a["x"][t]).then_inc(S["x_in"], 16)

            def load_chunk(c):
                if c >= RING:
                    sp.wait_ge(S["lo_ready"], c - RING + 1)
                sp.dma_start(raw[:, c % RING, :], a["front"][c]).then_inc(raw_in[c % RING], 16)

            for c in range(C_OUT):
                load_chunk(c)
            sp.wait_ge(S["ret_o"], len(ret_units))
            for t in range(NT):
                sp.dma_start(x_again[:, t, :], a["x"][t]).then_inc(S["xa_in"], 16)
            for c in range(C_OUT, C_END):
                load_chunk(c)
            sp.wait_ge(S["src_ready"], 3 * NT)
            sp.dma_start(a["x2_park"], x2[:, :, :]).then_inc(S["x2_out"], 16)

            def load_u(row, par):
                sp.dma_start(raw[:, par, :], a["experts"][row, 0]).then_inc(u_in[par], 16)

            def load_v(row, par):
                sp.dma_start(raw[:, 2 + par, :], a["experts"][row, 1]).then_inc(v_in[par], 16)

            for par in range(2):
                sp.wait_ge(S["lo_ready"], C_END - RING + par + 1)
                load_u(par, par)

            def early(row, par, more=True):
                if more:
                    sp.wait_ge(S["u_lo"], row + 1)
                    load_u(row + 2, par)
                for m in range(2):
                    sp.wait_ge(S["gelu_done"], row * 2 + (m + 1))
                    sp.dma_start(a["early"][row, m], early_g[:, m]).then_inc(early_out[m], 16)

            with sp.Fori(0, EARLY // 2 - 1) as i:
                for par in range(2):
                    early(i * 2 + par, par)
            for par in range(2):
                early(EARLY - 2 + par, par, more=False)
            for t in range(NT):
                sp.wait_ge(S["gate_evac"], 32 * (t + 1))
                sp.dma_start(a["gates"][:, :, tile_cols(t)].rearrange("i j t -> j i t"),
                             stage[:, t % 2]).then_inc(g_out[t % 2], 16)
            sp.wait_ge(g_out[0], 16 * (NT // 2))
            for par in range(2):
                load_v(par, par)
                load_u(EARLY + par, par)
            sp.dma_start(x2[:, :, :], a["x2_park"]).then_inc(S["x2_in"], 16)
            sp.wait_ge(g_out[1], 16 * (NT // 2))
            for m in range(2):
                sp.wait_ge(early_out[m], 16 * EARLY)

            def load_gates(i, e, par):
                sp.dma_start(g_in[:, par, :], a["gates"][row_of(i, e), :, half_cols(half_of(e))]
                             ).then_inc(gate_in[par], 16)

            def load_act(i, e, par):
                sp.dma_start(act_g[:, par, :], a["early"][row_of(i, e), half_of(e)]).then_inc(act_in[par], 16)

            for e in range(2):
                load_gates(0, e, e)
                load_act(0, e, e)
            for par in range(2):
                sp.wait_ge(S["v_lo"], par + 1)
                load_v(2 + par, par)
            for par in range(2):
                sp.wait_ge(S["u_lo"], EARLY + par + 1)
                load_u(EARLY + 2 + par, par)

            def step(i, e, early, end=False):
                r, par = e % 4 // 2, e % 2
                row = i * 4 + (2 * (e // 4) + 2 + r)
                if not (end and e >= 6):
                    sp.wait_ge(S["w_ready"], i * 8 + (e + 1))
                    load_gates(i, e + 2, par)
                    if early and not (end and e >= 6):
                        load_act(i, e + 2, par)
                if par == 0 and not early and not (end and e >= 0):
                    sp.wait_ge(S["u_lo"], row + 1)
                    load_u(row + 2, r)
                if par == 1 and not (end and not early):
                    sp.wait_ge(S["v_lo"], row + 1)
                    load_v(row + 2, r)

            with sp.Fori(0, EARLY_ITERS - 1) as i:
                for e in range(8):
                    step(i, e, True)
            for e in range(8):
                step(EARLY_ITERS - 1, e, early=e < 6)
            with sp.Fori(EARLY_ITERS, ITERS - 1) as i:
                for e in range(8):
                    step(i, e, False)
            for e in range(8):
                step(ITERS - 1, e, False, end=True)
            for t in range(NT):
                sp.wait_ge(S["y_out"], t + 1)
                sp.dma_start(a["y"][t], x2[:, t, :]).then_inc(S["late_in"], 16)
            sp.wait_ge(S["late_in"], 16 * NT)

        @block.gpsimd
        def _(pool):
            steps = Steps(pool, S["pool_step"])
            steps.add(pool.memset(s["ident"][:, :], 0.0))
            pool.iota(s["iota"][:, :], [[1, P]], base=0, channel_multiplier=0,
                      allow_small_or_imprecise_dtypes=True).then_inc(S["pool_const"], 1)
            steps.settle()
            pool.affine_select(out=s["ident"][:, :], in_=s["ident"][:, :], compare_op=ALU.not_equal, fill=1.0,
                               base=0, pattern=[[-1, P]], channel_multiplier=1).then_inc(S["pool_const"], 1)
            for dst, src in ((s["g1"], a["g1"]), (s["g2"], a["g2"]), (s["winmask"], a["winmask"])):
                pool.dma_start(dst[:, :], src).then_inc(S["const_in"], 16)
            pool.dma_start(s["dec_f"][:, :], a["dec_f"].partition_broadcast(P)).then_inc(S["const_in"], 16)
            pool.dma_start(s["dec_b"][:, :], a["dec_b"].partition_broadcast(P)).then_inc(S["const_in"], 16)
            pool.wait_ge(S["const_in"], 80)
            for h in range(NA_HEADS):
                if h >= 2:
                    pool.wait_ge(S["na_max"], NT * (h - 1))
                pool.dma_start(band[:, h % 2], a["band"][h].rearrange("p (r c) -> p r c", c=GRID_W)
                               ).then_inc(band_in[h % 2], 16)
                pool.wait_ge(band_in[h % 2], 16 * (h // 2 + 1))
                pool.tensor_tensor(band[:, h % 2], band[:, h % 2],
                                   s["winmask"][:, None, :].broadcast_to([P, BAND_ROWS, GRID_W]),
                                   ALU.add).then_inc(S["band_ready"], 1)
            pool.wait_ge(S["na_out"], UNITS)
            for dst, src in ((cos, a["cos"]), (sin, a["sin"]), (diff, a["diff"]), (perm, a["perm"])):
                pool.dma_start(dst[:, :], src).then_inc(S["mid_in"], 16)
            pool.dma_start(ngain[:, :], a["ret_norm"].partition_broadcast(P)).then_inc(S["mid_in"], 16)
            pool.wait_ge(S["mid_in"], 80)
            pool.wait_ge(S["t_evac"], 32)
            for r in range(16):
                if r >= 2:
                    pool.wait_ge(S["rot_done"], r - 1)
                pool.tensor_tensor(rot_cos[:, r % 2], ret_qk[:, r // 2, half_cols(r % 2)],
                                   cos[:, half_cols(r % 2)], ALU.mult).then_inc(S["rot_c"], 1)
            for t in range(NT):
                pool.wait_ge(S["gate_silu"], t + 1)
                pool.tensor_tensor(ret_gate[:, t], ret_gate[:, t], ngain[:, :], ALU.mult
                                   ).then_inc(S["gate_ready"], 1)
            pool.wait_ge(S["src_ready"], 3 * NT)
            pool.wait_ge(S["tr_done"], 3 * NT)
            pool.dma_start(keys_t[:, :, :], a["keys"]).then_inc(S["keys_in"], 16)

            def sums(t):
                pool.wait_ge(S["tk_first"], 4 * (t + 1))
                if t:
                    pool.wait_ge(S["tk_second"], t)
                v = tv[:, t % 2].rearrange("p (h two) k -> p h two k", two=2)
                pool.tensor_tensor(cand[:, :, :].rearrange("p h (x y) -> p h x y", x=TOPK),
                                   v[:, :, 0, :, None].broadcast_to([P, PEER_HEADS, TOPK, TOPK]),
                                   v[:, :, 1, None, :].broadcast_to([P, PEER_HEADS, TOPK, TOPK]),
                                   ALU.add).then_inc(S["cand_ready"], 1)

            def decode(t):
                pool.wait_ge(S["tk_pos"], t + 1)
                keys = tif[:, t % 2].rearrange("p (h two) k -> p h two k", two=2)
                for k, one in enumerate((one1, one2)):
                    o4 = one[:, :, :].rearrange("p (h k) j -> p h k j", h=PEER_HEADS)
                    pool.tensor_tensor(o4, o4, keys[:, :, k, None, :].broadcast_to([P, PEER_HEADS, TOPK, TOPK]),
                                       ALU.mult).then_inc(S["one_ready"], 1)

            def hold(ready, n):
                pool.wait_ge(ready, n)
                pool.sem_inc(S["pool_pass"], 1)

            def early(k0, k1):
                with pool.Fori(k0 // 2, k1 // 2) as i:
                    for par in range(2):
                        hold(S["u_hi"], i * 2 + (par + 1))
                        pool.tensor_tensor(sp_lo[:, par], raw[:, par], sp_hi[:, par].bitcast(F32), ALU.subtract
                                           ).then_inc(S["u_lo"], 1)

            early(0, 2)
            sums(0)
            row = 2
            for t, rows in enumerate(PERIODS):
                early(row, row + 4)
                if t + 1 < NT:
                    sums(t + 1)
                if rows > 4:
                    early(row + 4, row + rows)
                row += rows
                decode(t)
            pool.wait_ge(S["idx_ready"], NT)
            with pool.Fori(0, TOK // (4 * HOT)) as i:
                for k in range(HOT):
                    hold(S["hot_ready"], i * HOT + (k + 1))
                    pool.tensor_tensor(hot_a[:, k], hot_a[:, k],
                                       idx_t[:, 2, bass.ds(i * (4 * HOT) + 4 * k, 4), None].broadcast_to([P, 4, P]),
                                       ALU.mult).then_inc(S["hot_gated"], 1)
            for k in range(2):
                pool.wait_ge(g_out[k], 16 * (NT // 2))

            def lo(which, row, par, slot):
                hold(S[which + "_hi"], row + 1)
                pool.tensor_tensor(m_lo[:, slot], raw[:, par if which == "u" else 2 + par],
                                   m_hi[:, slot].bitcast(F32), ALU.subtract).then_inc(S[which + "_lo"], 1)

            for r in range(2):
                lo("v", r, r, 4 + r)
            for r in range(2):
                lo("u", EARLY + r, r, r)
            pool.dma_start(fgain[:, :], a["fgain"].partition_broadcast(P)).then_inc(S["fg_in"], 16)

            def rows_lo(i, pair, early):
                for r in range(2):
                    row, slot = i * 4 + (2 * pair + 2 + r), 2 * (1 - pair) + r
                    if not early:
                        lo("u", row, r, slot)
                    lo("v", row, r, 4 + slot)

            with pool.Fori(0, EARLY_ITERS) as i:
                for pair in range(2):
                    rows_lo(i, pair, True)
            with pool.Fori(EARLY_ITERS, ITERS - 1) as i:
                for pair in range(2):
                    rows_lo(i, pair, False)
            rows_lo(ITERS - 1, 0, False)

        @block.scalar
        def _(act):
            def hi(c):
                act.wait_ge(raw_in[c % RING], 16 * (c // RING + 1))
                if c >= RING:
                    act.wait_ge(*used(c - RING))
                act.activation(sp_hi[:, c % RING], raw[:, c % RING], ACT.Copy).then_inc(S["hi_ready"], 1)

            def squares(n, ready):
                src, scratch = (mix, junk) if n == 0 else (x2, junk) if n == 1 else (x2, junk2)
                for t in range(NT):
                    act.wait_ge(*ready(t))
                    if n + t:
                        act.wait_ge(S["ss_done"], NT * n + t)
                    act.activation(scratch[:, :], src[:, t, :], ACT.Square,
                                   accum_out=s["ssq"][:, NT * n + t:NT * n + t + 1]).then_inc(S["ss_done"], 1)
                act.wait_ge(S["ms_ready"], n + 1)
                act.activation(s["rms"][:, NT * n:NT * n + NT], s["ms"][:, NT * n:NT * n + NT],
                               ACT.Sqrt).then_inc(S["rms_ready"], 1)

            def turned_hi(n, gain):
                for t in range(NT):
                    tt = n * NT + t
                    act.wait_ge(S["tr_done"], tt + 1)
                    if n == 1:
                        act.wait_ge(*used(C_OUT - 1))
                    if n == 2:
                        act.wait_ge(*used(C_WQ - 1))
                    bank = 2 + 2 * (tt % 2)
                    for k in range(KD):
                        src = ps[:, bank + k // 4, (k % 4) * P:(k % 4 + 1) * P]
                        dst = ht_hi[:, k, tile_cols(t)]
                        if gain is None:
                            last = act.activation(dst, src, ACT.Copy)
                        else:
                            last = act.activation(dst, src, ACT.Copy, scale=gain[:, k:k + 1])
                    last.then_inc(S["hi_evac"], 1)

            def t_out(c, m, dst):
                n = 2 * t_index(c) + m
                act.wait_ge(S["t_done"], n + 1)
                act.activation(dst[:, half_cols(m)], ps[:, m, 0:HALF], ACT.Copy).then_inc(S["t_evac"], 1)

            for c in range(AHEAD):
                hi(c)
            squares(0, lambda t: (S["x_in"], 16 * NT))
            act.wait_ge(S["const_in"], 80)
            turned_hi(0, s["g1"])
            act.wait_ge(S["lg_arg"], 1)
            act.activation(s["lgt"][:, 8:16], s["lgt"][:, 16:24], ACT.Exp).then_inc(S["lg_exp"], 1)
            for c in range(C_NA_V):
                hi(c + AHEAD)
                for m in range(2):
                    t_out(c, m, na_qk[:, c, :])
            for c in range(C_NA_V, C_RET_QK):
                hi(c + AHEAD)
            for t in range(NT):
                act.wait_ge(S["v_done"], t + 1)
                act.activation(mix[:, t, WIDTH:], ps[:, 2 + t, :], ACT.Copy).then_inc(S["v_evac"], 1)
            for n in range(UNITS + 2):
                if n < UNITS:
                    L = SEQS[seq_of(n % NT)][1] * P
                    act.wait_ge(S["na_max"], n + 1)
                    if n >= 2:
                        act.wait_ge(S["na_turned"], n - 1)
                    act.activation(na_p[:, n % 2, 0:L], na_sc[:, n % 2, 0:L], ACT.Exp, bias=s["nmx"][:, n:n + 1],
                                   accum_out=s["psum_"][:, n:n + 1]).then_inc(S["na_exp"], 1)
                if 1 <= n <= UNITS:
                    u = n - 1
                    L = SEQS[seq_of(u % NT)][1] * P
                    act.wait_ge(S["na_turned"], u + 1)
                    if u >= 2:
                        act.wait_ge(S["na_summed"], u - 1)
                    act.activation(na_pt[:, u % 2, 0:L], ps[:, 4 + u % 2, 0:L], ACT.Copy
                                   ).then_inc(S["na_copied"], 1)
                c = C_RET_QK + n // 6
                if n < UNITS and n % 6 == 1:
                    hi(c + AHEAD)
                if n < UNITS and n % 6 == 3:
                    t_out(c, 0, ret_qk[:, c - C_RET_QK, :])
                if n and n <= UNITS and n % 6 == 0:
                    t_out(c - 1, 1, ret_qk[:, c - 1 - C_RET_QK, :])
            for g in range(2):
                for c in range(C_RET_V + 4 * g, C_RET_G + 4 * g):
                    if c + AHEAD < C_OUT:
                        hi(c + AHEAD)
                for t in range(NT):
                    act.wait_ge(S["v_done"], NT * (g + 1) + t + 1)
                    if g == 0:
                        act.activation(ret_v[:, t], ps[:, 2 + t, :], ACT.Copy).then_inc(S["v_evac"], 1)
                    else:
                        act.activation(ret_gate[:, t], ps[:, 2 + t, :], ACT.Silu).then_inc(S["gate_silu"], 1)
            for r, (h, q) in enumerate(ret_units):
                if q == 0:
                    act.wait_ge(S["decay_arg"], h + 1)
                    act.activation(dmat[:, h % 2], dmat[:, h % 2], ACT.Exp).then_inc(S["decay_ready"], 1)
                t0, n = SEQS[q]
                act.wait_ge(S["ret_stat"], r + 1)
                act.activation(mix[:, t0:t0 + n, WIDTH + h * P:WIDTH + (h + 1) * P],
                               ps[:, 6 + r % 2, 0:n * P].rearrange("p (t e) -> p t e", t=n),
                               ACT.Copy).then_inc(S["ret_copied"], 1)
            act.wait_ge(S["ret_var"], 1)
            act.activation(ret_std[:, :], ret_rs[:, :], ACT.Sqrt).then_inc(S["ret_sd"], 1)
            for c in range(C_OUT, C_OUT + AHEAD):
                hi(c)
            turned_hi(1, None)
            for c in range(C_OUT, C_WQ):
                hi(c + AHEAD)
            squares(1, lambda t: (S["v_evac"], 2 * NT + NT + t + 1))
            turned_hi(2, s["g2"])
            for c in range(C_WQ, C_END):
                if c + AHEAD < C_END:
                    hi(c + AHEAD)
                for m in range(2):
                    t_out(c, m, q_t[:, c - C_WQ, :])
            def early_hi(row, par, n):
                act.wait_ge(u_in[par], n)
                act.activation(sp_hi[:, par], raw[:, par], ACT.Copy).then_inc(S["u_hi"], 1)

            def early(k0, k1, last=False):
                with act.Fori(k0 // 2, k1 // 2 - last) as i:
                    early_pair(i, k0 == 0, False)
                if last:
                    early_pair(k1 // 2 - 1, False, True)

            def early_pair(i, first, last):
                for par in range(2):
                    for m in range(2):
                        act.wait_ge(S["a_done"], i * 4 + (2 * par + m + 1))
                        if not (first and par == 0):
                            act.wait_ge(early_out[m], i * 32 + 16 * par)
                        act.activation(early_g[:, m], ps[:, m, 0:HALF], ACT.Gelu_apprx_tanh
                                       ).then_inc(S["gelu_done"], 1)
                    if not last:
                        early_hi(i * 2 + (par + 2), par, i * 16 + 32)

            for par in range(2):
                early_hi(par, par, 16)
            early(0, 2)
            row = 2
            for t, rows in enumerate(PERIODS):
                if rows > 4:
                    early(row, row + 4)
                else:
                    early(row, row + 4, last=t == NT - 1)
                act.wait_ge(S["tk_diff"], t + 1)
                act.activation(gexp[:, t % 2], gexp[:, t % 2], ACT.Exp).then_inc(S["tk_exp"], 1)
                if rows > 4:
                    early(row + 4, row + rows)
                row += rows
            act.wait_ge(S["x2_out"], 16)

            def gates_out(g, col, slot, k):
                act.wait_ge(S["gate_mm"], g + 1)
                act.activation(stage[:, slot, :, bass.ds(col, 4)],
                               ps[:, k, :].rearrange("p (t i) -> p i t", t=4), ACT.Copy
                               ).then_inc(S["gate_evac"], 1)

            for t in range(NT):
                if t >= 2:
                    act.wait_ge(g_out[t % 2], 16 * (t // 2))
                with act.Fori(0, P // (4 * HOT)) as i:
                    for k in range(HOT):
                        gates_out(i * HOT + (32 * t + k), i * (4 * HOT) + 4 * k, t % 2, k)

            def hi(which, par, n, slot):
                act.wait_ge((u_in if which == "u" else v_in)[par], n)
                act.activation(m_hi[:, slot], raw[:, par if which == "u" else 2 + par], ACT.Copy
                               ).then_inc(S[which + "_hi"], 1)

            def step(i, e, early, end=False):
                r, par = e % 4 // 2, e % 2
                if not early:
                    act.wait_ge(S["a_done"], i * 8 + (e + 1))
                    act.wait_ge(S["w_ready"], i * 8 + (e - 1))
                    act.activation(act_g[:, par], ps[:, 6 + par, 0:HALF], ACT.Gelu_apprx_tanh
                                   ).then_inc(S["gelu_done"], 1)
                act.wait_ge(S["w_ready"], i * 8 + (e + 1))
                if positive(i * 24 + 3 * (e - 1)):
                    act.wait_ge(S["y_done"], i * 24 + 3 * (e - 1))
                act.activation(w_hi[:, par], w_f[:, par], ACT.Copy).then_inc(S["w_hi_ready"], 1)
                if not (end and e >= 4):
                    n, slot = i * 32 + 16 * (e // 4 + 2), 2 * (1 - e // 4) + r
                    if par == 0 and not early:
                        hi("u", r, n, slot)
                    if par == 1:
                        hi("v", r, n, 4 + slot)

            for r in range(2):
                hi("v", r, 16, 4 + r)
            for r in range(2):
                hi("u", r, 16 * (EARLY // 2 + 1), r)
            for e in range(8):
                step(0, e, True)
            with act.Fori(1, EARLY_ITERS) as i:
                for e in range(8):
                    step(i, e, True)
            with act.Fori(EARLY_ITERS, ITERS - 1) as i:
                for e in range(8):
                    step(i, e, False)
            for e in range(8):
                step(ITERS - 1, e, False, end=True)
            squares(2, lambda t: (S["y_added"], 3 * (2 * N_KEYS // 2 - 2) + t + 1))

        @block.tensor
        def _(pe):
            def exact(out, lhs, rhs, start, stop):
                for k, (l, r) in enumerate(((lhs[0], rhs[0]), (lhs[0], rhs[1]), (lhs[1], rhs[0]))):
                    last = pe.matmul(out, l, r, start=start and k == 0, stop=stop and k == 2,
                                     skip_group_check=True)
                return last

            def turn(n, src):
                for t in range(NT):
                    tt = n * NT + t
                    pe.wait_ge(S["src_ready"], tt + 1)
                    if tt >= 2:
                        pe.wait_ge(S["lo_evac"], tt - 1)
                    bank = 2 + 2 * (tt % 2)
                    for k in range(KD):
                        last = pe.transpose(ps[:, bank + k // 4, (k % 4) * P:(k % 4 + 1) * P],
                                            src(t)[:, k * P:(k + 1) * P], s["ident"][:, :])
                    last.then_inc(S["tr_done"], 1)

            def t_part(c, m, part):
                n = 2 * t_index(c) + m
                sl = c % RING
                if part == 0:
                    pe.wait_ge(S["lo_ready"], c + 1)
                    if n >= 2:
                        pe.wait_ge(S["t_evac"], n - 1)
                for e in range(8 * part, 8 * part + 8):
                    k, which = e // 3, e % 3
                    w = (sp_hi, sp_hi, sp_lo)[which][:, sl, k * P:(k + 1) * P]
                    x = (ht_hi, ht_lo, ht_hi)[which][:, k, half_cols(m)]
                    last = pe.matmul(ps[:, m, 0:HALF], w, x, start=e == 0, stop=e == 23, skip_group_check=True)
                if part == 2:
                    last.then_inc(S["t_done"], 1)

            def v_chunk(c):
                g, cc, sl = v_group(c), c % 4, c % RING
                pe.wait_ge(S["lo_ready"], c + 1)
                for t in range(NT):
                    for kk in range(2):
                        k, cols = 2 * cc + kk, slice(kk * 512, kk * 512 + 512)
                        last = exact(ps[:, 2 + t, :], (ht_hi[:, k, tile_cols(t)], ht_lo[:, k, tile_cols(t)]),
                                     (sp_hi[:, sl, cols], sp_lo[:, sl, cols]), k == 0, k == KD - 1)
                    if cc == 3:
                        last.then_inc(S["v_done"], 1)
                if cc < 3:
                    last.then_inc(S["v_used"], 1)

            pe.wait_ge(S["pool_const"], 2)
            turn(0, lambda t: h_tile[:, t % 2])
            pe.wait_ge(S["lo_evac"], NT)
            for c in range(C_NA_V):
                for m in range(2):
                    for part in range(3):
                        t_part(c, m, part)
            for c in range(C_NA_V, C_RET_QK):
                v_chunk(c)
            pe.wait_ge(S["t_evac"], 2 * C_NA_V)
            pe.wait_ge(S["v_evac"], NT)
            for n in range(UNITS + 2):
                if n < UNITS:
                    h, t = n // NT, n % NT
                    t0, nt = SEQS[seq_of(t)]
                    part = slice(64 * (h % 2), 64 * (h % 2) + 64)
                    if n >= 2:
                        pe.wait_ge(S["na_max"], n - 1)
                    pe.matmul(ps[:, 2 + n % 2, 0:nt * P], na_qk[part, h // 2, tile_cols(t)],
                              na_qk[part, 4 + h // 2, t0 * P:(t0 + nt) * P], start=True, stop=True
                              ).then_inc(S["na_scored"], 1)
                if 1 <= n <= UNITS:
                    u = n - 1
                    nt = SEQS[seq_of(u % NT)][1]
                    pe.wait_ge(S["na_exp"], u + 1)
                    if u >= 2:
                        pe.wait_ge(S["na_copied"], u - 1)
                    for k in range(nt):
                        last = pe.transpose(ps[:, 4 + u % 2, tile_cols(k)], na_p[:, u % 2, tile_cols(k)],
                                            s["ident"][:, :])
                    last.then_inc(S["na_turned"], 1)
                if n >= 2:
                    u = n - 2
                    h, t = u // NT, u % NT
                    t0, nt = SEQS[seq_of(t)]
                    pe.wait_ge(S["na_copied"], u + 1)
                    if u >= 2:
                        pe.wait_ge(S["na_out"], u - 1)
                    for k in range(nt):
                        last = pe.matmul(ps[:, 6 + u % 2, 0:NA_DIM], na_pt[:, u % 2, tile_cols(k)],
                                         mix[:, t0 + k, WIDTH + h * NA_DIM:WIDTH + (h + 1) * NA_DIM],
                                         start=k == 0, stop=k == nt - 1)
                    last.then_inc(S["na_summed"], 1)
                if n < UNITS:
                    t_part(C_RET_QK + n // 6, n % 6 // 3, n % 3)
            pe.wait_ge(S["na_out"], UNITS)
            pe.wait_ge(S["mid_in"], 80)
            for c in range(C_RET_V, C_OUT):
                if c == C_RET_G:
                    pe.wait_ge(S["v_evac"], 2 * NT)
                v_chunk(c)
                for r in (2 * (c - C_RET_V), 2 * (c - C_RET_V) + 1):
                    if r == 0:
                        pe.wait_ge(S["t_evac"], 32)
                    if r >= 2:
                        pe.wait_ge(S["rot_s"], r - 1)
                    pe.matmul(ps[:, r % 2, 0:HALF], perm[:, :], ret_qk[:, r // 2, half_cols(r % 2)],
                              start=True, stop=True).then_inc(S["rot_mm"], 1)
            pe.wait_ge(S["rot_done"], 16)
            pe.wait_ge(S["gate_silu"], NT)
            for r, (h, q) in enumerate(ret_units):
                t0, nt = SEQS[q]
                cols = slice(t0 * P, (t0 + nt) * P)
                for k in range(nt):
                    n = att_first[r] + k
                    if n >= 4:
                        pe.wait_ge(S["ret_att"], n - 3)
                    pe.matmul(ps[:, 2 + n % 4, 0:nt * P], ret_qk[:, 4 + h, tile_cols(t0 + k)],
                              ret_qk[:, h, cols], start=True, stop=True).then_inc(S["ret_qk_done"], 1)
                pe.wait_ge(S["ret_att"], att_first[r + 1])
                if r >= 2:
                    pe.wait_ge(S["ret_stat"], r - 1)
                    pe.wait_ge(S["ret_copied"], r - 1)
                for t in range(nt):
                    for k in range(nt):
                        last = pe.matmul(ps[:, 6 + r % 2, tile_cols(t)], att[:, r % 2, k, tile_cols(t)],
                                         ret_v[:, t0 + k, h * P:(h + 1) * P], start=k == 0, stop=k == nt - 1,
                                         skip_group_check=True)
                last.then_inc(S["ret_o"], 1)
            turn(1, lambda t: mix[:, t, :])
            pe.wait_ge(S["lo_evac"], 2 * NT)
            for c in range(C_OUT, C_WQ):
                if c == C_OUT + 4:
                    pe.wait_ge(S["v_evac"], 3 * NT)
                v_chunk(c)
            turn(2, lambda t: h_tile[:, t % 2])
            pe.wait_ge(S["lo_evac"], 3 * NT)
            for c in range(C_WQ, C_END):
                for m in range(2):
                    for part in range(3):
                        t_part(c, m, part)
            def turn_choice(t):
                pe.wait_ge(S["tk_chosen"], t + 1)
                if t:
                    pe.wait_ge(S["idx_ready"], t)
                for k in range(3):
                    last = pe.transpose(ps[:, 6, tile_cols(k)], chosen[:, k, :], s["ident"][:, :])
                last.then_inc(S["idx_turned"], 1)

            def key_scores(t):
                for g in range(4):
                    if t:
                        pe.wait_ge(S["tk_first"], 4 * t + g - 3)
                    for k in range(4):
                        last = pe.matmul(ps[:, 2 + g, tile_cols(k)], q_t[:, 4 * g + k, tile_cols(t)],
                                         keys_t[:, 4 * g + k, :], start=True, stop=True, skip_group_check=True)
                    last.then_inc(S["sc_done"], 1)

            def early(k0, k1):
                with pe.Fori(k0 // 2, k1 // 2) as i:
                    for par in range(2):
                        pe.wait_ge(S["u_lo"], i * 2 + (par + 1))
                        for m in range(2):
                            if not (k0 == 0 and par == 0):
                                pe.wait_ge(S["gelu_done"], i * 4 + (2 * par + m - 1))
                            for k in range(KD):
                                w = slice(k * P, (k + 1) * P)
                                last = exact(ps[:, m, 0:HALF], (sp_hi[:, par, w], sp_lo[:, par, w]),
                                             (ht_hi[:, k, half_cols(m)], ht_lo[:, k, half_cols(m)]),
                                             k == 0, k == KD - 1)
                            last.then_inc(S["a_done"], 1)

            pe.wait_ge(S["t_evac"], 64)
            pe.wait_ge(S["keys_in"], 16)
            key_scores(0)
            early(0, 2)
            row = 2
            for t, rows in enumerate(PERIODS):
                if t + 1 < NT:
                    key_scores(t + 1)
                early(row, row + rows)
                row += rows
                if t:
                    turn_choice(t - 1)
            turn_choice(NT - 1)
            pe.wait_ge(S["idx_ready"], NT)
            pe.wait_ge(S["gelu_done"], 2 * EARLY)

            def gates(g, k, first=False):
                pe.wait_ge(S["hot_gated"], g + 1)
                if not first:
                    pe.wait_ge(S["gate_evac"], g - (HOT - 1))
                for q in range(4):
                    last = pe.matmul(ps[:, k, tile_cols(q)], hot_b[:, k, q, :], hot_a[:, k, q, :],
                                     start=True, stop=True, skip_group_check=True)
                last.then_inc(S["gate_mm"], 1)

            for k in range(HOT):
                gates(k, k, first=True)
            with pe.Fori(1, TOK // (4 * HOT)) as i:
                for k in range(HOT):
                    gates(i * HOT + k, k)

            def scores(i, e):
                par, slot = e % 2, slot_of(e)
                pe.wait_ge(S["u_lo"], row_of(i, e) + 1)
                pe.wait_ge(S["gelu_done"], i * 8 + (e - 1))
                for k in range(KD):
                    w = slice(k * P, (k + 1) * P)
                    last = exact(ps[:, 6 + par, 0:HALF], (m_hi[:, slot, w], m_lo[:, slot, w]),
                                 (ht_hi[:, k, half_cols(half_of(e))], ht_lo[:, k, half_cols(half_of(e))]),
                                 k == 0, k == KD - 1)
                last.then_inc(S["a_done"], 1)

            def add_experts(i, e):
                par, slot = e % 2, 4 + slot_of(e)
                pe.wait_ge(S["v_lo"], row_of(i, e) + 1)
                pe.wait_ge(S["w_lo_ready"], i * 8 + (e + 1))
                for t in range(TPH):
                    w = (w_hi[:, par, tile_cols(t)], w_lo[:, par, tile_cols(t)])
                    if par == 0 and positive(i * 12 + (3 * (e // 2) - 2 + t)):
                        pe.wait_ge(S["y_added"], i * 12 + (3 * (e // 2) - 2 + t))
                    for c in range(2):
                        cols = slice(c * 512, c * 512 + 512)
                        last = exact(ps[:, 2 * t + c, :], w, (m_hi[:, slot, cols], m_lo[:, slot, cols]),
                                     par == 0, par == 1)
                    last.then_inc(S["y_done"], 1)

            pe.wait_ge(S["gate_evac"], 32 * NT)
            scores(EARLY_ITERS, 0)
            for e in range(8):
                add_experts(0, e)
            with pe.Fori(1, EARLY_ITERS) as i:
                for e in range(8):
                    add_experts(i, e)
            with pe.Fori(EARLY_ITERS, ITERS - 1) as i:
                for e in range(8):
                    scores(i, e + 1)
                    add_experts(i, e)
            for e in range(8):
                if e < 7:
                    scores(ITERS - 1, e + 1)
                add_experts(ITERS - 1, e)

        @block.vector
        def _(dve):
            steps = Steps(dve, S["dve_step"])

            def lo(c):
                dve.wait_ge(S["hi_ready"], c + 1)
                dve.tensor_tensor(sp_lo[:, c % RING], raw[:, c % RING], sp_hi[:, c % RING].bitcast(F32),
                                  ALU.subtract).then_inc(S["lo_ready"], 1)

            def rstd(n):
                cols = slice(NT * n, NT * n + NT)
                dve.wait_ge(S["ss_done"], NT * (n + 1))
                dve.tensor_scalar(s["ms"][:, cols], s["ssq"][:, cols], 1.0 / D_MODEL, EPS, ALU.mult, ALU.add
                                  ).then_inc(S["ms_ready"], 1)
                dve.wait_ge(S["rms_ready"], n + 1)
                steps.add(dve.reciprocal(s["rstd"][:, cols], s["rms"][:, cols]))
                steps.settle()

            def normed(n, t):
                src, col = (mix, t) if n == 0 else (x2, NT + t)
                tt = n * NT + t
                if t >= 2:
                    dve.wait_ge(S["tr_done"], tt - 1)
                dve.tensor_scalar(h_tile[:, t % 2], src[:, t, :], s["rstd"][:, col:col + 1], None, ALU.mult
                                  ).then_inc(S["src_ready"], 1)

            def turned_lo(n, t, gain):
                tt = n * NT + t
                dve.wait_ge(S["hi_evac"], tt + 1)
                bank = 2 + 2 * (tt % 2)
                for k in range(KD):
                    src = ps[:, bank + k // 4, (k % 4) * P:(k % 4 + 1) * P]
                    hi_part = ht_hi[:, k, tile_cols(t)].bitcast(F32)
                    dst = ht_lo[:, k, tile_cols(t)]
                    if gain is None:
                        last = dve.tensor_tensor(dst, src, hi_part, ALU.subtract)
                    else:
                        last = dve.scalar_tensor_tensor(dst, src, gain[:, k:k + 1], hi_part, ALU.mult, ALU.subtract)
                last.then_inc(S["lo_evac"], 1)

            def log_decays():
                lg, w = s["lg"], s["lgt"]
                d, y, z, z2, acc = (w[:, 8 * k:8 * k + 8] for k in range(5))
                dve.wait_ge(S["const_in"], 80)
                for k, src in enumerate((s["dec_f"], s["dec_b"])):
                    steps.add(dve.tensor_copy(d[:, 4 * k:4 * k + 4], src[:, :]))
                steps.settle()
                dve.tensor_scalar(y, d, -1.0, None, ALU.mult).then_inc(S["dve_step"], 1)
                steps.n += 1
                steps.settle()
                steps.add(dve.tensor_tensor(y, y, d, ALU.min))
                steps.settle()
                dve.tensor_copy(z, y).then_inc(S["lg_arg"], 1)
                dve.wait_ge(S["lg_exp"], 1)
                steps.add(dve.tensor_scalar(z2, y, 2.0, None, ALU.add))
                steps.settle()
                steps.add(dve.reciprocal(z, z2))
                steps.settle()
                steps.add(dve.tensor_tensor(z, z, y, ALU.mult))
                steps.settle()
                steps.add(dve.tensor_tensor(z2, z, z, ALU.mult))
                steps.add(dve.memset(acc, 2.0 / 19))
                steps.settle()
                for odd in range(17, 0, -2):
                    steps.add(dve.tensor_tensor(acc, acc, z2, ALU.mult))
                    steps.settle()
                    steps.add(dve.tensor_scalar(acc, acc, 2.0 / odd, None, ALU.add))
                    steps.settle()
                steps.add(dve.tensor_tensor(acc, acc, z, ALU.mult))
                steps.add(dve.tensor_scalar(y, d, 0.0, None, ALU.min))
                steps.settle()
                steps.add(dve.tensor_tensor(lg[:, :], y, acc, ALU.subtract))
                steps.settle()
                steps.add(dve.tensor_scalar(lg[:, 4:8], lg[:, 4:8], -1.0, None, ALU.mult))

            for c in range(AHEAD):
                lo(c)
            rstd(0)
            dve.wait_ge(S["const_in"], 80)
            for t in range(NT):
                normed(0, t)
                if t:
                    turned_lo(0, t - 1, s["g1"])
            turned_lo(0, NT - 1, s["g1"])
            log_decays()
            for c in range(C_NA_V):
                lo(c + AHEAD)
            for c in range(C_NA_V, C_RET_QK):
                lo(c + AHEAD)
            for n in range(UNITS + 2):
                if n < UNITS:
                    h, t = n // NT, n % NT
                    q = seq_of(t)
                    L = SEQS[q][1] * P
                    row = (6 - 2 * (t - SEQS[q][0]))
                    dve.wait_ge(S["na_scored"], n + 1)
                    dve.wait_ge(S["band_ready"], h + 1)
                    if n >= 2:
                        dve.wait_ge(S["na_exp"], n - 1)
                    sc = na_sc[:, n % 2, 0:L]
                    steps.add(dve.scalar_tensor_tensor(
                        sc, ps[:, 2 + n % 2, 0:L], NA_DIM ** -0.5,
                        band[:, h % 2, row:row + L // GRID_W, :].rearrange("p r c -> p (r c)"),
                        ALU.mult, ALU.add))
                    steps.settle()
                    steps.add(dve.reduce_max(s["mx"][:, n:n + 1], sc, AX.X))
                    steps.settle()
                    dve.tensor_scalar(s["nmx"][:, n:n + 1], s["mx"][:, n:n + 1], -1.0, None, ALU.mult
                                      ).then_inc(S["na_max"], 1)
                if n >= 2:
                    u = n - 2
                    h, t = u // NT, u % NT
                    dve.wait_ge(S["na_exp"], u + 1)
                    steps.add(dve.reciprocal(s["prec"][:, u:u + 1], s["psum_"][:, u:u + 1]))
                    steps.settle()
                    dve.wait_ge(S["na_summed"], u + 1)
                    dve.tensor_scalar(mix[:, t, h * NA_DIM:(h + 1) * NA_DIM], ps[:, 6 + u % 2, 0:NA_DIM],
                                      s["prec"][:, u:u + 1], None, ALU.mult).then_inc(S["na_out"], 1)
                if n < UNITS and n % 6 == 1:
                    lo(C_RET_QK + n // 6 + AHEAD)
            dve.wait_ge(S["mid_in"], 80)
            for c in range(C_RET_V, C_OUT):
                if c + AHEAD < C_OUT:
                    lo(c + AHEAD)
                for r in (2 * (c - C_RET_V), 2 * (c - C_RET_V) + 1):
                    dve.wait_ge(S["rot_mm"], r + 1)
                    dve.tensor_tensor(rot_sin[:, r % 2], ps[:, r % 2, 0:HALF], sin[:, half_cols(r % 2)],
                                      ALU.mult).then_inc(S["rot_s"], 1)
                    dve.wait_ge(S["rot_s"], r + 1)
                    dve.wait_ge(S["rot_c"], r + 1)
                    dve.tensor_tensor(ret_qk[:, r // 2, half_cols(r % 2)], rot_cos[:, r % 2], rot_sin[:, r % 2],
                                      ALU.add).then_inc(S["rot_done"], 1)

            def decay_argument(h):
                steps.add(dve.tensor_scalar(back[:, :], diff[:, :], 0.0, s["lg"][:, 4 + h:5 + h], ALU.min, ALU.mult))
                steps.add(dve.tensor_scalar(dmat[:, h % 2], diff[:, :], 0.0, s["lg"][:, h:h + 1], ALU.max, ALU.mult))
                steps.settle()
                dve.tensor_tensor(dmat[:, h % 2], dmat[:, h % 2], back[:, :], ALU.add
                                  ).then_inc(S["decay_arg"], 1)

            dve.wait_ge(S["rot_done"], 16)
            dve.wait_ge(S["na_exp"], UNITS)
            decay_argument(0)
            for r, (h, q) in enumerate(ret_units):
                t0, nt = SEQS[q]
                L = nt * P
                if q == 0 and h + 1 < RET_HEADS:
                    dve.wait_ge(S["decay_arg"], h + 1)
                    decay_argument(h + 1)
                if r >= 2:
                    dve.wait_ge(S["ret_o"], r - 1)
                dve.wait_ge(S["decay_ready"], h + 1)
                for k in range(nt):
                    dve.wait_ge(S["ret_qk_done"], att_first[r] + k + 1)
                    off = 384 - k * P
                    dve.scalar_tensor_tensor(att[:, r % 2, k, 0:L], ps[:, 2 + (att_first[r] + k) % 4, 0:L],
                                             RET_DIM ** -0.5, dmat[:, h % 2, off:off + L], ALU.mult, ALU.mult
                                             ).then_inc(S["ret_att"], 1)
                dve.wait_ge(S["ret_o"], r + 1)
                for t in range(nt):
                    last = dve.bn_stats(stats[:, (t0 + t) * RET_HEADS + h, :], ps[:, 6 + r % 2, tile_cols(t)])
                last.then_inc(S["ret_stat"], 1)
            dve.wait_ge(S["ret_stat"], len(ret_units))
            for k in range(NT * RET_HEADS):
                last = dve.bn_aggr(mv[:, k, :], stats[:, k, :])
            steps.add(last)
            steps.settle()
            dve.tensor_scalar(ret_rs[:, :], mv[:, :, 1], EPS, None, ALU.add).then_inc(S["ret_var"], 1)
            dve.wait_ge(S["ret_sd"], 1)
            steps.add(dve.reciprocal(ret_rs[:, :], ret_std[:, :]))
            steps.settle()
            dve.wait_ge(S["ret_copied"], len(ret_units))
            dve.wait_ge(S["gate_ready"], NT)
            for t in range(NT):
                for h in range(RET_HEADS):
                    o = mix[:, t, WIDTH + h * P:WIDTH + (h + 1) * P]
                    k = t * RET_HEADS + h
                    last = dve.tensor_scalar(o, o, mv[:, k, 0:1], ret_rs[:, k:k + 1], ALU.subtract, ALU.mult)
                steps.add(last)
                steps.settle()
                dve.tensor_tensor(mix[:, t, WIDTH:], mix[:, t, WIDTH:], ret_gate[:, t], ALU.mult
                                  ).then_inc(S["src_ready"], 1)
            for c in range(C_OUT, C_OUT + AHEAD):
                lo(c)
            for t in range(NT):
                turned_lo(1, t, None)
            dve.wait_ge(S["xa_in"], 16 * NT)
            for half in range(2):
                for c in range(C_OUT + 4 * half, C_OUT + 4 * half + 4):
                    lo(c + AHEAD)
                cols = slice(half * 512, half * 512 + 512)
                for t in range(NT):
                    dve.wait_ge(S["v_done"], NT * (3 + half) + t + 1)
                    dve.tensor_tensor(x2[:, t, cols], ps[:, 2 + t, :], x_again[:, t, cols], ALU.add
                                      ).then_inc(S["v_evac"], 1)
            rstd(1)
            for t in range(NT):
                normed(1, t)
                if t:
                    turned_lo(2, t - 1, s["g2"])
            turned_lo(2, NT - 1, s["g2"])
            for c in range(C_WQ, C_END - AHEAD):
                lo(c + AHEAD)

            def best_keys(t):
                sl = t % 2
                for g in range(4):
                    dve.wait_ge(S["sc_done"], 4 * t + g + 1)
                    sc = [ps[:, 2 + g, tile_cols(k)] for k in range(4)]
                    ks = [4 * g + k for k in range(4)]
                    for k in range(4):
                        last = dve.max(tv[:, sl, ks[k], 0:8], sc[k])
                    steps.add(last)
                    steps.settle()
                    for k in range(4):
                        dve.max_index(ti[:, sl, ks[k], 0:8], tv[:, sl, ks[k], 0:8], sc[k])
                        last = dve.match_replace(rep[:, k, :], tv[:, sl, ks[k], 0:8], sc[k], imm_value=-3e38)
                    steps.add(last)
                    steps.settle()
                    for k in range(4):
                        last = dve.max(tv[:, sl, ks[k], 8:16], rep[:, k, :])
                    steps.add(last)
                    steps.settle()
                    for k in range(4):
                        last = dve.max_index(ti[:, sl, ks[k], 8:16], tv[:, sl, ks[k], 8:16], rep[:, k, :])
                    last.then_inc(S["tk_first"], 1)

            def best_pairs(t):
                sl = t % 2
                dve.wait_ge(S["cand_ready"], t + 1)
                hs = range(PEER_HEADS)
                for h in hs:
                    last = dve.max(bv[:, h, 0:8], cand[:, h, :])
                steps.add(last)
                steps.settle()
                for h in hs:
                    last = dve.max_index(bp[:, h, 0:8], bv[:, h, 0:8], cand[:, h, :])
                for h in hs:
                    last = dve.match_replace(cand[:, h, :], bv[:, h, 0:8], cand[:, h, :], imm_value=-3e38)
                steps.add(last)
                steps.settle()
                for h in hs:
                    last = dve.max(bv[:, h, 8:16], cand[:, h, :])
                steps.add(last)
                steps.settle()
                for h in hs:
                    last = dve.max_index(bp[:, h, 8:16], bv[:, h, 8:16], cand[:, h, :])
                last.then_inc(S["tk_second"], 1)
                dve.wait_ge(S["tk_second"], t + 1)
                dve.tensor_tensor(gexp[:, sl], bv[:, :, :], bv[:, :, 0:1].broadcast_to([P, PEER_HEADS, TOPK]),
                                  ALU.subtract).then_inc(S["tk_diff"], 1)
                flat = bp[:, :, :].rearrange("p h k -> p (h k)")
                steps.add(dve.tensor_scalar(pa[:, 0, :], flat, 4, None, ALU.logical_shift_right))
                steps.add(dve.tensor_scalar(pa[:, 1, :], flat, 15, None, ALU.bitwise_and))
                steps.settle()
                dve.tensor_copy(paf[:, sl], pa[:, 0, :])
                dve.tensor_copy(pbf[:, sl], pa[:, 1, :])
                steps.add(dve.tensor_copy(tif[:, sl], ti[:, sl]))

            def hot_ranks(t):
                steps.settle()
                if t:
                    dve.wait_ge(S["tk_chosen"], t)
                for one, pos in ((one1, paf), (one2, pbf)):
                    last = dve.tensor_tensor(one[:, :, :], pos[:, t % 2, :, None].broadcast_to([P, P, TOPK]),
                                             s["iota"][:, None, 0:TOPK].broadcast_to([P, P, TOPK]), ALU.is_equal)
                last.then_inc(S["tk_pos"], 1)

            def choices(t):
                sl = t % 2
                dve.wait_ge(S["tk_exp"], t + 1)
                if t:
                    dve.wait_ge(S["idx_turned"], t)
                steps.add(dve.reduce_sum(gsum[:, :], gexp[:, sl], AX.X))
                steps.settle()
                steps.add(dve.reciprocal(grec[:, :], gsum[:, :]))
                steps.settle()
                dve.tensor_tensor(chosen[:, 2, :].rearrange("p (h k) -> p h k", h=PEER_HEADS), gexp[:, sl],
                                  grec[:, :, None].broadcast_to([P, PEER_HEADS, TOPK]), ALU.mult)
                for k, one in enumerate((one1, one2)):
                    dve.wait_ge(S["one_ready"], 2 * t + k + 1)
                    last = dve.reduce_sum(chosen[:, k, :], one[:, :, :], AX.X)
                last.then_inc(S["tk_chosen"], 1)

            def turned_choice(t):
                dve.wait_ge(S["idx_turned"], t + 1)
                dve.tensor_copy(idx_t[:, :, tile_cols(t)], ps[:, 6, 0:3 * P].rearrange("p (c n) -> p c n", c=3)
                                ).then_inc(S["idx_ready"], 1)

            best_keys(0)
            for t in range(NT):
                if t + 1 < NT:
                    best_keys(t + 1)
                if t >= 2:
                    turned_choice(t - 2)
                best_pairs(t)
                if t:
                    choices(t - 1)
                hot_ranks(t)
            turned_choice(NT - 2)
            choices(NT - 1)
            turned_choice(NT - 1)
            dve.wait_ge(S["idx_ready"], NT)
            for m in range(2):
                dve.wait_ge(early_out[m], 16 * EARLY)

            def hot(g, token, k, first=False):
                if not first:
                    dve.wait_ge(S["gate_mm"], g - (HOT - 1))
                for c, dst in ((1, hot_b), (0, hot_a)):
                    last = dve.tensor_tensor(dst[:, k], s["iota"][:, None, :].broadcast_to([P, 4, P]),
                                             idx_t[:, c, bass.ds(token, 4), None].broadcast_to([P, 4, P]),
                                             ALU.is_equal)
                last.then_inc(S["hot_ready"], 1)

            for k in range(HOT):
                hot(k, 4 * k, k, first=True)
            with dve.Fori(1, TOK // (4 * HOT)) as i:
                for k in range(HOT):
                    hot(i * HOT + k, i * (4 * HOT) + 4 * k, k)

            def add_sums(i, e):
                for t in range(TPH):
                    dve.wait_ge(S["y_done"], i * 24 + (3 * e - 2 + t))
                    for c in range(2):
                        o = x2[:, half_of(e + 7) * TPH + t, c * 512:c * 512 + 512]
                        last = dve.tensor_tensor(o, ps[:, 2 * t + c, :], o, ALU.add)
                    last.then_inc(S["y_added"], 1)

            def step(i, e, early):
                par = e % 2
                if early:
                    dve.wait_ge(act_in[par], i * 64 + 16 * (e // 2 + 1))
                else:
                    dve.wait_ge(S["gelu_done"], i * 8 + (e + 1))
                dve.wait_ge(gate_in[par], i * 64 + 16 * (e // 2 + 1))
                if positive(i * 8 + (e - 1)):
                    dve.wait_ge(S["w_lo_ready"], i * 8 + (e - 1))
                dve.tensor_tensor(w_f[:, par], act_g[:, par], g_in[:, par], ALU.mult).then_inc(S["w_ready"], 1)
                dve.wait_ge(S["w_hi_ready"], i * 8 + (e + 1))
                dve.tensor_tensor(w_lo[:, par], w_f[:, par], w_hi[:, par].bitcast(F32), ALU.subtract
                                  ).then_inc(S["w_lo_ready"], 1)
                if par == 0 and positive(i * 8 + e):
                    add_sums(i, e)

            for k in range(2):
                dve.wait_ge(g_out[k], 16 * (NT // 2))
            dve.wait_ge(S["x2_in"], 16)
            for e in range(8):
                step(0, e, True)
            with dve.Fori(1, EARLY_ITERS) as i:
                for e in range(8):
                    step(i, e, True)
            with dve.Fori(EARLY_ITERS, ITERS - 1) as i:
                for e in range(8):
                    step(i, e, False)
            for e in range(8):
                step(ITERS - 1, e, False)
            add_sums(ITERS - 1, 8)
            rstd(2)
            dve.wait_ge(S["fg_in"], 16)
            for t in range(NT):
                col = 2 * NT + t
                dve.scalar_tensor_tensor(x2[:, t, :], x2[:, t, :], s["rstd"][:, col:col + 1], fgain[:, :],
                                         ALU.mult, ALU.mult).then_inc(S["y_out"], 1)


def shape_constants():
    f = np.float32
    d = RET_DIM
    inv = (f(1.0) / (f(10000.0) ** (np.arange(0, d, 2, dtype=f) / f(d)))).astype(f)
    pos = np.concatenate([np.arange(SEQ), np.arange(DEC_SEQ)]).astype(f)
    ang = (inv[:, None] * pos[None, :]).astype(f)
    cos, sin = np.cos(ang), np.sin(ang)
    perm = np.zeros((P, P), f)
    for i in range(P // 2):
        perm[i + P // 2, i] = -1.0
        perm[i, i + P // 2] = 1.0
    diff = (np.arange(DIFF)[None, :] - 384 - np.arange(P)[:, None]).astype(f)
    start = np.clip(np.arange(GRID_W) - NA_COLS // 2, 0, GRID_W - NA_COLS)
    c = np.arange(GRID_W)
    inside = (c[None, :] >= start[:, None]) & (c[None, :] < start[:, None] + NA_COLS)
    mask = np.where(inside, 0.0, NEG).astype(f)
    return {"cos": np.concatenate([cos, cos]).astype(f), "sin": np.concatenate([sin, sin]).astype(f),
            "perm": perm, "diff": diff, "winmask": np.concatenate([mask, mask])}


def laid_out(x_prompt, x_sample, norm1_g, w_in, na_rpb, ret_decay_fwd, ret_decay_bwd, ret_norm_g, w_out,
             norm2_g, peer_w_q, peer_sub_keys, peer_u, peer_v, final_g):
    x = np.concatenate([x_prompt[0], x_sample[0]]).reshape(NT, P, D_MODEL)

    def stationary(w):
        n = w.shape[1] // P
        return w.reshape(KD, P, n, P).transpose(2, 1, 0, 3).reshape(n, P, 1024)

    def moving(w):
        n = w.shape[1] // 512
        return w.reshape(4, 2, P, n, 512).transpose(3, 0, 2, 1, 4).reshape(4 * n, P, 1024)

    w = w_in[0]
    cut = [w[:, 512 * k:512 * k + 512] for k in range(7)]
    front = np.concatenate([stationary(cut[0]), stationary(cut[1]), moving(cut[2]), stationary(cut[3]),
                            stationary(cut[4]), moving(cut[5]), moving(cut[6]), moving(w_out[0]),
                            stationary(peer_w_q[0])])
    u = peer_u[0].reshape(N_KEYS, N_KEYS, KD, P).transpose(0, 3, 2, 1).reshape(N_KEYS, 1, P, 1024)
    v = peer_v[0].reshape(N_KEYS, 1, P, 1024)
    par = np.arange(2)[:, None, None, None]
    qc = np.arange(GRID_W)[None, :, None, None]
    off = np.arange(BAND_ROWS)[None, None, :, None]
    kc = np.arange(GRID_W)[None, None, None, :]
    col = np.clip(kc - qc + NA_COLS - 1, 0, 2 * NA_COLS - 2)
    band = na_rpb[0][:, off + 1 - par, col].reshape(NA_HEADS, P, BAND_ROWS * GRID_W)
    out = {"x": x, "front": front, "experts": np.concatenate([u, v], axis=1), "band": band,
           "g1": norm1_g[0].reshape(KD, P).T, "g2": norm2_g[0].reshape(KD, P).T,
           "dec_f": ret_decay_fwd[0], "dec_b": ret_decay_bwd[0], "ret_norm": ret_norm_g[0], "fgain": final_g,
           "keys": peer_sub_keys[0].reshape(16, N_KEYS, P).transpose(2, 0, 1)}
    out.update(shape_constants())
    return {k: np.ascontiguousarray(v) for k, v in out.items()}


def kernel(**inputs):
    import concourse.bacc as bacc
    from concourse.bass_utils import run_bass_kernel_spmd

    nc = bacc.Bacc("TRN2", target_bir_lowering=False, num_devices=1)
    arrays, aps = {}, {}
    for name, v in laid_out(**{k: np.asarray(x) for k, x in inputs.items()}).items():
        arrays[f"in_{name}"] = v
        aps[name] = nc.dram_tensor(f"in_{name}", v.shape, mybir.dt.from_np(v.dtype), kind="ExternalInput").ap()
    aps["gates"] = nc.dram_tensor("gates", (N_KEYS, N_KEYS, TOK), F32, kind="Internal").ap()
    aps["early"] = nc.dram_tensor("early", (EARLY, 2, P, HALF), F32, kind="Internal").ap()
    aps["x2_park"] = nc.dram_tensor("x2_park", (P, NT, D_MODEL), F32, kind="Internal").ap()
    aps["y"] = nc.dram_tensor("out_y", (NT, P, D_MODEL), F32, kind="ExternalOutput").ap()
    encoder_program(nc, aps)
    got = run_bass_kernel_spmd(nc, [arrays], core_ids=[0]).results[0]["out_y"]
    y = got.reshape(TOK, D_MODEL)
    return y[:SEQ].reshape(1, SEQ, D_MODEL), y[SEQ:].reshape(1, DEC_SEQ, D_MODEL)
```

```python
import math
from contextlib import ExitStack

import concourse.bass as bass
import numpy as np
from concourse import mybir

F32 = mybir.dt.float32
F32R = mybir.dt.float32r
U32 = mybir.dt.uint32
ALU = mybir.AluOpType
ACT = mybir.ActivationFunctionType
AX = mybir.AxisListType

P = 128
D_MODEL = 1024
SEQ, DEC_SEQ = 256, 512
NT = (SEQ + DEC_SEQ) // P
TOK = NT * P
HALF = TOK // 2
TPH = NT // 2
KD = D_MODEL // P
GRID_W = 64
NA_HEADS, NA_DIM, NA_COLS, NA_ROWS = 8, 64, 16, 8
RET_HEADS, RET_DIM = 4, 128
WIDTH = 512
PEER_HEADS, TOPK, N_KEYS = 8, 16, 128
EPS = 1e-6
SEQS = [(0, SEQ // P), (SEQ // P, DEC_SEQ // P)]

C_NA_QK, C_NA_V, C_RET_QK, C_RET_V, C_RET_G, C_OUT, C_WQ, C_END = 0, 8, 12, 20, 24, 28, 36, 52
RING = 4
AHEAD = 3
BAND_ROWS = 14
DIFF = 896
EARLY_ROWS = [6] * NT + [4]
IN_GATES = 2
EARLY = sum(EARLY_ROWS) + IN_GATES * NT
STORES = 1 + EARLY_ROWS[0]
GATE_STORES = STORES * (NT - 2) + 1 + EARLY_ROWS[NT]
LAST_STORES = 15
HOT = 4
UNITS = NA_HEADS * NT
NEG = -1e30


def seq_of(tile):
    return 0 if tile < SEQS[1][0] else 1


class Steps:

    def __init__(self, eng, sem):
        self.eng, self.sem, self.n = eng, sem, 0

    def add(self, ins):
        ins.then_inc(self.sem, 1)
        self.n += 1

    def settle(self):
        self.eng.wait_ge(self.sem, self.n)


def encoder_program(nc, a):
    KB = 1024
    base0 = -(-nc.sbuf_base // 32) * 32
    ctx = ExitStack()
    with ctx:
        def sb(name, at, shape, dt=F32):
            n = int(np.prod(shape[1:])) * 4
            assert base0 + at + n <= nc.sbuf_usable_end, (name, at, n)
            return nc.alloc_sbuf_tensor_at(name, shape, dt, offset=base0 + at)

        def sem(name):
            return ctx.enter_context(nc.semaphore(name))

        ht_hi = sb("ht_hi", 0, [P, KD, TOK], F32R)
        ht_lo = sb("ht_lo", 24 * KB, [P, KD, TOK], F32R)
        at = 48 * KB
        small = {}
        for name, cols in (("ident", 128), ("iota", 128), ("g1", KD), ("g2", KD), ("dec_f", 4), ("dec_b", 4),
                           ("lg", 8), ("lgt", 40), ("ssq", 3 * NT), ("ms", 3 * NT), ("rms", 3 * NT),
                           ("rstd", 3 * NT), ("mx", UNITS), ("nmx", UNITS), ("psum_", UNITS), ("prec", UNITS),
                           ("winmask", GRID_W)):
            small[name] = sb(name, at, [P, cols])
            at += -(-cols * 4 // 32) * 32
        s = small
        A0 = -(-at // 256) * 256
        assert A0 <= 52 * KB

        mix = sb("mix", A0, [P, NT, D_MODEL])
        x2 = sb("x2", A0, [P, NT, D_MODEL])
        raw = sb("raw", A0 + 24 * KB, [P, RING, 1024])
        sp_hi = sb("sp_hi", A0 + 40 * KB, [P, RING, 1024], F32R)
        sp_lo = sb("sp_lo", A0 + 56 * KB, [P, RING, 1024], F32R)
        R0 = A0 + 72 * KB
        na_qk = sb("na_qk", R0, [P, 8, TOK])
        ret_v = sb("ret_v", R0, [P, NT, WIDTH])
        ret_gate = sb("ret_gate", R0 + 12 * KB, [P, NT, WIDTH])
        ret_qk = sb("ret_qk", R0 + 24 * KB, [P, 8, TOK])
        x_again = sb("x_again", R0 + 24 * KB, [P, NT, D_MODEL])
        W0 = R0 + 48 * KB
        h_tile = sb("h_tile", W0, [P, 2, D_MODEL])
        junk = sb("junk", W0 + 8 * KB, [P, D_MODEL])
        band = sb("band", W0 + 12 * KB, [P, 2, BAND_ROWS, GRID_W])
        na_sc = sb("na_sc", W0 + 19 * KB, [P, 2, 512])
        na_p = sb("na_p", W0 + 23 * KB, [P, 2, 512])
        na_pt = sb("na_pt", W0 + 27 * KB, [P, 2, 512])
        att = sb("att", W0, [P, 2, 4, 512])
        rot_sin = sb("rot_sin", W0, [P, 2, HALF])
        rot_cos = sb("rot_cos", W0 + 4 * KB, [P, 2, HALF])
        dmat = sb("dmat", W0 + 16 * KB, [P, 2, DIFF])
        diff = sb("diff", W0 + 23 * KB, [P, DIFF])
        cos = sb("cos", W0 + 26 * KB + 512, [P, TOK])
        sin = sb("sin", W0 + 29 * KB + 512, [P, TOK])
        back = sb("back", W0 + 26 * KB + 512, [P, DIFF])
        ngain = sb("ngain", W0 + 32 * KB + 512, [P, WIDTH])
        perm = sb("perm", W0 + 34 * KB + 512, [P, P])
        stats = sb("stats", W0 + 35 * KB, [P, NT * RET_HEADS, 6])
        mv = sb("mv", W0 + 35 * KB + 576, [P, NT * RET_HEADS, 2])
        ret_std = sb("ret_std", W0 + 35 * KB + 768, [P, NT * RET_HEADS])
        ret_rs = sb("ret_rs", W0 + 35 * KB + 864, [P, NT * RET_HEADS])

        q_t = sb("q_t", R0, [P, 16, TOK])
        keys_t = sb("keys_t", W0 + 12 * KB, [P, 16, N_KEYS])
        sc_out = sb("sc_out", A0, [P, 3, 16, N_KEYS])
        s_cur = sb("s_cur", W0 + 12 * KB, [P, 16, N_KEYS])
        cand = sb("cand", A0 + 32 * KB, [P, PEER_HEADS, 256])
        one1 = sb("one1", A0, [P, P, TOPK])
        one2 = sb("one2", A0 + 8 * KB, [P, P, TOPK])
        rep = sb("rep", W0, [P, 4, N_KEYS])
        tv = sb("tv", W0 + 2 * KB, [P, 2, 16, TOPK])
        ti = sb("ti", W0 + 4 * KB, [P, 2, 16, TOPK], U32)
        tif = sb("tif", W0 + 6 * KB, [P, 2, 16, TOPK])
        early_lo = sb("early_lo", A0 + 48 * KB, [P, 2, 1024], F32R)
        early_g = sb("early_g", W0 + 8 * KB, [P, 2, HALF])
        T0 = W0 + 20 * KB
        bv = sb("bv", T0, [P, PEER_HEADS, TOPK])
        bp = sb("bp", T0 + 512, [P, PEER_HEADS, TOPK], U32)
        pa = sb("pa", T0 + 1024, [P, 2, P], U32)
        paf = sb("paf", T0 + 2048, [P, P])
        pbf = sb("pbf", T0 + 2560, [P, P])
        gexp = sb("gexp", T0 + 3072, [P, 2, PEER_HEADS, TOPK])
        gsum = sb("gsum", T0 + 4096, [P, PEER_HEADS])
        grec = sb("grec", T0 + 4128, [P, PEER_HEADS])
        chosen = sb("chosen", T0 + 4160, [P, 3, P])
        idx_t = sb("idx_t", T0 + 5888, [P, 3, 2, P])
        stage = sb("stage", A0 + 56 * KB, [P, N_KEYS, P])
        hot_a = sb("hot_a", A0 + 16 * KB, [P, HOT, 4, P])
        hot_b = sb("hot_b", T0 + 8960, [P, HOT, 4, P])
        v_hi = sb("v_hi", A0 + 40 * KB, [P, 4, 1024], F32R)
        u_hi = sb("u_hi", A0 + 56 * KB, [P, 4, 1024], F32R)
        u_lo = sb("u_lo", A0 + 72 * KB, [P, 4, 1024], F32R)
        fgain = sb("fgain", A0 + 88 * KB, [P, D_MODEL])
        junk2 = sb("junk2", A0 + 92 * KB, [P, D_MODEL])
        g_in = sb("g_in", W0, [P, 2, HALF])
        act_g = sb("act_g", W0 + 3 * KB, [P, 2, HALF])
        w_f = sb("w_f", W0 + 6 * KB, [P, 2, HALF])
        w_hi = sb("w_hi", W0 + 9 * KB, [P, 2, HALF], F32R)
        w_lo = sb("w_lo", W0 + 12 * KB, [P, 2, HALF], F32R)
        v_lo = sb("v_lo", W0 + 15 * KB, [P, 4, 1024], F32R)
        split = {"u": (u_hi, u_lo), "v": (v_hi, v_lo)}

        ps = ctx.enter_context(nc.psum_tensor("ps", [P, 8, 512], F32))

        S = {n: sem(n) for n in (
            "pool_const", "const_in", "g1_in", "x_in0", "x_in1", "mid_in", "late_in", "raw_in0", "raw_in1", "raw_in2", "raw_in3",
            "hi_ready", "lo_ready", "v_used", "ss_done", "ms_ready", "rms_ready", "src_ready", "tr_done",
            "hi_evac", "lo_evac", "t_done", "t_evac", "v_done", "v_evac", "band_in0", "band_in1", "band_ready",
            "na_scored", "na_max", "na_exp", "na_turned", "na_copied", "na_summed", "na_out",
            "rot_mm", "rot_c", "rot_s", "rot_done", "decay_arg", "decay_ready", "ret_qk_done", "ret_att",
            "ret_o", "na_tr", "na_hi", "na_lo", "ret_stat", "ret_copied", "ret_var", "ret_sd", "gate_silu", "gate_ready", "xa_in",
            "dve_step", "pool_step", "sc_done", "tk_first", "tk_second", "tk_diff", "tk_exp", "tk_pos",
            "one_ready", "tk_chosen", "idx_turned", "idx_ready", "x2_out", "hot_ready", "hot_gated",
            "gate_mm", "g_out", "g_first", "x2_in0", "x2_in1", "evac", "park0", "park1", "s_in",
            "keys_in", "fg_in", "lg_arg", "pool_pass", "lg_exp",
            "u_in0", "u_in1", "v_in0", "v_in1", "g_in0", "g_in1", "act_in0", "act_in1", "early_out0", "early_out1", "u_hi", "u_lo", "v_hi", "v_lo",
            "a_done", "gelu_done", "w_ready", "w_hi_ready", "w_lo_ready", "y_done", "y_added", "y_out")}
        raw_in = [S[f"raw_in{i}"] for i in range(RING)]
        x_in = [S["x_in0"], S["x_in1"]]
        band_in = [S["band_in0"], S["band_in1"]]
        park, x2_in = [S["park0"], S["park1"]], [S["x2_in0"], S["x2_in1"]]
        u_in, v_in = [S["u_in0"], S["u_in1"]], [S["v_in0"], S["v_in1"]]
        gate_in = [S["g_in0"], S["g_in1"]]
        act_in, early_out = [S["act_in0"], S["act_in1"]], [S["early_out0"], S["early_out1"]]

        def gate_evacs(n):
            return n + 4 * NT

        ITERS, EARLY_ITERS = N_KEYS // 4, EARLY // 4

        def row_of(i, e):
            return i * 4 + (2 * (e // 4) + e % 2)

        def half_of(e):
            return e // 2 % 2

        def slot_of(e):
            return 2 * (e // 4 % 2) + e % 2

        def positive(n):
            return not isinstance(n, int) or n > 0

        def tile_cols(t):
            return slice(t * P, (t + 1) * P)

        def half_cols(m):
            return slice(m * HALF, (m + 1) * HALF)

        def is_token_major(c):
            return C_NA_V <= c < C_RET_QK or C_RET_V <= c < C_WQ

        def t_index(c):
            return c if c < C_NA_V else c - 4 if c < C_RET_V else c - 20

        def t_number(c, m):
            k = t_index(c)
            return 2 * k + m if k not in (0, 1, 16, 17) else 2 * (k - k % 2) + 2 * m + k % 2

        def first_order(c):
            return [(c, 0), (c + 1, 0), (c, 1), (c + 1, 1)]

        def v_group(c):
            return {C_NA_V: 0, C_RET_V: 1, C_RET_G: 2, C_OUT: 3, C_OUT + 4: 4}[c - c % 4]

        def used(c):
            if not is_token_major(c):
                return S["t_done"], t_number(c, 1) + 1
            return (S["v_done"], NT * v_group(c) + NT) if c % 4 == 3 else (S["v_used"], 3 * v_group(c) + c % 4 + 1)

        ret_units = [(h, q) for h in range(RET_HEADS) for q in range(2)]
        att_first = [0]
        for h, q in ret_units:
            att_first.append(att_first[-1] + SEQS[q][1])

        block = ctx.enter_context(nc.Block())

        @block.sync
        def _(sp):
            sp.dma_start(s["g1"][:, :], a["g1"]).then_inc(S["g1_in"], 16)
            for t in range(NT):
                sp.dma_start(mix[:, t, :], a["x"][t]).then_inc(x_in[t // TPH], 16)

            def load_chunk(c):
                if c >= RING:
                    sp.wait_ge(S["lo_ready"], c - RING + 1)
                sp.dma_start(raw[:, c % RING, :], a["front"][c]).then_inc(raw_in[c % RING], 16)

            for c in range(C_OUT + RING):
                load_chunk(c)
            sp.wait_ge(S["ret_o"], len(ret_units))
            for t in range(NT):
                sp.dma_start(x_again[:, t, :], a["x"][t]).then_inc(S["xa_in"], 16)
            for c in range(C_OUT + RING, C_END):
                load_chunk(c)
            sp.wait_ge(S["src_ready"], 3 * NT)
            sp.dma_start(a["x2_park"], x2[:, :, :]).then_inc(S["x2_out"], 16)

            def load_u(row, par):
                sp.dma_start(raw[:, par, :], a["experts"][row, 0]).then_inc(u_in[par], 16)

            def load_v(row, par):
                sp.dma_start(raw[:, 2 + par, :], a["experts"][row, 1]).then_inc(v_in[par], 16)

            for par in range(2):
                sp.wait_ge(S["lo_ready"], C_END - RING + par + 1)
                load_u(par, par)
            for t in range(1, NT):
                sp.wait_ge(S["evac"], 4 * t + 4)
                sp.dma_start(a["scores"][t], sc_out[:, (t - 1) % 2]).then_inc(park[(t - 1) % 2], 16)
            for k in range(2):
                sp.wait_ge(park[k], 16 * ((NT - k) // 2))

            def load_act(i, e, par):
                sp.dma_start(act_g[:, par, :], a["early"][row_of(i, e), half_of(e)]).then_inc(act_in[par], 16)

            def load_x2(m):
                tiles = slice(m * TPH, m * TPH + TPH)
                sp.dma_start(x2[:, tiles, :], a["x2_park"][:, tiles, :]).then_inc(x2_in[m], 16)

            def load_scores(t):
                sp.dma_start(s_cur[:, :, :], a["scores"][t]).then_inc(S["s_in"], 16)

            sp.wait_ge(S["sc_done"], 4 * NT)
            load_scores(1)

            def store_gates(t, first, n, done):
                sp.dma_start(a["gates"][bass.ds(first, n), :, tile_cols(t)].rearrange("i j t -> j i t"),
                             stage[:, bass.ds(first, n)]).then_inc(done, 16)

            PART = N_KEYS // 4
            def early(i, gates_of=None, first=0, n=0):
                for par in range(2):
                    sp.wait_ge(S["u_lo"], i * 2 + (par + 1))
                    load_u(i * 2 + (par + 2), par)
                    if n:
                        store_gates(gates_of, first + par * n, n, S["g_out"])
                    for m in range(2):
                        sp.wait_ge(S["gelu_done"], i * 4 + (2 * par + m + 1))
                        sp.dma_start(a["early"][i * 2 + par, m], early_g[:, m]).then_inc(early_out[m], 16)

            pair = 0
            for t, rows in enumerate(EARLY_ROWS):
                if t >= 2:
                    sp.wait_ge(S["evac"], gate_evacs(32 * (t - 1)))
                    store_gates(t - 2, 0, PART, S["g_out"])
                n = (N_KEYS - PART) // rows if t >= 2 else 0
                with sp.Fori(pair, pair + rows // 2) as i:
                    early(i, t - 2, i * (2 * n) + (PART - pair * 2 * n), n)
                pair += rows // 2
                if 1 <= t and t + 1 < NT:
                    sp.wait_ge(S["tk_first"], 4 * t + 4)
                    load_scores(t + 1)
                if t == NT:
                    sp.wait_ge(S["tk_second"], NT)
                    for par in range(2):
                        load_v(par, par)
                    sp.wait_ge(S["tk_chosen"], NT)
                    load_x2(0)
                    for m in range(2):
                        sp.wait_ge(early_out[m], 16)
                    load_act(0, 0, 0)
                    sp.wait_ge(early_out[0], 32)
                    load_act(0, 1, 1)
                if t:
                    early(pair)
                    pair += 1
            sp.wait_ge(S["evac"], gate_evacs(32 * NT))
            FIRST = 16
            store_gates(NT - 1, 0, FIRST, S["g_first"])
            def load_gates(i, e, par):
                sp.dma_start(g_in[:, par, :], a["gates"][row_of(i, e), :, half_cols(half_of(e))]
                             ).then_inc(gate_in[par], 16)

            sp.wait_ge(S["g_first"], 16)
            sp.wait_ge(S["g_out"], 16 * GATE_STORES)
            for e in range(2):
                load_gates(0, e, e)
            for par in range(2):
                sp.wait_ge(S["v_lo"], par + 1)
                load_v(2 + par, par)
            load_x2(1)

            def step(i, e, early, end=False):
                r, par = e % 4 // 2, e % 2
                row = i * 4 + (2 * (e // 4) + 2 + r)
                if not (end and e >= 6):
                    sp.wait_ge(S["w_ready"], i * 8 + (e + 1))
                    load_gates(i, e + 2, par)
                    if early:
                        load_act(i, e + 2, par)
                if par == 0 and not early and not end:
                    sp.wait_ge(S["u_lo"], row + 1)
                    load_u(row + 2, r)
                if par == 1 and not end:
                    sp.wait_ge(S["v_lo"], row + 1)
                    load_v(row + 2, r)

            for n in range(16):
                step(n // 8, n % 8, True)
                if 1 <= n < LAST_STORES:
                    part = (N_KEYS - FIRST) // (LAST_STORES - 1)
                    store_gates(NT - 1, FIRST + (n - 1) * part, part, S["g_first"])
            sp.wait_ge(S["g_first"], 16 * LAST_STORES)
            for m in range(2):
                sp.wait_ge(early_out[m], 16 * EARLY)
            with sp.Fori(2, 3) as i:
                for e in range(8):
                    step(i, e, True)
            for par in range(2):
                sp.wait_ge(S["u_lo"], EARLY + par + 1)
                load_u(EARLY + 2 + par, par)
            with sp.Fori(3, EARLY_ITERS - 1) as i:
                for e in range(8):
                    step(i, e, True)
            for e in range(8):
                step(EARLY_ITERS - 1, e, early=e < 6)
            with sp.Fori(EARLY_ITERS, ITERS - 1) as i:
                for e in range(8):
                    step(i, e, False)
            for e in range(8):
                step(ITERS - 1, e, False, end=True)
            for t in range(NT):
                sp.wait_ge(S["y_out"], t + 1)
                sp.dma_start(a["y"][t], x2[:, t, :]).then_inc(S["late_in"], 16)
            sp.wait_ge(S["late_in"], 16 * NT)

        @block.gpsimd
        def _(pool):
            steps = Steps(pool, S["pool_step"])
            steps.add(pool.memset(s["ident"][:, :], 0.0))
            pool.iota(s["iota"][:, :], [[1, P]], base=0, channel_multiplier=0,
                      allow_small_or_imprecise_dtypes=True).then_inc(S["pool_const"], 1)
            steps.settle()
            pool.affine_select(out=s["ident"][:, :], in_=s["ident"][:, :], compare_op=ALU.not_equal, fill=1.0,
                               base=0, pattern=[[-1, P]], channel_multiplier=1).then_inc(S["pool_const"], 1)
            for dst, src in ((s["g2"], a["g2"]), (s["winmask"], a["winmask"])):
                pool.dma_start(dst[:, :], src).then_inc(S["const_in"], 16)
            pool.dma_start(s["dec_f"][:, :], a["dec_f"].partition_broadcast(P)).then_inc(S["const_in"], 16)
            pool.dma_start(s["dec_b"][:, :], a["dec_b"].partition_broadcast(P)).then_inc(S["const_in"], 16)
            pool.wait_ge(S["const_in"], 64)
            for h in range(NA_HEADS):
                if h >= 2:
                    pool.wait_ge(S["na_max"], NT * (h - 1))
                pool.dma_start(band[:, h % 2], a["band"][h].rearrange("p (r c) -> p r c", c=GRID_W)
                               ).then_inc(band_in[h % 2], 16)
                pool.wait_ge(band_in[h % 2], 16 * (h // 2 + 1))
                pool.tensor_tensor(band[:, h % 2], band[:, h % 2],
                                   s["winmask"][:, None, :].broadcast_to([P, BAND_ROWS, GRID_W]),
                                   ALU.add).then_inc(S["band_ready"], 1)
            pool.wait_ge(S["na_out"], UNITS)
            for dst, src in ((cos, a["cos"]), (sin, a["sin"]), (diff, a["diff"]), (perm, a["perm"])):
                pool.dma_start(dst[:, :], src).then_inc(S["mid_in"], 16)
            pool.dma_start(ngain[:, :], a["ret_norm"].partition_broadcast(P)).then_inc(S["mid_in"], 16)
            pool.wait_ge(S["mid_in"], 80)
            pool.wait_ge(S["t_evac"], 32)
            for r in range(16):
                if r >= 2:
                    pool.wait_ge(S["rot_done"], r - 1)
                pool.tensor_tensor(rot_cos[:, r % 2], ret_qk[:, r // 2, half_cols(r % 2)],
                                   cos[:, half_cols(r % 2)], ALU.mult).then_inc(S["rot_c"], 1)
            for t in range(NT):
                pool.wait_ge(S["gate_silu"], t + 1)
                pool.tensor_tensor(ret_gate[:, t], ret_gate[:, t], ngain[:, :], ALU.mult
                                   ).then_inc(S["gate_ready"], 1)
            pool.wait_ge(S["src_ready"], 3 * NT)
            pool.wait_ge(S["tr_done"], 3 * NT)
            pool.dma_start(keys_t[:, :, :], a["keys"]).then_inc(S["keys_in"], 16)

            def decode(t):
                pool.wait_ge(S["tk_pos"], t + 1)
                keys = tif[:, t % 2].rearrange("p (h two) k -> p h two k", two=2)
                for k, one in enumerate((one1, one2)):
                    o4 = one[:, :, :].rearrange("p (h k) j -> p h k j", h=PEER_HEADS)
                    pool.tensor_tensor(o4, o4, keys[:, :, k, None, :].broadcast_to([P, PEER_HEADS, TOPK, TOPK]),
                                       ALU.mult).then_inc(S["one_ready"], 1)

            def hold(ready, n):
                pool.wait_ge(ready, n)
                pool.sem_inc(S["pool_pass"], 1)

            def early(i, rows=(0, 1)):
                for par in rows:
                    hold(S["u_hi"], i * 2 + (par + 1))
                    pool.tensor_tensor(early_lo[:, par], raw[:, par], sp_hi[:, par].bitcast(F32), ALU.subtract
                                       ).then_inc(S["u_lo"], 1)

            def lo(which, row, par, slot):
                hold(S[which + "_hi"], row + 1)
                hi_part, lo_part = split[which]
                pool.tensor_tensor(lo_part[:, slot], raw[:, par if which == "u" else 2 + par],
                                   hi_part[:, slot].bitcast(F32), ALU.subtract).then_inc(S[which + "_lo"], 1)

            def gated(t, i0, i1):
                with pool.Fori(i0, i1) as i:
                    for k in range(HOT):
                        hold(S["hot_ready"], i * HOT + (32 * t + k + 1))
                        pool.tensor_tensor(hot_a[:, k], hot_a[:, k],
                                           idx_t[:, 2, t % 2, bass.ds(i * (4 * HOT) + 4 * k, 4), None
                                                 ].broadcast_to([P, 4, P]), ALU.mult).then_inc(S["hot_gated"], 1)

            early(0)
            pair = 1
            for t, rows in enumerate(EARLY_ROWS):
                if t:
                    decode(t - 1)
                early(pair)
                if t < NT:
                    with pool.Fori(pair + 1, pair + rows // 2 - (t > 0)) as i:
                        early(i)
                pair += rows // 2
                if t:
                    early(pair - 1, [0])
                    gated(t - 1, 0, 1)
                    early(pair - 1, [1])
                    gated(t - 1, 1, 6)
                    if t < NT:
                        early(pair, [0])
                    gated(t - 1, 6, 8)
                    if t < NT:
                        early(pair, [1])
                        pair += 1
            for r in range(2):
                lo("v", r, r, r)
            pool.wait_ge(S["gate_mm"], 32 * NT)

            def rows_lo(i, pair, early):
                for r in range(2):
                    row, slot = i * 4 + (2 * pair + 2 + r), 2 * (1 - pair) + r
                    if not early:
                        lo("u", row, r, slot)
                    lo("v", row, r, slot)

            for pair in range(4):
                rows_lo(pair // 2, pair % 2, True)
            pool.wait_ge(S["g_first"], 16 * LAST_STORES)
            for r in range(2):
                lo("u", EARLY + r, r, r)
            pool.dma_start(fgain[:, :], a["fgain"].partition_broadcast(P)).then_inc(S["fg_in"], 16)

            with pool.Fori(2, EARLY_ITERS) as i:
                for pair in range(2):
                    rows_lo(i, pair, True)
            with pool.Fori(EARLY_ITERS, ITERS - 1) as i:
                for pair in range(2):
                    rows_lo(i, pair, False)
            rows_lo(ITERS - 1, 0, False)

        @block.scalar
        def _(act):
            def hi(c):
                act.wait_ge(raw_in[c % RING], 16 * (c // RING + 1))
                if c >= RING:
                    act.wait_ge(*used(c - RING))
                act.activation(sp_hi[:, c % RING], raw[:, c % RING], ACT.Copy).then_inc(S["hi_ready"], 1)

            def squares(n, m, ready):
                src, scratch = (mix, junk) if n == 0 else (x2, junk) if n == 1 else (x2, junk2)
                for t in range(m * TPH, m * TPH + TPH):
                    act.wait_ge(*ready(t))
                    if n + t:
                        act.wait_ge(S["ss_done"], NT * n + t)
                    act.activation(scratch[:, :], src[:, t, :], ACT.Square,
                                   accum_out=s["ssq"][:, NT * n + t:NT * n + t + 1]).then_inc(S["ss_done"], 1)

            def roots(n, m):
                act.wait_ge(S["ms_ready"], 2 * n + m + 1)
                cols = slice(NT * n + m * TPH, NT * n + m * TPH + TPH)
                act.activation(s["rms"][:, cols], s["ms"][:, cols], ACT.Sqrt).then_inc(S["rms_ready"], 1)

            def turned_hi(n, t, gain):
                tt = n * NT + t
                act.wait_ge(S["tr_done"], tt + 1)
                if n == 2:
                    act.wait_ge(*used(C_WQ - 1))
                for k in range(KD):
                    src = ps[:, 2 + 2 * (tt % 2) + k // 4, tile_cols(k % 4)]
                    last = act.activation(ht_hi[:, k, tile_cols(t)], src, ACT.Copy, scale=gain[:, k:k + 1])
                last.then_inc(S["hi_evac"], 1)

            def heads_hi(t, k0, ready, n, done):
                act.wait_ge(ready, n)
                last = act.activation(ht_hi[:, k0:k0 + 4, tile_cols(t)],
                                      ps[:, t % 2, :].rearrange("p (k n) -> p k n", k=4), ACT.Copy)
                last.then_inc(done, 1)

            def t_out(c, m, dst):
                n = t_number(c, m)
                act.wait_ge(S["t_done"], n + 1)
                act.activation(dst[:, half_cols(m)], ps[:, n % 2, 0:HALF], ACT.Copy).then_inc(S["t_evac"], 1)

            def norm(n, gain, ready):
                squares(n, 0, ready)
                roots(n, 0)
                squares(n, 1, ready)
                if n == 0:
                    act.wait_ge(S["g1_in"], 16)
                for t in range(NT):
                    turned_hi(2 * n, t, gain)
                    if t == 0:
                        roots(n, 1)
                    if n == 0 and t >= NT - AHEAD:
                        hi(t - (NT - AHEAD))

            norm(0, s["g1"], lambda t: (x_in[t // TPH], 16 * TPH))
            act.wait_ge(S["lg_arg"], 1)
            act.activation(s["lgt"][:, 8:16], s["lgt"][:, 16:24], ACT.Exp).then_inc(S["lg_exp"], 1)
            for c, m in first_order(C_NA_QK) + [(c, m) for c in range(2, C_NA_V) for m in range(2)]:
                if (c, m) in ((0, 0), (1, 1)) or m == 0 and c >= 2:
                    hi(c + AHEAD)
                t_out(c, m, na_qk[:, c, :])
            for c in range(C_NA_V, C_RET_QK):
                hi(c + AHEAD)
            for t in range(NT):
                act.wait_ge(S["v_done"], t + 1)
                act.activation(mix[:, t, WIDTH:], ps[:, 2 + t, :], ACT.Copy).then_inc(S["v_evac"], 1)
            for n in range(UNITS + 2):
                if n < UNITS:
                    L = SEQS[seq_of(n % NT)][1] * P
                    act.wait_ge(S["na_max"], n + 1)
                    if n >= 2:
                        act.wait_ge(S["na_turned"], n - 1)
                    act.activation(na_p[:, n % 2, 0:L], na_sc[:, n % 2, 0:L], ACT.Exp, bias=s["nmx"][:, n:n + 1],
                                   accum_out=s["psum_"][:, n:n + 1]).then_inc(S["na_exp"], 1)
                if 1 <= n <= UNITS:
                    u = n - 1
                    L = SEQS[seq_of(u % NT)][1] * P
                    act.wait_ge(S["na_turned"], u + 1)
                    if u >= 2:
                        act.wait_ge(S["na_summed"], u - 1)
                    act.activation(na_pt[:, u % 2, 0:L], ps[:, 4 + u % 2, 0:L], ACT.Copy
                                   ).then_inc(S["na_copied"], 1)
                c = C_RET_QK + n // 6
                if n < UNITS and n % 6 == 1:
                    hi(c + AHEAD)
                if n < UNITS and n % 6 == 3:
                    t_out(c, 0, ret_qk[:, c - C_RET_QK, :])
                if n and n <= UNITS and n % 6 == 0:
                    t_out(c - 1, 1, ret_qk[:, c - 1 - C_RET_QK, :])
            for g in range(2):
                for c in range(C_RET_V + 4 * g, C_RET_G + 4 * g):
                    if c + AHEAD < C_OUT:
                        hi(c + AHEAD)
                for t in range(NT):
                    act.wait_ge(S["v_done"], NT * (g + 1) + t + 1)
                    if g == 0:
                        act.activation(ret_v[:, t], ps[:, 2 + t, :], ACT.Copy).then_inc(S["v_evac"], 1)
                    else:
                        act.activation(ret_gate[:, t], ps[:, 2 + t, :], ACT.Silu).then_inc(S["gate_silu"], 1)
            for c in range(C_OUT, C_OUT + AHEAD):
                hi(c)
            def decay(h):
                act.wait_ge(S["decay_arg"], h + 1)
                act.activation(dmat[:, h % 2], dmat[:, h % 2], ACT.Exp).then_inc(S["decay_ready"], 1)

            decay(0)
            for r, (h, q) in enumerate(ret_units):
                if q == 0 and h + 1 < RET_HEADS:
                    decay(h + 1)
                if r < NT:
                    heads_hi(r, 0, S["na_tr"], r + 1, S["na_hi"])
                t0, n = SEQS[q]
                act.wait_ge(S["ret_stat"], r + 1)
                act.activation(mix[:, t0:t0 + n, WIDTH + h * P:WIDTH + (h + 1) * P],
                               ps[:, 6 + r % 2, 0:n * P].rearrange("p (t e) -> p t e", t=n),
                               ACT.Copy).then_inc(S["ret_copied"], 1)
            act.wait_ge(S["ret_var"], 1)
            act.activation(ret_std[:, :], ret_rs[:, :], ACT.Sqrt).then_inc(S["ret_sd"], 1)
            hi(C_OUT + AHEAD)
            for t in range(NT):
                heads_hi(t, 4, S["tr_done"], NT + t + 1, S["hi_evac"])
            for c in range(C_OUT + 1, C_WQ):
                hi(c + AHEAD)
            norm(1, s["g2"], lambda t: (S["v_evac"], 2 * NT + NT + t + 1))
            for c, m in first_order(C_WQ) + [(c, m) for c in range(C_WQ + 2, C_END) for m in range(2)]:
                if ((c, m) in ((C_WQ, 0), (C_WQ + 1, 1)) or m == 0 and c >= C_WQ + 2) and c + AHEAD < C_END:
                    hi(c + AHEAD)
                t_out(c, m, q_t[:, c - C_WQ, :])
            def early_hi(row, par, n):
                act.wait_ge(u_in[par], n)
                act.activation(sp_hi[:, par], raw[:, par], ACT.Copy).then_inc(S["u_hi"], 1)

            def early_gelu(i, par, m):
                act.wait_ge(S["a_done"], i * 4 + (2 * par + m + 1))
                if positive(i * 32 + 16 * par):
                    act.wait_ge(early_out[m], i * 32 + 16 * par)
                act.activation(early_g[:, m], ps[:, m, 0:HALF], ACT.Gelu_apprx_tanh
                               ).then_inc(S["gelu_done"], 1)

            def early_pair(i):
                for par in range(2):
                    for m in range(2):
                        early_gelu(i, par, m)
                    early_hi(i * 2 + (par + 2), par, i * 16 + 32)

            def gates_out(t, i, k):
                act.wait_ge(S["gate_mm"], i * HOT + (32 * t + k + 1))
                act.activation(stage[:, :, bass.ds(i * (4 * HOT) + 4 * k, 4)],
                               ps[:, 2 + k, :].rearrange("p (t i) -> p i t", t=4), ACT.Copy
                               ).then_inc(S["evac"], 1)

            for par in range(2):
                early_hi(par, par, 16)
            act.wait_ge(S["x2_out"], 16)
            for t in range(NT):
                if t >= 3:
                    act.wait_ge(park[(t - 1) % 2], 16 * ((t - 1) // 2))
                for g in range(4):
                    act.wait_ge(S["sc_done"], 4 * t + g + 1)
                    act.activation(sc_out[:, (t - 1) % 2 if t else 2, 4 * g:4 * g + 4, :],
                                   ps[:, 2 + g, :].rearrange("p (k n) -> p k n", k=4), ACT.Copy
                                   ).then_inc(S["evac"], 1)

            def hi(which, par, n, slot):
                act.wait_ge((u_in if which == "u" else v_in)[par], n)
                act.activation(split[which][0][:, slot], raw[:, par if which == "u" else 2 + par], ACT.Copy
                               ).then_inc(S[which + "_hi"], 1)

            early_pair(0)
            pair = 1
            for t, rows in enumerate(EARLY_ROWS):
                end = sum(EARLY_ROWS[:t + 1]) // 2 + max(t - 1, 0)
                with act.Fori(pair, end) as i:
                    early_pair(i)
                pair = end
                if t < NT:
                    act.wait_ge(S["tk_diff"], t + 1)
                    act.activation(gexp[:, t % 2], gexp[:, t % 2], ACT.Exp).then_inc(S["tk_exp"], 1)
                if t >= 2:
                    act.wait_ge(S["g_out"], 16 * (STORES * (t - 1) if t < NT else GATE_STORES))
                if t:
                    for par in range(2):
                        for m in range(2):
                            with act.Fori(4 * par + 2 * m, 4 * par + 2 * m + 2) as i:
                                for k in range(HOT):
                                    gates_out(t - 1, i, k)
                            early_gelu(pair, par, m)
                        if t < NT:
                            early_hi(pair * 2 + par + 2, par, pair * 16 + 32)
                    pair += 1
            for r in range(2):
                hi("v", r, 16, r)

            def step(i, e, early, end=False):
                r, par = e % 4 // 2, e % 2
                if not early:
                    act.wait_ge(S["a_done"], i * 8 + (e + 1))
                    act.wait_ge(S["w_ready"], i * 8 + (e - 1))
                    act.activation(act_g[:, par], ps[:, 6 + par, 0:HALF], ACT.Gelu_apprx_tanh
                                   ).then_inc(S["gelu_done"], 1)
                act.wait_ge(S["w_ready"], i * 8 + (e + 1))
                if positive(i * 24 + 3 * (e - 1)):
                    act.wait_ge(S["y_done"], i * 24 + 3 * (e - 1))
                act.activation(w_hi[:, par], w_f[:, par], ACT.Copy).then_inc(S["w_hi_ready"], 1)
                if not (end and e >= 4):
                    n, slot = i * 32 + 16 * (e // 4 + 2), 2 * (1 - e // 4) + r
                    if par == 0 and not early:
                        hi("u", r, n, slot)
                    if par == 1:
                        hi("v", r, n, slot)

            for n in range(16):
                step(n // 8, n % 8, True)
            act.wait_ge(S["g_first"], 16 * LAST_STORES)
            for r in range(2):
                hi("u", r, 16 * (EARLY // 2 + 1), r)
            with act.Fori(2, EARLY_ITERS) as i:
                for e in range(8):
                    step(i, e, True)
            with act.Fori(EARLY_ITERS, ITERS - 1) as i:
                for e in range(8):
                    step(i, e, False)
            for e in range(8):
                step(ITERS - 1, e, False, end=True)
            for m in range(2):
                squares(2, m, lambda t: (S["y_added"], 3 * (2 * N_KEYS // 2 - 2) + t + 1))
                roots(2, m)

        @block.tensor
        def _(pe):
            def exact(out, lhs, rhs, start, stop):
                for k, (l, r) in enumerate(((lhs[0], rhs[0]), (lhs[0], rhs[1]), (lhs[1], rhs[0]))):
                    last = pe.matmul(out, l, r, start=start and k == 0, stop=stop and k == 2,
                                     skip_group_check=True)
                return last

            def turn(n, t):
                tt = n * NT + t
                pe.wait_ge(S["src_ready"], tt + 1)
                if t >= 2:
                    pe.wait_ge(S["lo_evac"], tt - 1)
                bank = 2 + 2 * (tt % 2)
                for k in range(KD):
                    last = pe.transpose(ps[:, bank + k // 4, tile_cols(k % 4)], h_tile[:, t % 2, tile_cols(k)],
                                        s["ident"][:, :])
                last.then_inc(S["tr_done"], 1)

            def first_chunks(n, c):
                for t in range(NT - 1):
                    turn(n, t)
                t_part(c, 0, 0)
                t_part(c, 0, 1)
                turn(n, NT - 1)
                t_part(c, 0, 2)
                for part in range(3):
                    t_part(c + 1, 0, part)
                pe.wait_ge(S["lo_evac"], NT * n + NT)
                for cc in (c, c + 1):
                    for part in range(3):
                        t_part(cc, 1, part)

            def t_part(c, m, part):
                n = t_number(c, m)
                sl = c % RING
                if part == 0:
                    pe.wait_ge(S["lo_ready"], c + 1)
                    if n >= 2:
                        pe.wait_ge(S["t_evac"], n - 1)
                for e in range(8 * part, 8 * part + 8):
                    k, which = e // 3, e % 3
                    w = (sp_hi, sp_hi, sp_lo)[which][:, sl, k * P:(k + 1) * P]
                    x = (ht_hi, ht_lo, ht_hi)[which][:, k, half_cols(m)]
                    last = pe.matmul(ps[:, n % 2, 0:HALF], w, x, start=e == 0, stop=e == 23, skip_group_check=True)
                if part == 2:
                    last.then_inc(S["t_done"], 1)

            def v_chunk(c):
                g, cc, sl = v_group(c), c % 4, c % RING
                pe.wait_ge(S["lo_ready"], c + 1)
                for t in range(NT):
                    for kk in range(2):
                        k, cols = 2 * cc + kk, slice(kk * 512, kk * 512 + 512)
                        last = exact(ps[:, 2 + t, :], (ht_hi[:, k, tile_cols(t)], ht_lo[:, k, tile_cols(t)]),
                                     (sp_hi[:, sl, cols], sp_lo[:, sl, cols]), k == 0, k == KD - 1)
                    if cc == 3:
                        last.then_inc(S["v_done"], 1)
                if cc < 3:
                    last.then_inc(S["v_used"], 1)

            pe.wait_ge(S["pool_const"], 2)
            first_chunks(0, C_NA_QK)
            for c in range(C_NA_QK + 2, C_NA_V):
                for m in range(2):
                    for part in range(3):
                        t_part(c, m, part)
            for c in range(C_NA_V, C_RET_QK):
                v_chunk(c)
            pe.wait_ge(S["t_evac"], 2 * C_NA_V)
            pe.wait_ge(S["v_evac"], NT)
            for n in range(UNITS + 2):
                if n < UNITS:
                    h, t = n // NT, n % NT
                    t0, nt = SEQS[seq_of(t)]
                    part = slice(64 * (h % 2), 64 * (h % 2) + 64)
                    if n >= 2:
                        pe.wait_ge(S["na_max"], n - 1)
                    pe.matmul(ps[:, 2 + n % 2, 0:nt * P], na_qk[part, h // 2, tile_cols(t)],
                              na_qk[part, 4 + h // 2, t0 * P:(t0 + nt) * P], start=True, stop=True
                              ).then_inc(S["na_scored"], 1)
                if 1 <= n <= UNITS:
                    u = n - 1
                    nt = SEQS[seq_of(u % NT)][1]
                    pe.wait_ge(S["na_exp"], u + 1)
                    if u >= 2:
                        pe.wait_ge(S["na_copied"], u - 1)
                    for k in range(nt):
                        last = pe.transpose(ps[:, 4 + u % 2, tile_cols(k)], na_p[:, u % 2, tile_cols(k)],
                                            s["ident"][:, :])
                    last.then_inc(S["na_turned"], 1)
                if n >= 2:
                    u = n - 2
                    h, t = u // NT, u % NT
                    t0, nt = SEQS[seq_of(t)]
                    pe.wait_ge(S["na_copied"], u + 1)
                    if u >= 2:
                        pe.wait_ge(S["na_out"], u - 1)
                    for k in range(nt):
                        last = pe.matmul(ps[:, 6 + u % 2, 0:NA_DIM], na_pt[:, u % 2, tile_cols(k)],
                                         mix[:, t0 + k, WIDTH + h * NA_DIM:WIDTH + (h + 1) * NA_DIM],
                                         start=k == 0, stop=k == nt - 1)
                    last.then_inc(S["na_summed"], 1)
                if n < UNITS:
                    t_part(C_RET_QK + n // 6, n % 6 // 3, n % 3)
            pe.wait_ge(S["na_out"], UNITS)
            for c in range(C_RET_V, C_OUT):
                if c == C_RET_G:
                    pe.wait_ge(S["v_evac"], 2 * NT)
                v_chunk(c)
                for r in (2 * (c - C_RET_V), 2 * (c - C_RET_V) + 1):
                    if r == 0:
                        pe.wait_ge(S["mid_in"], 80)
                        pe.wait_ge(S["t_evac"], 32)
                    if r >= 2:
                        pe.wait_ge(S["rot_s"], r - 1)
                    pe.matmul(ps[:, r % 2, 0:HALF], perm[:, :], ret_qk[:, r // 2, half_cols(r % 2)],
                              start=True, stop=True).then_inc(S["rot_mm"], 1)
            pe.wait_ge(S["rot_done"], 16)
            pe.wait_ge(S["gate_silu"], NT)
            def ret_scores(r):
                h, q = ret_units[r]
                t0, nt = SEQS[q]
                for k in range(nt):
                    n = att_first[r] + k
                    if n >= 4:
                        pe.wait_ge(S["ret_att"], n - 3)
                    pe.matmul(ps[:, 2 + n % 4, 0:nt * P], ret_qk[:, 4 + h, tile_cols(t0 + k)],
                              ret_qk[:, h, t0 * P:(t0 + nt) * P], start=True, stop=True
                              ).then_inc(S["ret_qk_done"], 1)

            ret_scores(0)
            for r, (h, q) in enumerate(ret_units):
                if r + 1 < len(ret_units):
                    ret_scores(r + 1)
                if r < NT:
                    if r >= 2:
                        pe.wait_ge(S["na_lo"], r - 1)
                    for k in range(4):
                        last = pe.transpose(ps[:, r % 2, tile_cols(k)], mix[:, r, tile_cols(k)],
                                            s["ident"][:, :])
                    last.then_inc(S["na_tr"], 1)
                t0, nt = SEQS[q]
                pe.wait_ge(S["ret_att"], att_first[r + 1])
                if r >= 2:
                    pe.wait_ge(S["ret_stat"], r - 1)
                    pe.wait_ge(S["ret_copied"], r - 1)
                for t in range(nt):
                    for k in range(nt):
                        last = pe.matmul(ps[:, 6 + r % 2, tile_cols(t)], att[:, r % 2, k, tile_cols(t)],
                                         ret_v[:, t0 + k, h * P:(h + 1) * P], start=k == 0, stop=k == nt - 1,
                                         skip_group_check=True)
                last.then_inc(S["ret_o"], 1)
            pe.wait_ge(S["na_lo"], NT)
            pe.wait_ge(S["ret_stat"], len(ret_units))
            pe.wait_ge(S["ret_copied"], len(ret_units))
            v_chunk(C_OUT)
            v_chunk(C_OUT + 1)
            for t in range(NT):
                pe.wait_ge(S["src_ready"], NT + t + 1)
                if t >= 2:
                    pe.wait_ge(S["lo_evac"], NT + t - 1)
                for k in range(4):
                    last = pe.transpose(ps[:, t % 2, tile_cols(k)], mix[:, t, (4 + k) * P:(5 + k) * P],
                                        s["ident"][:, :])
                last.then_inc(S["tr_done"], 1)
            pe.wait_ge(S["lo_evac"], 2 * NT)
            for c in range(C_OUT + 2, C_WQ):
                if c == C_OUT + 4:
                    pe.wait_ge(S["v_evac"], 3 * NT)
                v_chunk(c)
            first_chunks(2, C_WQ)
            for c in range(C_WQ + 2, C_END):
                for m in range(2):
                    for part in range(3):
                        t_part(c, m, part)
            def key_scores(t):
                for g in range(4):
                    if t:
                        pe.wait_ge(S["evac"], 4 * t + g - 3)
                    for k in range(4):
                        last = pe.matmul(ps[:, 2 + g, tile_cols(k)], q_t[:, 4 * g + k, tile_cols(t)],
                                         keys_t[:, 4 * g + k, :], start=True, stop=True, skip_group_check=True)
                    last.then_inc(S["sc_done"], 1)

            def early_part(i, par, m, k0, k1):
                if k0 == 0:
                    pe.wait_ge(S["u_lo"], i * 2 + (par + 1))
                    if positive(i * 4 + (2 * par + m - 1)):
                        pe.wait_ge(S["gelu_done"], i * 4 + (2 * par + m - 1))
                for k in range(k0, k1):
                    w = slice(k * P, (k + 1) * P)
                    last = exact(ps[:, m, 0:HALF], (sp_hi[:, par, w], early_lo[:, par, w]),
                                 (ht_hi[:, k, half_cols(m)], ht_lo[:, k, half_cols(m)]), k == 0, k == KD - 1)
                if k1 == KD:
                    last.then_inc(S["a_done"], 1)

            def early_pair(i):
                for par in range(2):
                    for m in range(2):
                        early_part(i, par, m, 0, KD)

            def gates(t, pair):
                for g in range(32):
                    k = g % HOT
                    pe.wait_ge(S["hot_gated"], t * 32 + (g + 1))
                    pe.wait_ge(S["evac"], t * 32 + gate_evacs(g - 3))
                    for q in range(4):
                        last = pe.matmul(ps[:, 2 + k, tile_cols(q)], hot_b[:, k, q, :], hot_a[:, k, q, :],
                                         start=True, stop=True, skip_group_check=True)
                    last.then_inc(S["gate_mm"], 1)
                    early_part(pair, g // 16, g // 8 % 2, g % 8, g % 8 + 1)

            def turn_choice(t):
                pe.wait_ge(S["tk_chosen"], t + 1)
                for k in range(3):
                    last = pe.transpose(ps[:, 6, tile_cols(k)], chosen[:, k, :], s["ident"][:, :])
                last.then_inc(S["idx_turned"], 1)

            def period(t, pairs):
                pair = t * 4 - 1
                early_pair(pair)
                early_pair(pair + 1)
                turn_choice(t - 1)
                if pairs == 3:
                    early_pair(pair + 2)
                gates(t - 1, pair + pairs)

            pe.wait_ge(S["t_evac"], 64)
            pe.wait_ge(S["keys_in"], 16)
            for t in range(NT):
                key_scores(t)
            early_pair(0)
            with pe.Fori(1, 3) as i:
                early_pair(i)
            with pe.Fori(1, NT) as t:
                period(t, 3)
            period(NT, 2)
            pe.wait_ge(S["gelu_done"], 2 * EARLY)

            def scores(i, e):
                par, slot = e % 2, slot_of(e)
                pe.wait_ge(S["u_lo"], row_of(i, e) + 1)
                pe.wait_ge(S["gelu_done"], i * 8 + (e - 1))
                for k in range(KD):
                    w = slice(k * P, (k + 1) * P)
                    last = exact(ps[:, 6 + par, 0:HALF], (u_hi[:, slot, w], u_lo[:, slot, w]),
                                 (ht_hi[:, k, half_cols(half_of(e))], ht_lo[:, k, half_cols(half_of(e))]),
                                 k == 0, k == KD - 1)
                last.then_inc(S["a_done"], 1)

            def add_experts(i, e):
                par, slot = e % 2, slot_of(e)
                pe.wait_ge(S["v_lo"], row_of(i, e) + 1)
                pe.wait_ge(S["w_lo_ready"], i * 8 + (e + 1))
                for t in range(TPH):
                    w = (w_hi[:, par, tile_cols(t)], w_lo[:, par, tile_cols(t)])
                    if par == 0 and positive(i * 12 + (3 * (e // 2) - 2 + t)):
                        pe.wait_ge(S["y_added"], i * 12 + (3 * (e // 2) - 2 + t))
                    for c in range(2):
                        cols = slice(c * 512, c * 512 + 512)
                        last = exact(ps[:, 2 * t + c, :], w, (v_hi[:, slot, cols], v_lo[:, slot, cols]),
                                     par == 0, par == 1)
                    last.then_inc(S["y_done"], 1)

            pe.wait_ge(S["evac"], gate_evacs(32 * NT))
            for e in range(8):
                add_experts(0, e)
            with pe.Fori(1, EARLY_ITERS) as i:
                for e in range(8):
                    add_experts(i, e)
            scores(EARLY_ITERS, 0)
            with pe.Fori(EARLY_ITERS, ITERS - 1) as i:
                for e in range(8):
                    scores(i, e + 1)
                    add_experts(i, e)
            for e in range(8):
                if e < 7:
                    scores(ITERS - 1, e + 1)
                add_experts(ITERS - 1, e)

        @block.vector
        def _(dve):
            steps = Steps(dve, S["dve_step"])

            def lo(c):
                dve.wait_ge(S["hi_ready"], c + 1)
                dve.tensor_tensor(sp_lo[:, c % RING], raw[:, c % RING], sp_hi[:, c % RING].bitcast(F32),
                                  ALU.subtract).then_inc(S["lo_ready"], 1)

            def means(n, m):
                cols = slice(NT * n + m * TPH, NT * n + m * TPH + TPH)
                dve.wait_ge(S["ss_done"], NT * n + m * TPH + TPH)
                dve.tensor_scalar(s["ms"][:, cols], s["ssq"][:, cols], 1.0 / D_MODEL, EPS, ALU.mult, ALU.add
                                  ).then_inc(S["ms_ready"], 1)

            def rstd(n, m):
                cols = slice(NT * n + m * TPH, NT * n + m * TPH + TPH)
                dve.wait_ge(S["rms_ready"], 2 * n + m + 1)
                steps.add(dve.reciprocal(s["rstd"][:, cols], s["rms"][:, cols]))
                steps.settle()

            def normed(n, t):
                src, col = (mix, t) if n == 0 else (x2, NT + t)
                if t >= 2:
                    dve.wait_ge(S["tr_done"], 2 * n * NT + t - 1)
                dve.tensor_scalar(h_tile[:, t % 2], src[:, t, :], s["rstd"][:, col:col + 1], None, ALU.mult
                                  ).then_inc(S["src_ready"], 1)

            def turned_lo(n, t, gain):
                tt = n * NT + t
                dve.wait_ge(S["hi_evac"], tt + 1)
                bank = 2 + 2 * (tt % 2)
                for k in range(KD):
                    src = ps[:, bank + k // 4, (k % 4) * P:(k % 4 + 1) * P]
                    hi_part = ht_hi[:, k, tile_cols(t)].bitcast(F32)
                    dst = ht_lo[:, k, tile_cols(t)]
                    last = dve.scalar_tensor_tensor(dst, src, gain[:, k:k + 1], hi_part, ALU.mult, ALU.subtract)
                last.then_inc(S["lo_evac"], 1)

            def heads_lo(t, k0, ready, n, done):
                dve.wait_ge(ready, n)
                dve.tensor_tensor(ht_lo[:, k0:k0 + 4, tile_cols(t)],
                                  ps[:, t % 2, :].rearrange("p (k n) -> p k n", k=4),
                                  ht_hi[:, k0:k0 + 4, tile_cols(t)].bitcast(F32), ALU.subtract).then_inc(done, 1)

            def log_decays():
                lg, w = s["lg"], s["lgt"]
                d, y, z, z2, acc = (w[:, 8 * k:8 * k + 8] for k in range(5))
                dve.wait_ge(S["const_in"], 64)
                for k, src in enumerate((s["dec_f"], s["dec_b"])):
                    steps.add(dve.tensor_copy(d[:, 4 * k:4 * k + 4], src[:, :]))
                steps.settle()
                dve.tensor_scalar(y, d, -1.0, None, ALU.mult).then_inc(S["dve_step"], 1)
                steps.n += 1
                steps.settle()
                steps.add(dve.tensor_tensor(y, y, d, ALU.min))
                steps.settle()
                dve.tensor_copy(z, y).then_inc(S["lg_arg"], 1)
                dve.wait_ge(S["lg_exp"], 1)
                steps.add(dve.tensor_scalar(z2, y, 2.0, None, ALU.add))
                steps.settle()
                steps.add(dve.reciprocal(z, z2))
                steps.settle()
                steps.add(dve.tensor_tensor(z, z, y, ALU.mult))
                steps.settle()
                steps.add(dve.tensor_tensor(z2, z, z, ALU.mult))
                steps.add(dve.memset(acc, 2.0 / 19))
                steps.settle()
                for odd in range(17, 0, -2):
                    steps.add(dve.tensor_tensor(acc, acc, z2, ALU.mult))
                    steps.settle()
                    steps.add(dve.tensor_scalar(acc, acc, 2.0 / odd, None, ALU.add))
                    steps.settle()
                steps.add(dve.tensor_tensor(acc, acc, z, ALU.mult))
                steps.add(dve.tensor_scalar(y, d, 0.0, None, ALU.min))
                steps.settle()
                steps.add(dve.tensor_tensor(lg[:, :], y, acc, ALU.subtract))
                steps.settle()
                steps.add(dve.tensor_scalar(lg[:, 4:8], lg[:, 4:8], -1.0, None, ALU.mult))

            def norm(n, gain):
                means(n, 0)
                rstd(n, 0)
                for t in range(NT):
                    if t == TPH:
                        rstd(n, 1)
                    normed(n, t)
                    if n == 0 and t == 1:
                        dve.wait_ge(S["g1_in"], 16)
                    if t:
                        turned_lo(2 * n, t - 1, gain)
                    if t == 1:
                        means(n, 1)
                    if n == 0 and t > NT - AHEAD:
                        lo(t - 1 - (NT - AHEAD))
                turned_lo(2 * n, NT - 1, gain)

            norm(0, s["g1"])
            lo(AHEAD - 1)
            log_decays()
            for c in range(C_NA_V):
                lo(c + AHEAD)
            for c in range(C_NA_V, C_RET_QK):
                lo(c + AHEAD)
            for n in range(UNITS + 2):
                if n < UNITS:
                    h, t = n // NT, n % NT
                    q = seq_of(t)
                    L = SEQS[q][1] * P
                    row = (6 - 2 * (t - SEQS[q][0]))
                    dve.wait_ge(S["na_scored"], n + 1)
                    dve.wait_ge(S["band_ready"], h + 1)
                    if n >= 2:
                        dve.wait_ge(S["na_exp"], n - 1)
                    sc = na_sc[:, n % 2, 0:L]
                    steps.add(dve.scalar_tensor_tensor(
                        sc, ps[:, 2 + n % 2, 0:L], NA_DIM ** -0.5,
                        band[:, h % 2, row:row + L // GRID_W, :].rearrange("p r c -> p (r c)"),
                        ALU.mult, ALU.add))
                    steps.settle()
                    steps.add(dve.reduce_max(s["mx"][:, n:n + 1], sc, AX.X))
                    steps.settle()
                    dve.tensor_scalar(s["nmx"][:, n:n + 1], s["mx"][:, n:n + 1], -1.0, None, ALU.mult
                                      ).then_inc(S["na_max"], 1)
                if n >= 2:
                    u = n - 2
                    h, t = u // NT, u % NT
                    dve.wait_ge(S["na_exp"], u + 1)
                    steps.add(dve.reciprocal(s["prec"][:, u:u + 1], s["psum_"][:, u:u + 1]))
                    steps.settle()
                    dve.wait_ge(S["na_summed"], u + 1)
                    dve.tensor_scalar(mix[:, t, h * NA_DIM:(h + 1) * NA_DIM], ps[:, 6 + u % 2, 0:NA_DIM],
                                      s["prec"][:, u:u + 1], None, ALU.mult).then_inc(S["na_out"], 1)
                if n < UNITS and n % 6 == 1:
                    lo(C_RET_QK + n // 6 + AHEAD)
            dve.wait_ge(S["mid_in"], 80)
            for c in range(C_RET_V, C_OUT):
                if c + AHEAD < C_OUT:
                    lo(c + AHEAD)
                for r in (2 * (c - C_RET_V), 2 * (c - C_RET_V) + 1):
                    dve.wait_ge(S["rot_mm"], r + 1)
                    dve.tensor_tensor(rot_sin[:, r % 2], ps[:, r % 2, 0:HALF], sin[:, half_cols(r % 2)],
                                      ALU.mult).then_inc(S["rot_s"], 1)
                    dve.wait_ge(S["rot_s"], r + 1)
                    dve.wait_ge(S["rot_c"], r + 1)
                    dve.tensor_tensor(ret_qk[:, r // 2, half_cols(r % 2)], rot_cos[:, r % 2], rot_sin[:, r % 2],
                                      ALU.add).then_inc(S["rot_done"], 1)

            def decay_argument(h):
                steps.add(dve.tensor_scalar(back[:, :], diff[:, :], 0.0, s["lg"][:, 4 + h:5 + h], ALU.min, ALU.mult))
                steps.add(dve.tensor_scalar(dmat[:, h % 2], diff[:, :], 0.0, s["lg"][:, h:h + 1], ALU.max, ALU.mult))
                steps.settle()
                dve.tensor_tensor(dmat[:, h % 2], dmat[:, h % 2], back[:, :], ALU.add
                                  ).then_inc(S["decay_arg"], 1)

            dve.wait_ge(S["rot_done"], 16)
            dve.wait_ge(S["na_exp"], UNITS)
            for c in range(C_OUT, C_OUT + AHEAD):
                lo(c)
            decay_argument(0)

            def decayed(r):
                h, q = ret_units[r]
                nt = SEQS[q][1]
                L = nt * P
                if r >= 2:
                    dve.wait_ge(S["ret_o"], r - 1)
                dve.wait_ge(S["decay_ready"], h + 1)
                for k in range(nt):
                    dve.wait_ge(S["ret_qk_done"], att_first[r] + k + 1)
                    off = 384 - k * P
                    dve.scalar_tensor_tensor(att[:, r % 2, k, 0:L], ps[:, 2 + (att_first[r] + k) % 4, 0:L],
                                             RET_DIM ** -0.5, dmat[:, h % 2, off:off + L], ALU.mult, ALU.mult
                                             ).then_inc(S["ret_att"], 1)

            decayed(0)
            for r, (h, q) in enumerate(ret_units):
                t0, nt = SEQS[q]
                if q == 0 and h + 1 < RET_HEADS:
                    dve.wait_ge(S["decay_arg"], h + 1)
                    decay_argument(h + 1)
                if r + 1 < len(ret_units):
                    decayed(r + 1)
                if r < NT:
                    heads_lo(r, 0, S["na_hi"], r + 1, S["na_lo"])
                dve.wait_ge(S["ret_o"], r + 1)
                for t in range(nt):
                    last = dve.bn_stats(stats[:, (t0 + t) * RET_HEADS + h, :], ps[:, 6 + r % 2, tile_cols(t)])
                last.then_inc(S["ret_stat"], 1)
            dve.wait_ge(S["ret_stat"], len(ret_units))
            for k in range(NT * RET_HEADS):
                last = dve.bn_aggr(mv[:, k, :], stats[:, k, :])
            steps.add(last)
            steps.settle()
            dve.tensor_scalar(ret_rs[:, :], mv[:, :, 1], EPS, None, ALU.add).then_inc(S["ret_var"], 1)
            dve.wait_ge(S["ret_sd"], 1)
            steps.add(dve.reciprocal(ret_rs[:, :], ret_std[:, :]))
            steps.settle()
            dve.wait_ge(S["ret_copied"], len(ret_units))
            dve.wait_ge(S["gate_ready"], NT)
            for t in range(NT):
                for h in range(RET_HEADS):
                    o = mix[:, t, WIDTH + h * P:WIDTH + (h + 1) * P]
                    k = t * RET_HEADS + h
                    last = dve.tensor_scalar(o, o, mv[:, k, 0:1], ret_rs[:, k:k + 1], ALU.subtract, ALU.mult)
                steps.add(last)
                steps.settle()
                dve.tensor_tensor(mix[:, t, WIDTH:], mix[:, t, WIDTH:], ret_gate[:, t], ALU.mult
                                  ).then_inc(S["src_ready"], 1)
            lo(C_OUT + AHEAD)
            for t in range(NT):
                heads_lo(t, 4, S["hi_evac"], NT + t + 1, S["lo_evac"])
            dve.wait_ge(S["xa_in"], 16 * NT)
            for half in range(2):
                for c in range(C_OUT + 4 * half + (half == 0), C_OUT + 4 * half + 4):
                    lo(c + AHEAD)
                cols = slice(half * 512, half * 512 + 512)
                for t in range(NT):
                    dve.wait_ge(S["v_done"], NT * (3 + half) + t + 1)
                    dve.tensor_tensor(x2[:, t, cols], ps[:, 2 + t, :], x_again[:, t, cols], ALU.add
                                      ).then_inc(S["v_evac"], 1)
            norm(1, s["g2"])
            for c in range(C_WQ, C_END - AHEAD):
                lo(c + AHEAD)

            def best_keys(t):
                sl = t % 2
                if t:
                    dve.wait_ge(S["s_in"], 16 * t)
                for g in range(4):
                    if t == 0:
                        dve.wait_ge(S["evac"], g + 1)
                    ks = [4 * g + k for k in range(4)]
                    sc = [(s_cur if t else sc_out[:, 2])[:, k, :] for k in ks]
                    for k in range(4):
                        last = dve.max(tv[:, sl, ks[k], 0:8], sc[k])
                    steps.add(last)
                    steps.settle()
                    for k in range(4):
                        dve.max_index(ti[:, sl, ks[k], 0:8], tv[:, sl, ks[k], 0:8], sc[k])
                        last = dve.match_replace(rep[:, k, :], tv[:, sl, ks[k], 0:8], sc[k], imm_value=-3e38)
                    steps.add(last)
                    steps.settle()
                    for k in range(4):
                        last = dve.max(tv[:, sl, ks[k], 8:16], rep[:, k, :])
                    steps.add(last)
                    steps.settle()
                    for k in range(4):
                        last = dve.max_index(ti[:, sl, ks[k], 8:16], tv[:, sl, ks[k], 8:16], rep[:, k, :])
                    last.then_inc(S["tk_first"], 1)

            def best_pairs(t):
                sl = t % 2
                v = tv[:, sl].rearrange("p (h two) k -> p h two k", two=2)
                dve.wait_ge(S["tk_first"], 4 * t + 4)
                steps.add(dve.tensor_tensor(cand[:, :, :].rearrange("p h (x y) -> p h x y", x=TOPK),
                                            v[:, :, 0, :, None].broadcast_to([P, PEER_HEADS, TOPK, TOPK]),
                                            v[:, :, 1, None, :].broadcast_to([P, PEER_HEADS, TOPK, TOPK]),
                                            ALU.add))
                steps.settle()
                hs = range(PEER_HEADS)
                for h in hs:
                    last = dve.max(bv[:, h, 0:8], cand[:, h, :])
                steps.add(last)
                steps.settle()
                for h in hs:
                    last = dve.max_index(bp[:, h, 0:8], bv[:, h, 0:8], cand[:, h, :])
                for h in hs:
                    last = dve.match_replace(cand[:, h, :], bv[:, h, 0:8], cand[:, h, :], imm_value=-3e38)
                steps.add(last)
                steps.settle()
                for h in hs:
                    last = dve.max(bv[:, h, 8:16], cand[:, h, :])
                steps.add(last)
                steps.settle()
                for h in hs:
                    last = dve.max_index(bp[:, h, 8:16], bv[:, h, 8:16], cand[:, h, :])
                last.then_inc(S["tk_second"], 1)
                dve.wait_ge(S["tk_second"], t + 1)
                dve.tensor_tensor(gexp[:, sl], bv[:, :, :], bv[:, :, 0:1].broadcast_to([P, PEER_HEADS, TOPK]),
                                  ALU.subtract).then_inc(S["tk_diff"], 1)
                flat = bp[:, :, :].rearrange("p h k -> p (h k)")
                steps.add(dve.tensor_scalar(pa[:, 0, :], flat, 4, None, ALU.logical_shift_right))
                steps.add(dve.tensor_scalar(pa[:, 1, :], flat, 15, None, ALU.bitwise_and))
                steps.settle()
                dve.tensor_copy(paf[:, :], pa[:, 0, :])
                dve.tensor_copy(pbf[:, :], pa[:, 1, :])
                steps.add(dve.tensor_copy(tif[:, sl], ti[:, sl]))

            def hot_ranks(t):
                steps.settle()
                if t:
                    dve.wait_ge(S["tk_chosen"], t)
                for one, pos in ((one1, paf), (one2, pbf)):
                    last = dve.tensor_tensor(one[:, :, :], pos[:, :, None].broadcast_to([P, P, TOPK]),
                                             s["iota"][:, None, 0:TOPK].broadcast_to([P, P, TOPK]), ALU.is_equal)
                last.then_inc(S["tk_pos"], 1)

            def choices(t):
                sl = t % 2
                dve.wait_ge(S["tk_exp"], t + 1)
                if t:
                    dve.wait_ge(S["idx_turned"], t)
                steps.add(dve.reduce_sum(gsum[:, :], gexp[:, sl], AX.X))
                steps.settle()
                steps.add(dve.reciprocal(grec[:, :], gsum[:, :]))
                steps.settle()
                dve.tensor_tensor(chosen[:, 2, :].rearrange("p (h k) -> p h k", h=PEER_HEADS), gexp[:, sl],
                                  grec[:, :, None].broadcast_to([P, PEER_HEADS, TOPK]), ALU.mult)
                for k, one in enumerate((one1, one2)):
                    dve.wait_ge(S["one_ready"], 2 * t + k + 1)
                    last = dve.reduce_sum(chosen[:, k, :], one[:, :, :], AX.X)
                last.then_inc(S["tk_chosen"], 1)

            def turned_choice(t):
                dve.wait_ge(S["idx_turned"], t + 1)
                dve.tensor_copy(idx_t[:, :, t % 2, :], ps[:, 6, 0:3 * P].rearrange("p (c n) -> p c n", c=3)
                                ).then_inc(S["idx_ready"], 1)

            def hot(t, i, k, first=False):
                if not first:
                    dve.wait_ge(S["gate_mm"], i * HOT + (32 * t + k - (HOT - 1)))
                for c, dst in ((1, hot_b), (0, hot_a)):
                    last = dve.tensor_tensor(dst[:, k], s["iota"][:, None, :].broadcast_to([P, 4, P]),
                                             idx_t[:, c, t % 2, bass.ds(i * (4 * HOT) + 4 * k, 4), None
                                                   ].broadcast_to([P, 4, P]), ALU.is_equal)
                last.then_inc(S["hot_ready"], 1)

            dve.wait_ge(S["lo_ready"], C_END)
            for t in range(NT + 1):
                if t < NT:
                    best_keys(t)
                if t:
                    choices(t - 1)
                if t < NT:
                    best_pairs(t)
                    if t == 0:
                        for k in range(2):
                            dve.wait_ge(park[k], 16 * ((NT - k) // 2))
                if t < NT:
                    hot_ranks(t)
                if t:
                    turned_choice(t - 1)
                if t:
                    dve.wait_ge(S["idx_ready"], t)
                    if t == 1:
                        for k in range(HOT):
                            hot(0, 0, k, first=True)
                    with dve.Fori(int(t == 1), P // (4 * HOT)) as i:
                        for k in range(HOT):
                            hot(t - 1, i, k)

            def add_sums(i, e):
                if isinstance(i, int) and i == 0:
                    dve.wait_ge(x2_in[half_of(e + 7)], 16)
                for t in range(TPH):
                    dve.wait_ge(S["y_done"], i * 24 + (3 * e - 2 + t))
                    for c in range(2):
                        o = x2[:, half_of(e + 7) * TPH + t, c * 512:c * 512 + 512]
                        last = dve.tensor_tensor(o, ps[:, 2 * t + c, :], o, ALU.add)
                    last.then_inc(S["y_added"], 1)

            def step(i, e, early):
                par = e % 2
                if early:
                    dve.wait_ge(act_in[par], i * 64 + 16 * (e // 2 + 1))
                else:
                    dve.wait_ge(S["gelu_done"], i * 8 + (e + 1))
                dve.wait_ge(gate_in[par], i * 64 + 16 * (e // 2 + 1))
                if positive(i * 8 + (e - 1)):
                    dve.wait_ge(S["w_lo_ready"], i * 8 + (e - 1))
                dve.tensor_tensor(w_f[:, par], act_g[:, par], g_in[:, par], ALU.mult).then_inc(S["w_ready"], 1)
                dve.wait_ge(S["w_hi_ready"], i * 8 + (e + 1))
                dve.tensor_tensor(w_lo[:, par], w_f[:, par], w_hi[:, par].bitcast(F32), ALU.subtract
                                  ).then_inc(S["w_lo_ready"], 1)
                if par == 0 and positive(i * 8 + e):
                    add_sums(i, e)

            for e in range(8):
                step(0, e, True)
            with dve.Fori(1, EARLY_ITERS) as i:
                for e in range(8):
                    step(i, e, True)
            with dve.Fori(EARLY_ITERS, ITERS - 1) as i:
                for e in range(8):
                    step(i, e, False)
            for e in range(8):
                step(ITERS - 1, e, False)

            def final(m):
                means(2, m)
                rstd(2, m)
                for t in range(m * TPH, m * TPH + TPH):
                    col = 2 * NT + t
                    dve.scalar_tensor_tensor(x2[:, t, :], x2[:, t, :], s["rstd"][:, col:col + 1], fgain[:, :],
                                             ALU.mult, ALU.mult).then_inc(S["y_out"], 1)

            dve.wait_ge(S["fg_in"], 16)
            final(0)
            add_sums(ITERS - 1, 8)
            final(1)


def shape_constants():
    f = np.float32
    d = RET_DIM
    inv = (f(1.0) / (f(10000.0) ** (np.arange(0, d, 2, dtype=f) / f(d)))).astype(f)
    pos = np.concatenate([np.arange(SEQ), np.arange(DEC_SEQ)]).astype(f)
    ang = (inv[:, None] * pos[None, :]).astype(f)
    cos, sin = np.cos(ang), np.sin(ang)
    perm = np.zeros((P, P), f)
    for i in range(P // 2):
        perm[i + P // 2, i] = -1.0
        perm[i, i + P // 2] = 1.0
    diff = (np.arange(DIFF)[None, :] - 384 - np.arange(P)[:, None]).astype(f)
    start = np.clip(np.arange(GRID_W) - NA_COLS // 2, 0, GRID_W - NA_COLS)
    c = np.arange(GRID_W)
    inside = (c[None, :] >= start[:, None]) & (c[None, :] < start[:, None] + NA_COLS)
    mask = np.where(inside, 0.0, NEG).astype(f)
    return {"cos": np.concatenate([cos, cos]).astype(f), "sin": np.concatenate([sin, sin]).astype(f),
            "perm": perm, "diff": diff, "winmask": np.concatenate([mask, mask])}


def laid_out(x_prompt, x_sample, norm1_g, w_in, na_rpb, ret_decay_fwd, ret_decay_bwd, ret_norm_g, w_out,
             norm2_g, peer_w_q, peer_sub_keys, peer_u, peer_v, final_g):
    x = np.concatenate([x_prompt[0], x_sample[0]]).reshape(NT, P, D_MODEL)

    def stationary(w):
        n = w.shape[1] // P
        return w.reshape(KD, P, n, P).transpose(2, 1, 0, 3).reshape(n, P, 1024)

    def moving(w):
        n = w.shape[1] // 512
        return w.reshape(4, 2, P, n, 512).transpose(3, 0, 2, 1, 4).reshape(4 * n, P, 1024)

    w = w_in[0]
    cut = [w[:, 512 * k:512 * k + 512] for k in range(7)]
    front = np.concatenate([stationary(cut[0]), stationary(cut[1]), moving(cut[2]), stationary(cut[3]),
                            stationary(cut[4]), moving(cut[5]), moving(cut[6]), moving(w_out[0]),
                            stationary(peer_w_q[0])])
    u = peer_u[0].reshape(N_KEYS, N_KEYS, KD, P).transpose(0, 3, 2, 1).reshape(N_KEYS, 1, P, 1024)
    v = peer_v[0].reshape(N_KEYS, 1, P, 1024)
    par = np.arange(2)[:, None, None, None]
    qc = np.arange(GRID_W)[None, :, None, None]
    off = np.arange(BAND_ROWS)[None, None, :, None]
    kc = np.arange(GRID_W)[None, None, None, :]
    col = np.clip(kc - qc + NA_COLS - 1, 0, 2 * NA_COLS - 2)
    band = na_rpb[0][:, off + 1 - par, col].reshape(NA_HEADS, P, BAND_ROWS * GRID_W)
    out = {"x": x, "front": front, "experts": np.concatenate([u, v], axis=1), "band": band,
           "g1": norm1_g[0].reshape(KD, P).T, "g2": norm2_g[0].reshape(KD, P).T,
           "dec_f": ret_decay_fwd[0], "dec_b": ret_decay_bwd[0], "ret_norm": ret_norm_g[0], "fgain": final_g,
           "keys": peer_sub_keys[0].reshape(16, N_KEYS, P).transpose(2, 0, 1)}
    out.update(shape_constants())
    return {k: np.ascontiguousarray(v) for k, v in out.items()}


def kernel(**inputs):
    import concourse.bacc as bacc
    from concourse.bass_utils import run_bass_kernel_spmd

    nc = bacc.Bacc("TRN2", target_bir_lowering=False, num_devices=1)
    arrays, aps = {}, {}
    for name, v in laid_out(**{k: np.asarray(x) for k, x in inputs.items()}).items():
        arrays[f"in_{name}"] = v
        aps[name] = nc.dram_tensor(f"in_{name}", v.shape, mybir.dt.from_np(v.dtype), kind="ExternalInput").ap()
    aps["gates"] = nc.dram_tensor("gates", (N_KEYS, N_KEYS, TOK), F32, kind="Internal").ap()
    aps["early"] = nc.dram_tensor("early", (EARLY, 2, P, HALF), F32, kind="Internal").ap()
    aps["scores"] = nc.dram_tensor("scores", (NT, P, 16, N_KEYS), F32, kind="Internal").ap()
    aps["x2_park"] = nc.dram_tensor("x2_park", (P, NT, D_MODEL), F32, kind="Internal").ap()
    aps["y"] = nc.dram_tensor("out_y", (NT, P, D_MODEL), F32, kind="ExternalOutput").ap()
    encoder_program(nc, aps)
    got = run_bass_kernel_spmd(nc, [arrays], core_ids=[0]).results[0]["out_y"]
    y = got.reshape(TOK, D_MODEL)
    return y[:SEQ].reshape(1, SEQ, D_MODEL), y[SEQ:].reshape(1, DEC_SEQ, D_MODEL)
```
